# Optimizing a Trainium2 kernel written in Bass

```python
import math
import jax, jax.numpy as jnp
from jax import lax
import numpy as np

D_MODEL = 1024
BATCH = 1
SEQ = 512
DEPTH = 1
DEC_BATCH = 1
DEC_SEQ = 64
PAST_LEN = 256

CHUNK = 64
POOL_WIDTH = D_MODEL // 2
POOL_WINDOWS = (2, 4, 8, 16)
N_POOL_GROUPS = len(POOL_WINDOWS)
POOL_GROUP = POOL_WIDTH // N_POOL_GROUPS
POOL_HIST = max(POOL_WINDOWS) - 1
N_HEADS = 4
HEAD_DIM = D_MODEL // (4 * N_HEADS)
V_DIM = 2 * HEAD_DIM
QK_WIDTH = N_HEADS * 2 * HEAD_DIM
ATTN_WIDTH = N_HEADS * V_DIM
PROJ_WIDTH = POOL_WIDTH + 2 * QK_WIDTH + ATTN_WIDTH
MIX_WIDTH = POOL_WIDTH + ATTN_WIDTH
ATTN_SCALE = HEAD_DIM ** -0.5
Q_BLOCK = 128
NEG_INF = -1e30
N_GROUPS = 4
EXPERTS_PER_GROUP = 4
N_EXPERTS = N_GROUPS * EXPERTS_PER_GROUP
TOP_K = 2
D_EXPERT = 256
EPS = 1e-6

kernel_name = "hymba_pool_diffattn_hiermoe_stream_step"

def rmsnorm(x, g):
    xf = x.astype(jnp.float32)
    y = xf * lax.rsqrt(jnp.mean(xf * xf, axis=-1, keepdims=True) + EPS)
    return (y * g.astype(jnp.float32)).astype(x.dtype)

def lambda_init_for(layer):
    return 0.8 - 0.6 * math.exp(-0.3 * layer)

def multiscale_pool(u, hist, start_pos, w_pool, pool_scale):
    B, T, C = u.shape
    ext = jnp.concatenate([hist.astype(jnp.float32), u.astype(jnp.float32)], axis=1)
    csum = jnp.concatenate([jnp.zeros((B, 1, C), jnp.float32), jnp.cumsum(ext, axis=1)], axis=1)
    pos = start_pos + jnp.arange(T, dtype=jnp.int32)
    uf = u.astype(jnp.float32)
    diffs = []
    for g, w in enumerate(POOL_WINDOWS):
        lo_c, hi_c = g * POOL_GROUP, (g + 1) * POOL_GROUP
        hi = csum[:, POOL_HIST + 1:POOL_HIST + 1 + T, lo_c:hi_c]
        lo = csum[:, POOL_HIST + 1 - w:POOL_HIST + 1 - w + T, lo_c:hi_c]
        cnt = jnp.minimum(w, pos + 1).astype(jnp.float32)[None, :, None]
        diffs.append((hi - lo) / cnt - uf[..., lo_c:hi_c])
    d = jnp.stack(diffs, axis=2)
    y = jnp.einsum('btgc,gce->btge', d, w_pool.astype(jnp.float32)).reshape(B, T, C)
    return (y * pool_scale.astype(jnp.float32)).astype(u.dtype)

def diff_attend(q, k, v, q_pos, k_pos, lam):
    s = jnp.einsum('bqhcd,bkhcd->bhcqk', q, k) * ATTN_SCALE
    mask = (k_pos[None, :] // CHUNK) <= (q_pos[:, None] // CHUNK)
    s = jnp.where(mask, s, NEG_INF)
    p = jax.nn.softmax(s, axis=-1)
    a = p[:, :, 0] - lam * p[:, :, 1]
    return jnp.einsum('bhqk,bkhe->bqhe', a, v)

def layer_forward(x, pool_hist, k_hist, v_hist, start_pos, layer,
                  g_mix, w_in, w_pool, pool_scale, lam_q1, lam_k1, lam_q2, lam_k2, g_subln, w_out,
                  g_ffn, w_group, b_group, w_erouter, b_erouter, w_gate, w_up, w_down):
    B, T, _ = x.shape
    h = rmsnorm(x, g_mix)
    proj = h @ w_in
    u = proj[..., :POOL_WIDTH]
    q = proj[..., POOL_WIDTH:POOL_WIDTH + QK_WIDTH]
    k = proj[..., POOL_WIDTH + QK_WIDTH:POOL_WIDTH + 2 * QK_WIDTH]
    v = proj[..., POOL_WIDTH + 2 * QK_WIDTH:]
    k_new = k.reshape(B, T, N_HEADS, 2 * HEAD_DIM)
    v_new = v.reshape(B, T, N_HEADS, V_DIM)

    pool_out = multiscale_pool(u, pool_hist, start_pos, w_pool, pool_scale)
    new_pool = jnp.concatenate([pool_hist, u], axis=1)[:, -POOL_HIST:]

    if k_hist is None:
        k_all, v_all = k_new, v_new
    else:
        k_all = jnp.concatenate([k_hist.astype(k_new.dtype), k_new], axis=1)
        v_all = jnp.concatenate([v_hist.astype(v_new.dtype), v_new], axis=1)
    Tk = k_all.shape[1]
    k_pos = jnp.arange(Tk, dtype=jnp.int32)
    q_pos = start_pos + jnp.arange(T, dtype=jnp.int32)
    qf = q.reshape(B, T, N_HEADS, 2, HEAD_DIM).astype(jnp.float32)
    kf = k_all.reshape(B, Tk, N_HEADS, 2, HEAD_DIM).astype(jnp.float32)
    vf = v_all.astype(jnp.float32)
    li = lambda_init_for(layer)
    lam = (jnp.exp(jnp.sum(lam_q1.astype(jnp.float32) * lam_k1.astype(jnp.float32)))
           - jnp.exp(jnp.sum(lam_q2.astype(jnp.float32) * lam_k2.astype(jnp.float32))) + li)
    if T > Q_BLOCK:
        nb = T // Q_BLOCK
        qb = qf.reshape(B, nb, Q_BLOCK, N_HEADS, 2, HEAD_DIM).transpose(1, 0, 2, 3, 4, 5)
        pb = q_pos.reshape(nb, Q_BLOCK)
        ob = lax.map(lambda a: diff_attend(a[0], kf, vf, a[1], k_pos, lam), (qb, pb))
        o = ob.transpose(1, 0, 2, 3, 4).reshape(B, T, N_HEADS, V_DIM)
    else:
        o = diff_attend(qf, kf, vf, q_pos, k_pos, lam)
    o = o * lax.rsqrt(jnp.mean(o * o, axis=-1, keepdims=True) + EPS) * g_subln.astype(jnp.float32) * (1.0 - li)
    attn_out = o.reshape(B, T, ATTN_WIDTH).astype(x.dtype)

    x = x + jnp.concatenate([pool_out, attn_out], axis=-1) @ w_out

    h2 = rmsnorm(x, g_ffn)
    hf = h2.astype(jnp.float32)
    g_logits = hf @ w_group.astype(jnp.float32) + b_group.astype(jnp.float32)
    g_prob = jax.nn.softmax(g_logits, axis=-1)
    g_idx = jnp.argmax(g_logits, axis=-1)
    g_gate = jnp.take_along_axis(g_prob, g_idx[..., None], axis=-1)
    e_logits = (hf @ w_erouter.astype(jnp.float32) + b_erouter.astype(jnp.float32)).reshape(B, T, N_GROUPS, EXPERTS_PER_GROUP)
    e_sel = jnp.take_along_axis(e_logits, g_idx[..., None, None], axis=2)[..., 0, :]
    top_v, top_i = lax.top_k(e_sel, TOP_K)
    top_w = jax.nn.softmax(top_v, axis=-1) * g_gate
    expert_id = g_idx[..., None] * EXPERTS_PER_GROUP + top_i
    combine = jnp.sum(jax.nn.one_hot(expert_id, N_EXPERTS, dtype=jnp.float32) * top_w[..., None], axis=2)
    moe = jnp.zeros((B, T, D_MODEL), jnp.float32)
    for e in range(N_EXPERTS):
        he = jax.nn.silu(h2 @ w_gate[e]) * (h2 @ w_up[e])
        moe = moe + combine[..., e:e + 1] * (he @ w_down[e]).astype(jnp.float32)
    x = x + moe.astype(x.dtype)
    return x, k_new, v_new, new_pool

def setup_inputs(seed: int = 0) -> dict:
    key = jax.random.key(seed)
    ks = jax.random.split(key, 24)
    f32 = jnp.float32
    nrm = lambda k, shape, s: jax.random.normal(k, shape, f32) * s
    return {
        "x_prompt": nrm(ks[0], (BATCH, SEQ, D_MODEL), 1.0),
        "x_sample": nrm(ks[1], (DEC_BATCH, DEC_SEQ, D_MODEL), 1.0),
        "cache_k": nrm(ks[2], (DEPTH, DEC_BATCH, PAST_LEN, N_HEADS, 2 * HEAD_DIM), 1.0),
        "cache_v": nrm(ks[3], (DEPTH, DEC_BATCH, PAST_LEN, N_HEADS, V_DIM), 1.0),
        "state_pool": nrm(ks[4], (DEPTH, DEC_BATCH, POOL_HIST, POOL_WIDTH), 1.0),
        "g_mix": 1.0 + nrm(ks[5], (DEPTH, D_MODEL), 0.05),
        "w_in": nrm(ks[6], (DEPTH, D_MODEL, PROJ_WIDTH), D_MODEL ** -0.5),
        "w_pool": nrm(ks[7], (DEPTH, N_POOL_GROUPS, POOL_GROUP, POOL_GROUP), POOL_GROUP ** -0.5),
        "pool_scale": 1.0 + nrm(ks[8], (DEPTH, POOL_WIDTH), 0.1),
        "lam_q1": nrm(ks[9], (DEPTH, HEAD_DIM), 0.1),
        "lam_k1": nrm(ks[10], (DEPTH, HEAD_DIM), 0.1),
        "lam_q2": nrm(ks[11], (DEPTH, HEAD_DIM), 0.1),
        "lam_k2": nrm(ks[12], (DEPTH, HEAD_DIM), 0.1),
        "g_subln": 1.0 + nrm(ks[13], (DEPTH, V_DIM), 0.05),
        "w_out": nrm(ks[14], (DEPTH, MIX_WIDTH, D_MODEL), MIX_WIDTH ** -0.5),
        "g_ffn": 1.0 + nrm(ks[15], (DEPTH, D_MODEL), 0.05),
        "w_group": nrm(ks[16], (DEPTH, D_MODEL, N_GROUPS), D_MODEL ** -0.5),
        "b_group": nrm(ks[17], (DEPTH, N_GROUPS), 0.01),
        "w_erouter": nrm(ks[18], (DEPTH, D_MODEL, N_EXPERTS), D_MODEL ** -0.5),
        "b_erouter": nrm(ks[19], (DEPTH, N_EXPERTS), 0.01),
        "w_gate": nrm(ks[20], (DEPTH, N_EXPERTS, D_MODEL, D_EXPERT), D_MODEL ** -0.5),
        "w_up": nrm(ks[21], (DEPTH, N_EXPERTS, D_MODEL, D_EXPERT), D_MODEL ** -0.5),
        "w_down": nrm(ks[22], (DEPTH, N_EXPERTS, D_EXPERT, D_MODEL), D_EXPERT ** -0.5),
        "g_final": 1.0 + nrm(ks[23], (D_MODEL,), 0.05),
    }

def reference(x_prompt, x_sample, cache_k, cache_v, state_pool,
              g_mix, w_in, w_pool, pool_scale, lam_q1, lam_k1, lam_q2, lam_k2, g_subln, w_out,
              g_ffn, w_group, b_group, w_erouter, b_erouter, w_gate, w_up, w_down, g_final):
    xp, xs = x_prompt, x_sample
    kp_l, vp_l, pp_l, ks_l, vs_l, ps_l = [], [], [], [], [], []
    for l in range(DEPTH):
        w = (g_mix[l], w_in[l], w_pool[l], pool_scale[l], lam_q1[l], lam_k1[l], lam_q2[l], lam_k2[l],
             g_subln[l], w_out[l], g_ffn[l], w_group[l], b_group[l], w_erouter[l], b_erouter[l],
             w_gate[l], w_up[l], w_down[l])
        zero_hist = jnp.zeros((xp.shape[0], POOL_HIST, POOL_WIDTH), xp.dtype)
        xp, kp, vp, pp = layer_forward(xp, zero_hist, None, None, 0, l, *w)
        xs, kn, vn, pn = layer_forward(xs, state_pool[l].astype(xs.dtype), cache_k[l], cache_v[l], PAST_LEN, l, *w)
        kp_l.append(kp); vp_l.append(vp); pp_l.append(pp)
        ks_l.append(kn); vs_l.append(vn); ps_l.append(pn)
    y_prompt = rmsnorm(xp, g_final)
    y_sample = rmsnorm(xs, g_final)
    k_prompt = jnp.stack(kp_l); v_prompt = jnp.stack(vp_l); pool_prompt = jnp.stack(pp_l)
    k_sample = jnp.stack(ks_l); v_sample = jnp.stack(vs_l); pool_sample = jnp.stack(ps_l)
    return (y_prompt, y_sample, k_prompt, v_prompt, pool_prompt, k_sample, v_sample, pool_sample)


_drawn_inputs = setup_inputs


def setup_inputs(seed=0):
    import zlib

    import numpy as np

    out = dict(_drawn_inputs(seed))
    spreads = {}
    factors = {'lam_q1': 3.596,
     'lam_k1': 7.303,
     'b_group': 12.313,
     'b_erouter': 8.0,
     'lam_q2': 3.439,
     'lam_k2': 8.0}
    for name, (base, spread) in spreads.items():
        noise = np.random.default_rng([zlib.crc32(name.encode()), seed]).standard_normal(out[name].shape)
        drawn = base * np.exp(spread * noise) if base else spread * noise
        out[name] = __import__('jax').numpy.asarray(drawn.astype(out[name].dtype))
    for name, factor in factors.items():
        out[name] = (out[name] * factor).astype(out[name].dtype)
    return out
```

```python
import math
from contextlib import ExitStack

import numpy as np

import concourse.bass as bass
from concourse import mybir

F32 = mybir.dt.float32
BF16 = mybir.dt.bfloat16
I32 = mybir.dt.int32
ALU = mybir.AluOpType
ACT = mybir.ActivationFunctionType
X = mybir.AxisListType.X
DS = bass.ds

P = 128
D = 1024
KC = D // P
N_PROMPT, N_SAMPLE = 512, 64
T = N_PROMPT + N_SAMPLE
NT = 5
PT = N_PROMPT // P
PAST = 256
CHUNK = 64
HIST = 15
WINDOWS = (2, 4, 8, 16)
H = 4
HD = 64
VD = 2 * HD
PW = 512
SCALE = HD ** -0.5
NEG = -1e30
LAMBDA_INIT = 0.8 - 0.6 * math.exp(0.0)
EPS = 1e-6
G, EPG = 4, 4
E = G * EPG
FE = 256
FC = FE // P
NL = G + E
CAP = 128
MAXOV = (2 * T) // (CAP + 1)
OVK = -(-(T - CAP) // P)
NSLOT = E * P
RING = 4
NOWHERE = 1024
UNITS = NT * H
OV_STEPS = 7
WB = KC * FE


def rows(t):
    return P if t < PT else N_SAMPLE


def build(nc, x_prompt, x_sample, cache_k, cache_v, state_pool, g_mix, w_in, w_pool, pool_scale,
          lam_q1, lam_k1, lam_q2, lam_k2, g_subln, w_out, g_ffn, w_group, b_group, w_erouter,
          b_erouter, w_gate, w_up, w_down, g_final,
          y_prompt, y_sample, k_prompt, v_prompt, pool_prompt, k_sample, v_sample, pool_sample):
    ctx = ExitStack()
    with ctx:
        def sb(name, shape, dt=F32):
            return ctx.enter_context(nc.sbuf_tensor(name, shape, dt))

        def sem(name):
            return ctx.enter_context(nc.semaphore(name))

        def sems(name, n):
            return [sem(f"{name}{i}") for i in range(n)]

        xp = x_prompt.rearrange("a (t p) d -> (a t) p d", p=P)
        xs = x_sample.rearrange("a s d -> (a s) d")
        win_v = w_in.rearrange("a (p k) n -> (a p) k n", k=KC)
        wout_v = w_out.rearrange("a (f p) n -> p (a f) n", p=P)
        ck_v = cache_k.rearrange("a b (t p) h d -> p (a b t) (h d)", p=P)
        cv_v = cache_v.rearrange("a b (t p) h d -> p (a b t) (h d)", p=P)
        kp_v = k_prompt.rearrange("a b (t p) h d -> (a b t) p (h d)", p=P)
        vp_v = v_prompt.rearrange("a b (t p) h d -> (a b t) p (h d)", p=P)
        ks_v = k_sample.rearrange("a b s h d -> (a b s) (h d)")
        vs_v = v_sample.rearrange("a b s h d -> (a b s) (h d)")
        yp_v = y_prompt.rearrange("a (t p) d -> (a t) p d", p=P)
        ys_v = y_sample.rearrange("a s d -> (a s) d")
        wg_v = w_gate.rearrange("a e (p k) f -> (a e) p (k f)", k=KC)
        wu_v = w_up.rearrange("a e (p k) f -> (a e) p (k f)", k=KC)
        wd_v = w_down.rearrange("a e (c p) n -> (a e) p c n", p=P)
        h2_dram = nc.dram_tensor("h2_rows", (T, D), F32, kind="Internal").ap()
        y_dram = nc.dram_tensor("expert_rows", (NSLOT, D), F32, kind="Internal").ap()

        region_a = sb("region_a", [P, 12800])
        w_in_sb = [region_a[:, b * 4096:(b + 1) * 4096].rearrange("p (k n) -> p k n", k=KC) for b in range(2)]
        hT = region_a[:, 8192:12800].rearrange("p (k t) -> p k t", k=KC)
        region_w = sb("region_w", [P, 8192])
        w_out_sb = region_w[:, :].rearrange("p (f n) -> p f n", f=KC)
        ring0 = sb("ring0", [P, 6144])
        ring = [ring0[:, :], region_a[:, 0:6144], region_a[:, 6144:12288], region_w[:, 0:6144]]
        wg_sb = [r[:, 0:WB].rearrange("p (k f) -> p k f", k=KC) for r in ring]
        wu_sb = [r[:, WB:2 * WB].rearrange("p (k f) -> p k f", k=KC) for r in ring]
        wd_sb = [r[:, 2 * WB:3 * WB].rearrange("p (c n) -> p c n", c=FC) for r in ring]

        region_q = sb("region_q", [P, 5632])
        qT = region_q[:, 0:2304].rearrange("p (h t) -> p h t", h=H)
        kT = region_q[:, 2304:4608].rearrange("p (h t) -> p h t", h=H)
        kcT = region_q[:, 4608:5632].rearrange("p (h t) -> p h t", h=H)
        x2 = region_q[:, 0:NT * D].rearrange("p (t d) -> p t d", t=NT)

        mixT = sb("mixT", [P, KC, T])

        region_v = sb("region_v", [P, 3584])
        v_pr = region_v[:, 0:2048].rearrange("p (t n) -> p t n", t=PT)
        v_sa = region_v[:, 2048:3584].rearrange("p (t n) -> p t n", t=3)
        h2n = region_v[:, 0:2048].rearrange("p (b d) -> p b d", b=2)
        h2T = region_v[:, 2048:3072].rearrange("p (k t) -> p k t", k=KC)
        onehot_all = region_v[:, 0:640].bitcast(BF16).rearrange("p (b t s) -> p b t s", b=2, t=NT)

        region_k = sb("region_k", [P, 2048])
        kc_raw = region_k[:, 0:1024].rearrange("p (t n) -> p t n", t=2)
        k_st = region_k[:, 1024:2048].rearrange("p (b n) -> p b n", b=2)
        state_out = region_k[0:HIST, 0:1024].rearrange("p (b n) -> p b n", b=2)

        region_p = sb("region_p", [P, 2048])
        prob = region_p[:, :].rearrange("p (b c k) -> p b c k", b=2, c=2)
        xT = region_p[:, :].rearrange("p (b k s) -> p b k s", b=2, k=KC)
        region_t = sb("region_t", [P, 1536])
        aT = region_t[:, 0:1024].rearrange("p (b k) -> p b k", b=2)
        otok = region_t[:, 1024:1536]
        gact = region_t[:, 0:512].rearrange("p (b c s) -> p b c s", b=2, c=FC)
        heT = region_t[:, 512:1024].rearrange("p (b c s) -> p b c s", b=2, c=FC)

        region_x = sb("region_x", [P, 4096])
        xraw = region_x[:, 0:2048].rearrange("p (b d) -> p b d", b=2)
        xn = region_x[:, 2048:4096].rearrange("p (b d) -> p b d", b=2)
        EXT = HIST + N_PROMPT + HIST + N_SAMPLE
        S0 = 2 * HIST + N_PROMPT
        uext = region_x[:, 0:2 * EXT].rearrange("p (b t) -> p b t", b=2)
        usum = region_x[:, 2 * EXT:4 * EXT].rearrange("p (b t) -> p b t", b=2)
        w_pool_sb = region_x[:, 4 * EXT:4 * EXT + 512].rearrange("p (g e) -> p g e", g=H)
        xg = region_x[:, 0:2048].rearrange("p (b d) -> p b d", b=2)
        yst = region_x[:, 2048:4096].rearrange("p (b d) -> p b d", b=2)
        slot_to_token = region_x[:, D:D + NT * P].rearrange("p (t s) -> p t s", t=NT)

        y1 = region_a[:, 0:2048].rearrange("p (b d) -> p b d", b=2)
        y2 = region_a[:, 2048:4096].rearrange("p (b d) -> p b d", b=2)
        yout = region_a[:, 4096:6144].rearrange("p (b d) -> p b d", b=2)
        acc = region_a[:, 6144:8192].rearrange("p (b d) -> p b d", b=2)
        gfin = region_w[:, 6144:7168]

        ident = sb("ident", [P, P])
        iota_row = sb("iota_row", [P, P])
        tri = sb("tri", [P, P], BF16)
        ones = sb("ones", [P, P], BF16)
        gmix_sb = sb("gmix_sb", [P, KC])
        gffn_sb = sb("gffn_sb", [P, KC])
        pscale = sb("pscale", [P, H])
        gsub = sb("gsub", [P, 1])
        wr = sb("wr", [P, KC, NL])
        bias = sb("bias", [P, NL])
        lam_in = sb("lam_in", [1, 4, HD])
        lam_t = sb("lam_t", [1, 8])
        neglam = sb("neglam", [P, 1])
        hist_in = sb("hist_in", [HIST, PW])
        histT = sb("histT", [P, H, HIST])
        ustate = sb("ustate", [P, 2, H, HIST])
        inv_cnt = sb("inv_cnt", [P, 16])
        ss = sb("ss", [P, NT])
        rs = sb("rs", [P, 3, NT])
        mx = sb("mx", [P, 2, 2])
        negm = sb("negm", [P, 2, 2])
        psums = sb("psums", [P, NT, H, 2])
        coef = sb("coef", [P, 2])
        oss = sb("oss", [P, NT, H])
        osc = sb("osc", [P, 4, H])
        rev = sb("rev", [P, 4])
        tokv = sb("tokv", [P, NT, 2], BF16)
        idx = sb("idx", [P, 2], I32)
        ctl = sb("ctl", [1, MAXOV + 1], I32)
        wtok = sb("wtok", [P, 2, NT])
        yslot = sb("yslot", [P, 2, NT], I32)
        yslot_f = sb("yslot_f", [P, 2, NT])
        rm = sb("rm", [P, NT, E + 3])
        e128 = sb("e128", [P, E])
        jrow = sb("jrow", [P, MAXOV])
        jbase = sb("jbase", [P, MAXOV])
        ovoff = sb("ovoff", [P, 2 * NT])
        ovw = sb("ovw", [P, 2, NT])
        slot_tok = sb("slot_tok", [P, 1])
        wmain = sb("wmain", [P, 2, NT])
        fix = sb("fix", [P, HIST])

        scratch = [0]

        def rt(*shape):
            n = int(np.prod(shape))
            a = region_k[:, scratch[0]:scratch[0] + n]
            scratch[0] += n
            assert scratch[0] <= 2048
            if len(shape) == 1:
                return a
            names = "abcd"[:len(shape)]
            return a.rearrange(f"p ({' '.join(names)}) -> p {' '.join(names)}",
                               **{c: s for c, s in zip(names, shape)})
        lg = rt(NT, NL)
        g1h = rt(NT, G)
        esel = rt(NT, EPG)
        top = rt(2, NT, EPG)
        rt4 = rt(NT, G)
        rt1 = rt(4, NT)
        gex = rt(NT, G)
        m12 = rt(2, NT, E)
        msum = rt(NT, E)
        msum_b = rt(NT * E // 2).bitcast(BF16).rearrange("p (t e) -> p t e", t=NT)
        rank = rt(NT, E)
        base = rt(NT + 1, E)
        over = rt(E)
        cum = rt(2, E)
        isov = rt(NT, E)
        rt4b = rt(NT, G)
        ylin = rt(NT, E)
        etmp = rt(NT, E)
        jcmp = rt(MAXOV, E)
        jsum = rt(MAXOV)

        ps = ctx.enter_context(nc.psum_tensor("ps", [P, 8, 512], F32))

        x_loaded = sems("x_loaded", 2)
        gmix_loaded = sem("gmix_loaded")
        consts_loaded = sem("consts_loaded")
        lam_loaded = sem("lam_loaded")
        gsub_loaded = sem("gsub_loaded")
        w_in_loaded = sems("w_in_loaded", 2)
        cache_loaded = sem("cache_loaded")
        w_pool_loaded = sem("w_pool_loaded")
        w_out_loaded = sem("w_out_loaded")
        xres_loaded = sems("xres_loaded", NT)
        ring_loaded = sems("ring_loaded", RING)
        gfin_loaded = sem("gfin_loaded")
        consts_made = sem("consts_made")
        pool_step = sem("pool_step")
        dve_step = sem("dve_step")
        x_squared = sem("x_squared")
        xn_ready = sem("xn_ready")
        x_transposed = sem("x_transposed")
        hT_dve = sem("hT_dve")
        hT_act = sem("hT_act")
        v_full = sem("v_full")
        v_evac = sem("v_evac")
        v_stored = sem("v_stored")
        qk_full = sem("qk_full")
        qkp_evac = sem("qkp_evac")
        qks_evac = sem("qks_evac")
        ktok_full = sem("ktok_full")
        ktok_evac = sem("ktok_evac")
        k_stored = sems("k_stored", 2)
        kc_full = sem("kc_full")
        kc_evac = sem("kc_evac")
        hist_full = sem("hist_full")
        hist_evac = sem("hist_evac")
        lam_dots = sem("lam_dots")
        lam_exp = sem("lam_exp")
        lam_made = sem("lam_made")
        lam_spread = sem("lam_spread")
        scores_full = sem("scores_full")
        negm_ready = sem("negm_ready")
        exp_done = sem("exp_done")
        a_ready = sem("a_ready")
        aT_full = sem("aT_full")
        aT_evac = sem("aT_evac")
        pv_done = sem("pv_done")
        o_squared = sem("o_squared")
        o_ready = sem("o_ready")
        oT_full = sem("oT_full")
        oT_evac = sem("oT_evac")
        u_full = sem("u_full")
        u_evac_act = sem("u_evac_act")
        u_evac_dve = sem("u_evac_dve")
        u_summed = sem("u_summed")
        diff_ready = sem("diff_ready")
        pool_full = sem("pool_full")
        pool_evac_act = sem("pool_evac_act")
        pool_evac_dve = sem("pool_evac_dve")
        state_full = sem("state_full")
        state_evac = sem("state_evac")
        state_stored = sem("state_stored")
        op_full = sem("op_full")
        x2_ready = sem("x2_ready")
        x2_squared = sem("x2_squared")
        h2n_ready = sem("h2n_ready")
        h2_stored = sems("h2_stored", 2)
        h2_transposed = sem("h2_transposed")
        h2T_dve = sem("h2T_dve")
        h2T_act = sem("h2T_act")
        router_done = sem("router_done")
        gate_in = sem("gate_in")
        gate_exp = sem("gate_exp")
        mask_ready = sem("mask_ready")
        rank_full = sem("rank_full")
        routed = sem("routed")
        xg_cleared = sem("xg_cleared")
        onehot_ready = sem("onehot_ready")
        idx_full = sem("idx_full")
        idx_ready = sem("idx_ready")
        xg_loaded = sems("xg_loaded", 2)
        xg_transposed = sem("xg_transposed")
        xT_dve = sem("xT_dve")
        xT_act = sem("xT_act")
        gate_full = sem("gate_full")
        up_full = sem("up_full")
        gact_ready = sem("gact_ready")
        he_ready = sem("he_ready")
        down_done = sem("down_done")
        y_evac_act = sem("y_evac_act")
        y_evac_dve = sem("y_evac_dve")
        y_stored = sem("y_stored")
        yst_free = sem("yst_free")
        ov_step = sem("ov_step")
        ov_onehot = sem("ov_onehot")
        ov_idx_full = sem("ov_idx_full")
        ov_idx_ready = sem("ov_idx_ready")
        ov_gathered = sem("ov_gathered")
        ov_w_loaded = sem("ov_w_loaded")
        ov_transposed = sem("ov_transposed")
        ov_xT_ready = sem("ov_xT_ready")
        ov_gate_full = sem("ov_gate_full")
        ov_gact_ready = sem("ov_gact_ready")
        ov_he_ready = sem("ov_he_ready")
        ov_down_done = sem("ov_down_done")
        ov_y_ready = sem("ov_y_ready")
        ov_combine_full = sem("ov_combine_full")
        ov_added = sem("ov_added")
        ov_tile_done = sem("ov_tile_done")
        ov_w_free = sem("ov_w_free")
        ov_gather_begun = sem("ov_gather_begun")
        y_all_stored = sem("y_all_stored")
        y_gathered = sems("y_gathered", 2)
        acc_ready = sem("acc_ready")
        acc_squared = sem("acc_squared")
        out_ready = sem("out_ready")
        out_stored = sems("out_stored", 2)

        block = ctx.enter_context(nc.Block())
        V_BLK, K_BLK, Q_BLK, U_BLK = 3, 2, 1, 0
        IN_ORDER = (V_BLK, K_BLK, Q_BLK, U_BLK)

        @block.sync
        def _(sp):
            def load_x(t):
                src = xp[t] if t < PT else xs
                sp.dma_start(xraw[0:rows(t), t % 2, :], src).then_inc(x_loaded[t % 2], 16)

            def load_w_in(j):
                b = IN_ORDER[j]
                sp.dma_start(w_in_sb[j % 2], win_v[:, :, b * PW:(b + 1) * PW]).then_inc(w_in_loaded[j % 2], 16)

            def load_expert(slot, e, signal=None):
                signal = signal or ring_loaded[slot]
                sp.dma_start(ring[slot][:, 0:WB], wg_v[DS(e, 1)].rearrange("a p n -> (a p) n")).then_inc(signal, 16)
                sp.dma_start(ring[slot][:, WB:2 * WB], wu_v[DS(e, 1)].rearrange("a p n -> (a p) n")).then_inc(signal, 16)
                sp.dma_start(wd_sb[slot], wd_v[DS(e, 1)].rearrange("a p c n -> (a p) c n")).then_inc(signal, 16)

            load_x(0)
            sp.dma_start(gmix_sb[:, :], g_mix.rearrange("a (p k) -> (a p) k", k=KC)).then_inc(gmix_loaded, 16)
            load_w_in(0)
            load_x(1)
            for t in range(2, NT):
                sp.wait_ge(xn_ready, t - 1)
                load_x(t)
            load_w_in(1)
            sp.dma_start(kc_raw, ck_v).then_inc(cache_loaded, 16)
            sp.dma_start(hist_in[:, :], state_pool.rearrange("a b s c -> (a b s) c")).then_inc(cache_loaded, 16)
            sp.dma_start(v_sa[:, 0:2, :], cv_v).then_inc(cache_loaded, 16)
            for n, v in enumerate((lam_q1, lam_q2, lam_k1, lam_k2)):
                sp.dma_start(lam_in[:, n, :], v).then_inc(lam_loaded, 16)
            sp.dma_start(gsub[:, :], g_subln.rearrange("a (v o) -> (a v) o", o=1)).then_inc(gsub_loaded, 16)
            with nc.allow_non_contiguous_dma(reason="512 scale values"):
                sp.dma_start(pscale[:, :], pool_scale.rearrange("a (g p) -> p (a g)", p=P)).then_inc(w_pool_loaded, 16)
            for j in (2, 3):
                sp.wait_ge(*((v_full, NT) if j == 2 else (qk_full, H)))
                load_w_in(j)
                if j == 2:
                    sp.wait_ge(x_transposed, NT)
                    sp.dma_start(w_pool_sb, w_pool.rearrange("a g c e -> c (a g) e")).then_inc(w_pool_loaded, 16)
            sp.dma_start(w_out_sb, wout_v).then_inc(w_out_loaded, 16)
            sp.dma_start(gffn_sb[:, :], g_ffn.rearrange("a (p k) -> (a p) k", k=KC)).then_inc(consts_loaded, 16)
            sp.dma_start(wr[:, :, 0:G], w_group.rearrange("a (p k) g -> (a p) k g", k=KC)).then_inc(consts_loaded, 16)
            sp.dma_start(wr[:, :, G:NL], w_erouter.rearrange("a (p k) g -> (a p) k g", k=KC)).then_inc(consts_loaded, 16)
            sp.dma_start(bias[:, 0:G], b_group.to_broadcast([P, G])).then_inc(consts_loaded, 16)
            sp.dma_start(bias[:, G:NL], b_erouter.to_broadcast([P, E])).then_inc(consts_loaded, 16)
            load_expert(0, 0)
            sp.wait_ge(scores_full, UNITS)
            for t in range(NT):
                src = xp[t] if t < PT else xs
                sp.dma_start(x2[0:rows(t), t, :], src).then_inc(xres_loaded[t], 16)
            sp.wait_ge(u_full, H)
            load_expert(1, 1)
            load_expert(2, 2)
            sp.wait_ge(op_full, NT)
            load_expert(3, 3)
            sp.dma_start(gfin, g_final.rearrange("(a d) -> a d", a=1).to_broadcast([P, D])).then_inc(gfin_loaded, 16)

            sp.sem_inc(yst_free, 2)

            def store_rows(i, b, row):
                sp.wait_ge(y_evac_act, i + 2)
                sp.wait_ge(y_evac_dve, i + 2)
                sp.dma_start(y_dram[row, :], yst[:, b, :]).then_inc(y_stored, 16)
                sp.wait_ge(y_stored, i * 16 + 16)
                sp.sem_inc(yst_free, 1)

            with sp.Fori(0, E // RING - 1) as it:
                for u in range(RING):
                    i = it * RING + u
                    sp.wait_ge(down_done, i + 1)
                    load_expert(u, i + RING)
                    store_rows(i, u % 2, DS(i * P, P))
            for i in range(E - RING, E):
                store_rows(i, i % 2, slice(i * P, (i + 1) * P))

            sp.sem_inc(y_all_stored, 1)

            sp.wait_ge(routed, 1)
            n_ov = sp.value_load(ctl[0:1, MAXOV:MAXOV + 1], min_val=0, max_val=MAXOV)
            with sp.Fori(0, MAXOV) as j:
                with sp.If(j < n_ov):
                    e = sp.value_load(ctl[0:1, DS(j, 1)], min_val=0, max_val=E - 1)
                    load_expert(0, e, ov_w_loaded)
                    sp.wait_ge(ov_down_done, j + 1)
                    sp.sem_inc(ov_w_free, 1)
                sp.nop()
            for t in range(NT):
                sp.wait_ge(out_ready, t + 1)
                sp.dma_start(yp_v[t] if t < PT else ys_v, yout[0:rows(t), t % 2, :]).then_inc(out_stored[t % 2], 16)
            sp.wait_ge(out_stored[0], 48)
            sp.wait_ge(out_stored[1], 32)

        @block.gpsimd
        def _(pool):
            made = [0]

            def step(ins):
                made[0] += 1
                ins.then_inc(pool_step, 1)
                pool.wait_ge(pool_step, made[0])

            step(pool.memset(ident[:, :], 0.0))
            pool.affine_select(out=ident[:, :], in_=ident[:, :], compare_op=ALU.not_equal, fill=1.0, base=0,
                               pattern=[[-1, P]], channel_multiplier=1).then_inc(consts_made, 1)
            step(pool.memset(ones[:, :], 1.0))
            step(pool.affine_select(out=tri[:, :], in_=ones[:, :], compare_op=ALU.is_gt, fill=0.0, base=0,
                                    pattern=[[1, P]], channel_multiplier=-1))
            step(pool.iota(iota_row[:, :], pattern=[[1, P]], base=0, channel_multiplier=0,
                           allow_small_or_imprecise_dtypes=True))
            step(pool.iota(inv_cnt[:, :], pattern=[[1, 16]], base=1, channel_multiplier=0,
                           allow_small_or_imprecise_dtypes=True))
            step(pool.iota(rev[:, :], pattern=[[-1, 4]], base=4, channel_multiplier=0,
                           allow_small_or_imprecise_dtypes=True))
            step(pool.iota(e128[:, :], pattern=[[P, E]], base=0, channel_multiplier=0,
                           allow_small_or_imprecise_dtypes=True))
            step(pool.iota(jrow[:, :], pattern=[[1, MAXOV]], base=0, channel_multiplier=0,
                           allow_small_or_imprecise_dtypes=True))
            step(pool.iota(jbase[:, :], pattern=[[P, MAXOV]], base=E * P, channel_multiplier=0,
                           allow_small_or_imprecise_dtypes=True))
            step(pool.iota(tokv[:, :, 0], pattern=[[P, NT]], base=-NOWHERE, channel_multiplier=0,
                           allow_small_or_imprecise_dtypes=True))
            pool.iota(tokv[:, :, 1], pattern=[[0, NT]], base=0, channel_multiplier=1,
                      allow_small_or_imprecise_dtypes=True).then_inc(consts_made, 1)

            for t in range(NT):
                pool.wait_ge(v_evac, t + 1)
                dst = vp_v[t] if t < PT else vs_v
                src = v_pr[:, t, :] if t < PT else v_sa[0:N_SAMPLE, 2, :]
                pool.dma_start(dst, src).then_inc(v_stored, 16)
            for t in range(NT):
                pool.wait_ge(ktok_evac, t + 1)
                pool.dma_start(kp_v[t] if t < PT else ks_v, k_st[0:rows(t), t % 2, :]).then_inc(k_stored[t % 2], 16)

            pool.wait_ge(lam_made, 1)
            pool.partition_broadcast(neglam[:, :], lam_t[0:1, 6:7]).then_inc(lam_spread, 1)

            for g in range(H):
                pool.wait_ge(u_evac_act, g + 1)
                pool.wait_ge(u_evac_dve, g + 1)
                if g >= 1:
                    pool.wait_ge(diff_ready, g)
                src, shift = uext[:, g % 2, :], 1
                for lev in range(g + 1):
                    dst = usum[:, lev % 2, :]
                    lo = 2 * shift - 1
                    ins = pool.tensor_tensor(dst[:, lo:EXT], src[:, lo:EXT], src[:, lo - shift:EXT - shift], ALU.add)
                    step(ins)
                    src, shift = dst, 2 * shift
                pool.tensor_copy(ustate[:, 0, g, :], uext[:, g % 2, N_PROMPT:N_PROMPT + HIST])
                pool.tensor_copy(ustate[:, 1, g, :], uext[:, g % 2, EXT - HIST:EXT]).then_inc(u_summed, 1)
            pool.wait_ge(state_evac, 1)
            pool.dma_start(pool_prompt.rearrange("a b s c -> (a b s) c"), state_out[:, 0, :]).then_inc(state_stored, 16)
            pool.dma_start(pool_sample.rearrange("a b s c -> (a b s) c"), state_out[:, 1, :]).then_inc(state_stored, 16)

            for t in range(NT):
                pool.wait_ge(h2n_ready, t + 1)
                pool.dma_start(h2_dram[t * P:t * P + rows(t), :], h2n[0:rows(t), t % 2, :]).then_inc(h2_stored[t % 2], 16)
            pool.wait_ge(pool_full, 1)
            pool.memset(xg[:, :, :], 0.0).then_inc(xg_cleared, 1)
            pool.wait_ge(xg_cleared, 1)
            pool.wait_ge(h2_stored[0], 48)
            pool.wait_ge(h2_stored[1], 32)
            for i in range(E + 2):
                pool.wait_ge(idx_ready, i + 1)
                if i >= 2:
                    pool.wait_ge(xg_transposed, i - 1)
                pool.indirect_dma_start(
                    out=xg[:, i % 2, :], out_offset=None, in_=h2_dram,
                    in_offset=bass.IndirectOffsetOnAxis(ap=idx[:, i % 2:i % 2 + 1], axis=0),
                    bounds_check=T - 1, oob_is_err=False).then_inc(xg_loaded[i % 2], 16)
            pool.wait_ge(xg_transposed, E + 1)
            pool.wait_ge(routed, 1)
            n_ov = pool.value_load(ctl[0:1, MAXOV:MAXOV + 1], min_val=0, max_val=MAXOV)
            with pool.Fori(0, MAXOV) as j:
                with pool.If(j < n_ov):
                    pool.wait_ge(ov_idx_ready, j + 1)
                    pool.sem_inc(ov_gather_begun, 1)
                    pool.indirect_dma_start(
                        out=xg[:, 0, :], out_offset=None, in_=h2_dram,
                        in_offset=bass.IndirectOffsetOnAxis(ap=idx[:, 0:1], axis=0),
                        bounds_check=T - 1, oob_is_err=False).then_inc(ov_gathered, 16)
                pool.nop()
            pool.wait_ge(y_all_stored, 1)
            for t in range(NT):
                if t >= 2:
                    pool.wait_ge(acc_ready, t - 1)
                n = rows(t)
                for c, dst in ((0, y1), (1, y2)):
                    pool.indirect_dma_start(
                        out=dst[0:n, t % 2, :], out_offset=None, in_=y_dram,
                        in_offset=bass.IndirectOffsetOnAxis(ap=yslot[0:n, c, t:t + 1], axis=0),
                        bounds_check=NSLOT - 1, oob_is_err=False).then_inc(y_gathered[t % 2], 16)
            pool.wait_ge(v_stored, 16 * NT)
            pool.wait_ge(k_stored[0], 48)
            pool.wait_ge(k_stored[1], 32)
            pool.wait_ge(state_stored, 32)

        @block.tensor
        def _(pe):
            def transpose_x(t):
                n = rows(t)
                pe.wait_ge(xn_ready, t + 1)
                if t == 0:
                    pe.wait_ge(consts_made, 1)
                if t >= 2:
                    pe.wait_ge(hT_dve, t - 1)
                    pe.wait_ge(hT_act, t - 1)
                src = xn[0:n, t % 2, :].rearrange("p (q k) -> p k q", k=KC)
                for k in range(KC):
                    o = ps[:, 2 * (t % 2) + k // 4, (k % 4) * P:(k % 4) * P + n]
                    ins = pe.transpose(o, src[:, k, :], ident[0:n, 0:n])
                ins.then_inc(x_transposed, 1)

            def project_v(t):
                n = rows(t)
                pe.wait_ge(hT_dve, t + 1)
                pe.wait_ge(hT_act, t + 1)
                if t == 0:
                    pe.wait_ge(w_in_loaded[0], 16)
                if t >= 2:
                    pe.wait_ge(v_evac, t - 1)
                for k in range(KC):
                    ins = pe.matmul(ps[0:n, 4 + t % 2, :], hT[:, k, t * P:t * P + n], w_in_sb[0][:, k, :],
                                    start=(k == 0), stop=(k == KC - 1))
                ins.then_inc(v_full, 1)

            def project_head(j):
                c = j % H
                w = w_in_sb[1 if j < H else 0]
                if j == 0:
                    pe.wait_ge(w_in_loaded[1], 16)
                    pe.wait_ge(v_evac, NT)
                if j == H:
                    pe.wait_ge(w_in_loaded[0], 32)
                if j >= 2:
                    pe.wait_ge(qkp_evac, j - 1)
                    pe.wait_ge(qks_evac, j - 1)
                for k in range(KC):
                    lhs = w[:, k, c * P:(c + 1) * P]
                    pe.matmul(ps[:, 4 + j % 2, :], lhs, hT[:, k, 0:N_PROMPT], start=(k == 0), stop=(k == KC - 1))
                    ins = pe.matmul(ps[:, 6 + j % 2, 0:N_SAMPLE], lhs, hT[:, k, N_PROMPT:T],
                                    start=(k == 0), stop=(k == KC - 1))
                ins.then_inc(qk_full, 1)

            transpose_x(0)
            transpose_x(1)
            for t in range(NT):
                project_v(t)
                if t + 2 < NT:
                    transpose_x(t + 2)
            for j in range(H):
                project_head(j)
            project_head(H)
            pe.wait_ge(qkp_evac, H)
            pe.wait_ge(qks_evac, H)
            pe.wait_ge(hT_dve, NT)
            pe.wait_ge(hT_act, NT)
            for t in range(NT):
                n = rows(t)
                if t == 4:
                    pe.wait_ge(ktok_evac, 1)
                for h in range(H):
                    ins = pe.transpose(ps[0:n, t % 4, h * P:(h + 1) * P], kT[:, h, t * P:t * P + n], ident[:, :])
                ins.then_inc(ktok_full, 1)
            pe.wait_ge(cache_loaded, 48)
            for c in range(2):
                pe.wait_ge(ktok_evac, 2 + c)
                for h in range(2):
                    for t in range(2):
                        ins = pe.transpose(ps[:, 1 + c, (2 * h + t) * P:(2 * h + t + 1) * P],
                                           kc_raw[:, t, (2 * c + h) * P:(2 * c + h + 1) * P], ident[:, :])
                ins.then_inc(kc_full, 1)
            pe.wait_ge(ktok_evac, 4)
            for g in range(H):
                ins = pe.transpose(ps[:, 3, g * HIST:(g + 1) * HIST], hist_in[:, g * P:(g + 1) * P],
                                   ident[0:HIST, 0:HIST])
            ins.then_inc(hist_full, 1)
            for j in range(H + 1, 2 * H):
                project_head(j)

            pe.wait_ge(qkp_evac, 2 * H)
            pe.wait_ge(qks_evac, 2 * H)
            pe.wait_ge(kc_evac, 2)
            pe.wait_ge(ktok_evac, NT)
            pe.wait_ge(hist_evac, 1)

            def scores(n):
                t, h = divmod(n, H)
                b = 2 * (n % 2)
                if n >= 2:
                    pe.wait_ge(exp_done, n - 1)
                for c in range(2):
                    r = slice(c * HD, (c + 1) * HD)
                    q = qT[r, h, t * P:t * P + rows(t)]
                    if t < PT:
                        ins = pe.matmul(ps[:, b + c, 0:(t + 1) * P], q, kT[r, h, 0:(t + 1) * P], start=True, stop=True)
                    else:
                        pe.matmul(ps[0:N_SAMPLE, b + c, 0:PAST], q, kcT[r, h, :], start=True, stop=True)
                        ins = pe.matmul(ps[0:N_SAMPLE, b + c, PAST:PAST + N_SAMPLE], q, kT[r, h, N_PROMPT:T],
                                        start=True, stop=True)
                ins.then_inc(scores_full, 1)

            def key_tiles(t):
                return [(k, P) for k in range(t + 1)] if t < PT else [(0, P), (1, P), (2, N_SAMPLE)]

            def transpose_a(n):
                t, h = divmod(n, H)
                m = rows(t)
                pe.wait_ge(a_ready, n + 1)
                if n >= 1:
                    pe.wait_ge(aT_evac, n)
                if n >= 6 and (n - 6) % H == 0:
                    pe.wait_ge(oT_evac, (n - 6) // H + 1)
                for k, keys in key_tiles(t):
                    ins = pe.transpose(ps[0:keys, 4, k * P:k * P + m], prob[0:m, n % 2, 0, k * P:k * P + keys],
                                       ident[0:m, 0:m])
                ins.then_inc(aT_full, 1)

            def weighted_values(n):
                t, h = divmod(n, H)
                m = rows(t)
                pe.wait_ge(aT_evac, n + 1)
                if n == UNITS - H:
                    pe.wait_ge(cache_loaded, 48)
                if h == 0 and t >= 1:
                    pe.wait_ge(o_ready, t)
                tiles = key_tiles(t)
                for k, keys in tiles:
                    v = (v_pr if t < PT else v_sa)[0:keys, k, h * VD:(h + 1) * VD]
                    ins = pe.matmul(ps[0:m, 5, h * VD:(h + 1) * VD], aT[0:keys, n % 2, k * P:k * P + m], v,
                                    start=(k == 0), stop=(k == len(tiles) - 1))
                ins.then_inc(pv_done, 1)

            def transpose_o(t):
                m = rows(t)
                pe.wait_ge(o_ready, t + 1)
                for h in range(H):
                    ins = pe.transpose(ps[:, 4, h * P:h * P + m], otok[0:m, h * VD:(h + 1) * VD], ident[0:m, 0:m])
                ins.then_inc(oT_full, 1)

            def project_u(n, half):
                if n >= 4 * H:
                    return
                g, k = n // 4, 2 * (n % 4) + half
                if n == 0 and half == 0:
                    pe.wait_ge(w_in_loaded[1], 32)
                if k == 0 and g >= 1:
                    pe.wait_ge(u_evac_act, g)
                    pe.wait_ge(u_evac_dve, g)
                lhs = w_in_sb[1][:, k, g * P:(g + 1) * P]
                pe.matmul(ps[:, 6, :], lhs, hT[:, k, 0:N_PROMPT], start=(k == 0), stop=(k == KC - 1))
                ins = pe.matmul(ps[:, 7, 0:N_SAMPLE], lhs, hT[:, k, N_PROMPT:T], start=(k == 0), stop=(k == KC - 1))
                if k == KC - 1:
                    ins.then_inc(u_full, 1)

            scores(0)
            for n in range(UNITS):
                if n + 1 < UNITS:
                    scores(n + 1)
                project_u(n, 0)
                transpose_a(n)
                project_u(n, 1)
                weighted_values(n)
                if n >= 5 and (n - 5) % H == 0:
                    transpose_o((n - 5) // H)

            pe.wait_ge(exp_done, UNITS)
            pe.wait_ge(u_evac_act, H)
            pe.wait_ge(u_evac_dve, H)
            pe.wait_ge(w_pool_loaded, 32)
            for g in range(H):
                pe.wait_ge(diff_ready, g + 1)
                pe.matmul(ps[:, g, :], w_pool_sb[:, g, :], mixT[:, g, 0:N_PROMPT], start=True, stop=True)
                ins = pe.matmul(ps[:, 7, g * N_SAMPLE:(g + 1) * N_SAMPLE], w_pool_sb[:, g, :],
                                mixT[:, g, N_PROMPT:T], start=True, stop=True)
            ins.then_inc(pool_full, 1)
            transpose_o(NT - 1)
            for b in range(2):
                for g in range(H):
                    ins = pe.transpose(ps[0:HIST, 5 + b, g * P:(g + 1) * P], ustate[:, b, g, :], ident[:, :])
            ins.then_inc(state_full, 1)

            def project_out(t):
                n = rows(t)
                if t == 0:
                    pe.wait_ge(w_out_loaded, 16)
                    pe.wait_ge(oT_evac, NT)
                    pe.wait_ge(pool_evac_act, 1)
                    pe.wait_ge(pool_evac_dve, 1)
                if t >= 2:
                    pe.wait_ge(x2_ready, t - 1)
                for half in range(2):
                    for f in range(KC):
                        ins = pe.matmul(ps[0:n, 2 * (t % 2) + half, :], mixT[:, f, t * P:t * P + n],
                                        w_out_sb[:, f, half * 512:(half + 1) * 512],
                                        start=(f == 0), stop=(f == KC - 1))
                ins.then_inc(op_full, 1)

            def route(t):
                n = rows(t)
                pe.wait_ge(h2n_ready, t + 1)
                if t == 0:
                    pe.wait_ge(state_evac, 1)
                else:
                    pe.wait_ge(h2T_dve, t)
                    pe.wait_ge(h2T_act, t)
                src = h2n[0:n, t % 2, :].rearrange("p (q k) -> p k q", k=KC)
                for k in range(KC):
                    ins = pe.transpose(ps[:, 4 + k // 4, (k % 4) * P:(k % 4) * P + n], src[:, k, :], ident[0:n, 0:n])
                ins.then_inc(h2_transposed, 1)
                pe.wait_ge(h2T_dve, t + 1)
                pe.wait_ge(h2T_act, t + 1)
                if t == 0:
                    pe.wait_ge(consts_loaded, 80)
                for k in range(KC):
                    ins = pe.matmul(ps[:, 6, t * NL:(t + 1) * NL], h2T[:, k, :], wr[:, k, :],
                                    start=(k == 0), stop=(k == KC - 1))
                ins.then_inc(router_done, 1)

            project_out(0)
            for t in range(1, NT):
                project_out(t)
                route(t - 1)
            route(NT - 1)

            pe.wait_ge(mask_ready, 1)
            pe.matmul(ps[:, 7, 0:NT * E], tri[:, :], msum_b.rearrange("p t e -> p (t e)"), start=True, stop=True)
            pe.matmul(ps[:, 7, 128:128 + NT * E], ones[:, :], msum_b.rearrange("p t e -> p (t e)"),
                      start=True, stop=True).then_inc(rank_full, 1)

            def slot_tokens(b, signal):
                for t in range(NT):
                    ins = pe.matmul(ps[:, 6 + b, 0:2], onehot_all[:, b, t, :], tokv[:, t, :], start=(t == 0), stop=(t == NT - 1))
                ins.then_inc(signal, 1)

            def transpose_rows(b, signal):
                src = xg[:, b, :].rearrange("p (q k) -> p k q", k=KC)
                for k in range(KC):
                    ins = pe.transpose(ps[:, k // 4, (k % 4) * P:(k % 4 + 1) * P], src[:, k, :], ident[:, :])
                ins.then_inc(signal, 1)

            def gate_up(slot, b, gate_signal, up_signal):
                for w, bank, signal in ((wg_sb[slot], 2, gate_signal), (wu_sb[slot], 3, up_signal)):
                    for c in range(FC):
                        for k in range(KC):
                            ins = pe.matmul(ps[:, bank, c * P:(c + 1) * P], w[:, k, c * P:(c + 1) * P],
                                            xT[:, b, k, :], start=(k == 0), stop=(k == KC - 1))
                    if signal is not None:
                        ins.then_inc(signal, 1)

            def down(slot, b, signal):
                for half in range(2):
                    for c in range(FC):
                        ins = pe.matmul(ps[:, 4 + half, :], heT[:, b, c, :], wd_sb[slot][:, c, half * 512:(half + 1) * 512],
                                        start=(c == 0), stop=(c == FC - 1))
                ins.then_inc(signal, 1)

            for i in range(2):
                pe.wait_ge(onehot_ready, i + 1)
                slot_tokens(i, idx_full)
            pe.wait_ge(x2_ready, NT)
            pe.wait_ge(xg_loaded[0], 16)
            transpose_rows(0, xg_transposed)
            with pe.Fori(0, E // RING) as it:
                for u in range(RING):
                    i = it * RING + u
                    b = u % 2
                    pe.wait_ge(onehot_ready, i + 3)
                    pe.wait_ge(idx_ready, i + 1)
                    slot_tokens(b, idx_full)
                    pe.wait_ge(xT_dve, i + 1)
                    pe.wait_ge(xT_act, i + 1)
                    pe.wait_ge(ring_loaded[u], it * 48 + 48)
                    gate_up(u, b, gate_full, up_full)
                    pe.wait_ge(xg_loaded[1 - b], it * (8 * RING) + 16 * ((u + 1) // 2 + 1))
                    transpose_rows(1 - b, xg_transposed)
                    pe.wait_ge(he_ready, i + 1)
                    pe.wait_ge(y_evac_act, i + 1)
                    pe.wait_ge(y_evac_dve, i + 1)
                    down(u, b, down_done)

            n_ov = pe.value_load(ctl[0:1, MAXOV:MAXOV + 1], min_val=0, max_val=MAXOV)
            pe.wait_ge(idx_ready, E + 2)
            pe.wait_ge(xT_dve, E + 1)
            pe.wait_ge(xT_act, E + 1)
            pe.wait_ge(y_evac_act, E + 1)
            pe.wait_ge(y_evac_dve, E + 1)
            with pe.Fori(0, MAXOV) as j:
                with pe.If(j < n_ov):
                    pe.wait_ge(ov_onehot, j + 1)
                    for c in range(2):
                        for t in range(NT):
                            ins = pe.matmul(ps[:, 6, 0:2], onehot_all[:, c, t, :], tokv[:, t, :],
                                            start=(c == 0 and t == 0), stop=(c == 1 and t == NT - 1))
                    ins.then_inc(ov_idx_full, 1)
                    pe.wait_ge(ov_gathered, j * 16 + 16)
                    transpose_rows(0, ov_transposed)
                    pe.wait_ge(ov_xT_ready, j + 1)
                    pe.wait_ge(ov_w_loaded, j * 48 + 48)
                    gate_up(0, 0, None, ov_gate_full)
                    pe.wait_ge(ov_he_ready, j + 1)
                    down(0, 0, ov_down_done)
                    pe.wait_ge(ov_y_ready, j + 1)
                    for t in range(NT):
                        if t >= 2:
                            pe.wait_ge(ov_added, j * NT + (t - 1))
                        for half in range(2):
                            ins = pe.matmul(ps[0:rows(t), 4 - 2 * (t % 2) + half, :], slot_to_token[:, t, 0:rows(t)],
                                            yst[:, 0, half * 512:(half + 1) * 512], start=True, stop=True)
                        ins.then_inc(ov_combine_full, 1)
                pe.nop()

        @block.scalar
        def _(act):
            def transposed_times_gain(out, banks_col, gain, n, signal):
                for k in range(4):
                    ins = act.activation(out[:, 4 + k, 0:n], banks_col[:, k * P:k * P + n], ACT.Copy,
                                         scale=gain[:, 4 + k:5 + k])
                ins.then_inc(signal, 1)

            def hT_evac(t):
                n = rows(t)
                act.wait_ge(x_transposed, t + 1)
                if t == 0:
                    act.wait_ge(gmix_loaded, 16)
                transposed_times_gain(hT[:, :, t * P:t * P + n], ps[:, 2 * (t % 2) + 1, :], gmix_sb, n, hT_act)

            def v_out(t):
                n = rows(t)
                act.wait_ge(v_full, t + 1)
                dst = v_pr[:, t, :] if t < PT else v_sa[0:N_SAMPLE, 2, :]
                act.copy(dst, ps[0:n, 4 + t % 2, :]).then_inc(v_evac, 1)

            for t in range(NT):
                n = rows(t)
                act.wait_ge(x_loaded[t % 2], 16 * (t // 2 + 1))
                if t >= 2:
                    act.wait_ge(x_transposed, t - 1)
                act.activation(xn[0:n, t % 2, :], xraw[0:n, t % 2, :], ACT.Square,
                               accum_out=ss[0:n, t:t + 1]).then_inc(x_squared, 1)
                if t >= 1:
                    hT_evac(t - 1)
                if t >= 2:
                    v_out(t - 2)
            hT_evac(NT - 1)
            v_out(NT - 2)
            v_out(NT - 1)

            def head_out(j):
                act.wait_ge(qk_full, j + 1)
                dst = (kT if j < H else qT)[:, j % H, 0:N_PROMPT]
                act.copy(dst, ps[:, 4 + j % 2, :]).then_inc(qkp_evac, 1)

            for j in range(H + 1):
                head_out(j)
            act.wait_ge(lam_dots, 1)
            act.activation(lam_t[:, 2:4], lam_t[:, 0:2], ACT.Exp).then_inc(lam_exp, 1)
            for c in range(2):
                act.wait_ge(kc_full, c + 1)
                act.copy(kcT[:, 2 * c:2 * c + 2, :], ps[:, 1 + c, :].rearrange("p (h t) -> p h t", h=2)).then_inc(kc_evac, 1)
            for j in range(H + 1, 2 * H):
                head_out(j)

            def exps(n):
                t, h = divmod(n, H)
                m, w = rows(t), (t + 1) * P if t < PT else PAST + N_SAMPLE
                act.wait_ge(negm_ready, n + 1)
                if n >= 2:
                    act.wait_ge(aT_full, n - 1)
                for c in range(2):
                    ins = act.activation(prob[0:m, n % 2, c, 0:w], ps[0:m, 2 * (n % 2) + c, 0:w], ACT.Exp,
                                         bias=negm[0:m, n % 2, c:c + 1], scale=SCALE,
                                         accum_out=psums[0:m, t, h, c:c + 1])
                ins.then_inc(exp_done, 1)

            def aT_out(n):
                t, h = divmod(n, H)
                act.wait_ge(aT_full, n + 1)
                if n >= 2:
                    act.wait_ge(pv_done, n - 1)
                if t < PT:
                    w = (t + 1) * P
                    act.copy(aT[:, n % 2, 0:w], ps[:, 4, 0:w]).then_inc(aT_evac, 1)
                else:
                    two = lambda a: a.rearrange("p (k q) -> p k q", k=2)[:, :, 0:N_SAMPLE]
                    act.copy(two(aT[:, n % 2, 0:2 * P]), two(ps[:, 4, 0:2 * P]))
                    act.copy(aT[0:N_SAMPLE, n % 2, 2 * P:2 * P + N_SAMPLE],
                             ps[0:N_SAMPLE, 4, 2 * P:2 * P + N_SAMPLE]).then_inc(aT_evac, 1)

            def o_squares(t):
                m = rows(t)
                act.wait_ge(pv_done, H * (t + 1))
                if t >= 1:
                    act.wait_ge(oT_full, t)
                for h in range(H):
                    ins = act.activation(otok[0:m, h * VD:(h + 1) * VD], ps[0:m, 5, h * VD:(h + 1) * VD], ACT.Square,
                                         accum_out=oss[0:m, t, h:h + 1])
                ins.then_inc(o_squared, 1)

            def u_out(g):
                act.wait_ge(u_full, g + 1)
                if g >= 2:
                    act.wait_ge(u_summed, g - 1)
                    act.wait_ge(diff_ready, g - 1)
                else:
                    act.wait_ge(xn_ready, NT)
                act.copy(uext[:, g % 2, HIST:HIST + N_PROMPT], ps[:, 6, :]).then_inc(u_evac_act, 1)

            exps(0)
            for n in range(UNITS):
                if n + 1 < UNITS:
                    exps(n + 1)
                if n % H == 0 and n >= H:
                    u_out(n // H - 1)
                    o_squares(n // H - 1)
                aT_out(n)
            o_squares(NT - 1)
            act.wait_ge(pool_full, 1)
            for g in range(H):
                ins = act.activation(mixT[:, g, 0:N_PROMPT], ps[:, g, :], ACT.Copy, scale=pscale[:, g:g + 1])
            ins.then_inc(pool_evac_act, 1)

            def h2_square(t):
                n = rows(t)
                act.wait_ge(x2_ready, t + 1)
                if t >= 2:
                    act.wait_ge(h2_transposed, t - 1)
                    act.wait_ge(h2_stored[t % 2], 16 * (t // 2))
                act.activation(h2n[0:n, t % 2, :], x2[0:n, t, :], ACT.Square,
                               accum_out=ss[0:n, t:t + 1]).then_inc(x2_squared, 1)

            def h2T_evac(t):
                act.wait_ge(h2_transposed, t + 1)
                if t >= 1:
                    act.wait_ge(router_done, t)
                transposed_times_gain(h2T, ps[:, 5, :], gffn_sb, rows(t), h2T_act)

            act.wait_ge(consts_loaded, 80)
            act.wait_ge(pv_done, UNITS)
            act.wait_ge(v_stored, 16 * NT)
            for t in range(NT):
                h2_square(t)
                if t >= 1:
                    h2T_evac(t - 1)
            h2T_evac(NT - 1)

            act.wait_ge(gate_in, 1)
            act.activation(gex, gex, ACT.Exp).then_inc(gate_exp, 1)
            act.wait_ge(gate_in, 2)
            act.activation(rt1[:, 3, :], rt1[:, 3, :], ACT.Exp).then_inc(gate_exp, 1)

            def rows_out(b, k):
                return act.activation(xT[:, b, k, :], ps[:, 1, (k - 4) * P:(k - 3) * P], ACT.Copy, scale=gffn_sb[:, k:k + 1])

            act.wait_ge(h2T_dve, NT)
            act.sem_inc(y_evac_act, 1)
            act.wait_ge(xg_transposed, 1)
            for k in range(4, KC):
                ins = rows_out(0, k)
            ins.then_inc(xT_act, 1)
            act.wait_ge(routed, 1)
            with act.Fori(0, E // RING) as it:
                for u in range(RING):
                    i = it * RING + u
                    b = u % 2
                    act.wait_ge(gate_full, i + 1)
                    act.activation(gact[:, b], ps[:, 2, 0:FE].rearrange("p (c s) -> p c s", c=FC),
                                   ACT.Silu).then_inc(gact_ready, 1)
                    act.wait_ge(xg_transposed, i + 2)
                    for k in range(4, KC):
                        ins = rows_out(1 - b, k)
                    ins.then_inc(xT_act, 1)
                    act.wait_ge(down_done, i + 1)
                    act.wait_ge(yst_free, i + 1)
                    act.copy(yst[:, b, 0:512], ps[:, 4, :]).then_inc(y_evac_act, 1)
            n_ov = act.value_load(ctl[0:1, MAXOV:MAXOV + 1], min_val=0, max_val=MAXOV)
            with act.Fori(0, MAXOV) as j:
                with act.If(j < n_ov):
                    act.wait_ge(ov_gate_full, j + 1)
                    act.activation(gact[:, 0], ps[:, 2, 0:FE].rearrange("p (c s) -> p c s", c=FC),
                                   ACT.Silu).then_inc(ov_gact_ready, 1)
                act.nop()
            act.wait_ge(y_all_stored, 1)
            for t in range(NT):
                n = rows(t)
                act.wait_ge(acc_ready, t + 1)
                if t >= 2:
                    act.wait_ge(out_stored[t % 2], 16 * (t // 2))
                act.activation(yout[0:n, t % 2, :], acc[0:n, t % 2, :], ACT.Square,
                               accum_out=ss[0:n, t:t + 1]).then_inc(acc_squared, 1)

        @block.vector
        def _(dve):
            steps = [0]

            def step(ins):
                steps[0] += 1
                ins.then_inc(dve_step, 1)
                dve.wait_ge(dve_step, steps[0])

            def wide(a, shape):
                return a.unsqueeze(len(a.shape)).to_broadcast(shape)

            def inverse_root(y, m, tmp, half):
                step(dve.tensor_scalar(tmp.bitcast(I32), m.bitcast(I32), 1, None, ALU.arith_shift_right))
                step(dve.tensor_scalar(y.bitcast(I32), tmp.bitcast(I32), -1.0, float(0x5F3759DF), ALU.mult, ALU.add))
                step(dve.tensor_scalar(half, m, -0.5, None, ALU.mult))
                for _ in range(4):
                    step(dve.tensor_tensor(tmp, y, y, ALU.mult))
                    step(dve.tensor_tensor(tmp, tmp, half, ALU.mult))
                    step(dve.scalar_tensor_tensor(y, tmp, 1.5, y, ALU.add, ALU.mult))

            def row_scale(t):
                n = rows(t)
                m, y, tmp, half = (rs[0:n, 1, t:t + 1], rs[0:n, 0, t:t + 1], rs[0:n, 2, t:t + 1], ovoff[0:n, t:t + 1])
                step(dve.tensor_scalar(m, ss[0:n, t:t + 1], 1.0 / D, EPS, ALU.mult, ALU.add))
                inverse_root(y, m, tmp, half)
                return y

            def hT_evac(t):
                n = rows(t)
                dve.wait_ge(x_transposed, t + 1)
                if t == 0:
                    dve.wait_ge(gmix_loaded, 16)
                dve.tensor_tensor(hT[:, 0:4, t * P:t * P + n],
                                  ps[:, 2 * (t % 2), :].rearrange("p (k t) -> p k t", k=4)[:, :, 0:n],
                                  wide(gmix_sb[:, 0:4], [P, 4, n]), ALU.mult).then_inc(hT_dve, 1)

            for t in range(NT):
                n = rows(t)
                dve.wait_ge(x_squared, t + 1)
                y = row_scale(t)
                dve.tensor_scalar(xn[0:n, t % 2, :], xraw[0:n, t % 2, :], y, None, ALU.mult).then_inc(xn_ready, 1)
                if t >= 1:
                    hT_evac(t - 1)
            hT_evac(NT - 1)

            dve.wait_ge(lam_loaded, 64)
            step(dve.tensor_tensor(lam_in[:, 0:2, :], lam_in[:, 0:2, :], lam_in[:, 2:4, :], ALU.mult))
            dve.tensor_reduce(lam_t[:, 0:2], lam_in[:, 0:2, :], X, ALU.add).then_inc(lam_dots, 1)
            dve.wait_ge(consts_made, 2)
            step(dve.reciprocal(inv_cnt[:, :], inv_cnt[:, :]))
            dve.wait_ge(gsub_loaded, 16)
            step(dve.tensor_scalar(gsub[:, :], gsub[:, :], 1.0 - LAMBDA_INIT, None, ALU.mult))

            def head_out(j):
                dve.wait_ge(qk_full, j + 1)
                dst = (kT if j < H else qT)[:, j % H, N_PROMPT:T]
                dve.tensor_copy(dst, ps[:, 6 + j % 2, 0:N_SAMPLE]).then_inc(qks_evac, 1)

            for j in range(H + 1):
                head_out(j)
            for t in range(NT):
                n = rows(t)
                dve.wait_ge(ktok_full, t + 1)
                if t >= 2:
                    dve.wait_ge(k_stored[t % 2], 16 * (t // 2))
                dve.tensor_copy(k_st[0:n, t % 2, :], ps[0:n, t % 4, :]).then_inc(ktok_evac, 1)
            dve.wait_ge(hist_full, 1)
            dve.tensor_copy(histT[:, :, :], ps[:, 3, 0:H * HIST].rearrange("p (g s) -> p g s", g=H)).then_inc(hist_evac, 1)
            dve.wait_ge(lam_exp, 1)
            step(dve.tensor_tensor(lam_t[:, 4:5], lam_t[:, 3:4], lam_t[:, 2:3], ALU.subtract))
            dve.tensor_scalar(lam_t[:, 6:7], lam_t[:, 4:5], -LAMBDA_INIT, None, ALU.add).then_inc(lam_made, 1)
            for j in range(H + 1, 2 * H):
                head_out(j)

            def maxima(n):
                t, h = divmod(n, H)
                m, w, b = rows(t), (t + 1) * P if t < PT else PAST + N_SAMPLE, 2 * (n % 2)
                dve.wait_ge(scores_full, n + 1)
                if t < PT:
                    step(dve.memset(ps[0:CHUNK, b:b + 2, w - CHUNK:w], NEG))
                if n >= 2:
                    dve.wait_ge(exp_done, n - 1)
                step(dve.tensor_reduce(mx[0:m, n % 2, :], ps[0:m, b:b + 2, 0:w], X, ALU.max))
                dve.tensor_scalar(negm[0:m, n % 2, :], mx[0:m, n % 2, :], -SCALE, None, ALU.mult).then_inc(negm_ready, 1)

            def differences(n):
                t, h = divmod(n, H)
                m, w = rows(t), (t + 1) * P if t < PT else PAST + N_SAMPLE
                dve.wait_ge(exp_done, n + 1)
                if n == 0:
                    dve.wait_ge(lam_spread, 1)
                step(dve.reciprocal(coef[0:m, 0:1], psums[0:m, t, h, 1:2]))
                step(dve.scalar_tensor_tensor(coef[0:m, 1:2], psums[0:m, t, h, 0:1], neglam[0:m, :], coef[0:m, 0:1],
                                              ALU.mult, ALU.mult))
                dve.scalar_tensor_tensor(prob[0:m, n % 2, 0, 0:w], prob[0:m, n % 2, 1, 0:w], coef[0:m, 1:2],
                                         prob[0:m, n % 2, 0, 0:w], ALU.mult, ALU.add).then_inc(a_ready, 1)

            def o_norm(t):
                m = rows(t)
                r0, q, fac = osc[0:m, 0, :], osc[0:m, 1, :], osc[0:m, 2, :]
                step(dve.reciprocal(r0, psums[0:m, t, :, 0]))
                step(dve.tensor_tensor(q, r0, r0, ALU.mult))
                dve.wait_ge(o_squared, t + 1)
                step(dve.tensor_tensor(q, q, oss[0:m, t, :], ALU.mult))
                step(dve.tensor_scalar(q, q, 1.0 / VD, EPS, ALU.mult, ALU.add))
                inverse_root(fac, q, osc[0:m, 3, :], ovoff[0:m, NT:NT + H])
                step(dve.tensor_tensor(fac, fac, r0, ALU.mult))
                dve.tensor_tensor(otok[0:m, :].rearrange("p (h v) -> p h v", h=H),
                                  ps[0:m, 5, :].rearrange("p (h v) -> p h v", h=H),
                                  wide(fac, [m, H, VD]), ALU.mult).then_inc(o_ready, 1)

            def oT_out(t):
                m = rows(t)
                dve.wait_ge(oT_full, t + 1)
                dve.tensor_scalar(mixT[:, H:2 * H, t * P:t * P + m],
                                  ps[:, 4, :].rearrange("p (h q) -> p h q", h=H)[:, :, 0:m],
                                  gsub[:, 0:1], None, ALU.mult).then_inc(oT_evac, 1)

            def u_out(g):
                dve.wait_ge(u_full, g + 1)
                if g >= 2:
                    dve.wait_ge(u_summed, g - 1)
                else:
                    step(dve.memset(uext[:, g % 2, 0:HIST], 0.0))
                step(dve.tensor_copy(uext[:, g % 2, HIST + N_PROMPT:S0], histT[:, g, :]))
                dve.tensor_copy(uext[:, g % 2, S0:EXT], ps[:, 7, 0:N_SAMPLE]).then_inc(u_evac_dve, 1)

            def window_diff(g):
                w = WINDOWS[g]
                u, s = uext[:, g % 2, :], usum[:, g % 2, :]
                dve.wait_ge(u_summed, g + 1)
                if g >= 2:
                    dve.wait_ge(dve_step, steps[0])
                step(dve.tensor_tensor(fix[:, 0:w - 1], s[:, HIST:HIST + w - 1], inv_cnt[:, 0:w - 1], ALU.mult))
                step(dve.tensor_tensor(mixT[:, g, 0:w - 1], fix[:, 0:w - 1], u[:, HIST:HIST + w - 1], ALU.subtract))
                step(dve.scalar_tensor_tensor(mixT[:, g, w - 1:N_PROMPT], s[:, HIST + w - 1:HIST + N_PROMPT], 1.0 / w,
                                              u[:, HIST + w - 1:HIST + N_PROMPT], ALU.mult, ALU.subtract))
                dve.scalar_tensor_tensor(mixT[:, g, N_PROMPT:T], s[:, S0:EXT], 1.0 / w, u[:, S0:EXT],
                                         ALU.mult, ALU.subtract).then_inc(diff_ready, 1)

            maxima(0)
            for n in range(UNITS):
                if n + 1 < UNITS:
                    maxima(n + 1)
                if n >= 6 and (n - 6) % H == 0:
                    oT_out((n - 6) // H)
                if n % H == 0 and n >= H:
                    u_out(n // H - 1)
                differences(n)
                if n % H == 0 and n >= H:
                    o_norm(n // H - 1)
                if n % H == 3 and n >= 7:
                    window_diff((n - 7) // H)
            o_norm(NT - 1)
            dve.wait_ge(pool_full, 1)
            dve.tensor_tensor(mixT[:, 0:H, N_PROMPT:T], ps[:, 7, 0:H * N_SAMPLE].rearrange("p (g t) -> p g t", g=H),
                              wide(pscale[:, :], [P, H, N_SAMPLE]), ALU.mult).then_inc(pool_evac_dve, 1)
            oT_out(NT - 1)
            dve.wait_ge(state_full, 1)
            dve.tensor_copy(state_out[:, :, :], ps[0:HIST, 5:7, :]).then_inc(state_evac, 1)

            def residual(t):
                n = rows(t)
                dve.wait_ge(op_full, t + 1)
                dve.wait_ge(xres_loaded[t], 16)
                dve.tensor_tensor(x2[0:n, t, :].rearrange("p (b d) -> p b d", b=2),
                                  ps[0:n, 2 * (t % 2):2 * (t % 2) + 2, :],
                                  x2[0:n, t, :].rearrange("p (b d) -> p b d", b=2), ALU.add).then_inc(x2_ready, 1)

            def h2_norm(t):
                n = rows(t)
                dve.wait_ge(x2_squared, t + 1)
                y = row_scale(t)
                dve.tensor_scalar(h2n[0:n, t % 2, :], x2[0:n, t, :], y, None, ALU.mult).then_inc(h2n_ready, 1)

            def h2T_evac(t):
                n = rows(t)
                dve.wait_ge(h2_transposed, t + 1)
                if t >= 1:
                    dve.wait_ge(router_done, t)
                else:
                    dve.wait_ge(consts_loaded, 80)
                if n < P:
                    step(dve.memset(h2T[:, :, n:P], 0.0))
                dve.tensor_tensor(h2T[:, 0:4, 0:n], ps[:, 4, :].rearrange("p (k t) -> p k t", k=4)[:, :, 0:n],
                                  wide(gffn_sb[:, 0:4], [P, 4, n]), ALU.mult).then_inc(h2T_dve, 1)

            for t in range(NT):
                residual(t)
                h2_norm(t)
                if t >= 1:
                    h2T_evac(t - 1)
            h2T_evac(NT - 1)

            dve.wait_ge(router_done, NT)
            dve.wait_ge(k_stored[0], 48)
            dve.wait_ge(k_stored[1], 32)
            dve.wait_ge(state_stored, 32)
            T4, T44 = [P, NT, G], [P, NT, G, EPG]
            step(dve.tensor_tensor(lg, ps[:, 6, 0:NT * NL].rearrange("p (t l) -> p t l", t=NT),
                                   bias[:, :].unsqueeze(1).to_broadcast([P, NT, NL]), ALU.add))
            gl = lg[:, :, 0:G]
            el = lg[:, :, G:NL].rearrange("p t (g j) -> p t g j", g=G)

            def first_max(src, col, out):
                step(dve.tensor_reduce(rt1[:, col, :], src, X, ALU.max))
                step(dve.tensor_tensor(rt4, src, wide(rt1[:, col, :], T4), ALU.is_equal))
                step(dve.tensor_tensor(rt4, rt4, rev[:, :].unsqueeze(1).to_broadcast(T4), ALU.mult))
                step(dve.tensor_reduce(rt1[:, 2, :], rt4, X, ALU.max))
                step(dve.tensor_tensor(out, rt4, wide(rt1[:, 2, :], T4), ALU.is_equal))

            first_max(gl, 0, g1h)
            dve.tensor_tensor(gex, gl, wide(rt1[:, 0, :], T4), ALU.subtract).then_inc(gate_in, 1)
            dve.wait_ge(gate_in, 1)
            sel = etmp.rearrange("p t (g j) -> p t g j", g=G)
            step(dve.tensor_tensor(sel, el, wide(g1h, T44), ALU.mult))
            step(dve.tensor_reduce(esel, etmp.rearrange("p t (g j) -> p t j g", g=G), X, ALU.add))
            first_max(esel, 0, top[:, 0])
            step(dve.scalar_tensor_tensor(rt4b, top[:, 0], NEG, esel, ALU.mult, ALU.add))
            first_max(rt4b, 1, top[:, 1])
            dve.tensor_tensor(rt1[:, 3, :], rt1[:, 1, :], rt1[:, 0, :], ALU.subtract).then_inc(gate_in, 1)
            for c in range(2):
                out = m12[:, c].rearrange("p t (g j) -> p t g j", g=G)
                step(dve.tensor_tensor(out, wide(g1h, T44), top[:, c].unsqueeze(2).to_broadcast(T44), ALU.mult))
            step(dve.memset(m12[N_SAMPLE:P, :, NT - 1, :], 0.0))
            step(dve.tensor_tensor(msum, m12[:, 0], m12[:, 1], ALU.add))
            dve.tensor_copy(msum_b, msum).then_inc(mask_ready, 1)
            dve.wait_ge(gate_exp, 2)
            step(dve.tensor_reduce(rt1[:, 2, :], gex, X, ALU.add))
            step(dve.tensor_scalar(rt1[:, 1, :], rt1[:, 3, :], 1.0, None, ALU.add))
            step(dve.tensor_tensor(rt1[:, 1, :], rt1[:, 1, :], rt1[:, 2, :], ALU.mult))
            step(dve.reciprocal(wtok[:, 0, :], rt1[:, 1, :]))
            step(dve.tensor_tensor(wtok[:, 1, :], wtok[:, 0, :], rt1[:, 3, :], ALU.mult))
            dve.wait_ge(rank_full, 1)
            within = ps[:, 7, 0:NT * E].rearrange("p (t e) -> p t e", t=NT)
            totals = ps[:, 7, 128:128 + NT * E].rearrange("p (t e) -> p t e", t=NT)
            step(dve.memset(base[:, 0, :], 0.0))
            for t in range(NT):
                step(dve.tensor_tensor(base[:, t + 1, :], totals[:, t, :], base[:, t, :], ALU.add))
            step(dve.tensor_tensor(rank, within, base[:, 0:NT, :], ALU.add))
            step(dve.memset(rm[:, :, E:], -1.0))
            step(dve.scalar_tensor_tensor(etmp, rank, 1.0, msum, ALU.add, ALU.mult))
            step(dve.tensor_scalar(rm[:, :, 0:E], etmp, -1.0, None, ALU.add))

            iota_t = iota_row[:, :].unsqueeze(1).to_broadcast([P, NT, P])

            def expert_onehot(e, b):
                col = rm[:, :, DS(e, 1)].rearrange("p t a -> p (t a)")
                return dve.tensor_tensor(onehot_all[:, b], iota_t, wide(col, [P, NT, P]), ALU.is_equal)

            def to_index(b):
                return dve.tensor_scalar(idx[:, b:b + 1], ps[:, 6 + b, 0:1], ps[:, 6 + b, 1:2],
                                         float(NOWHERE), ALU.add, ALU.add)

            dve.wait_ge(h2_stored[0], 48)
            dve.wait_ge(h2_stored[1], 32)
            expert_onehot(0, 0).then_inc(onehot_ready, 1)
            expert_onehot(1, 1).then_inc(onehot_ready, 1)
            for i in range(2):
                dve.wait_ge(idx_full, i + 1)
                to_index(i).then_inc(idx_ready, 1)
            expert_onehot(2, 0).then_inc(onehot_ready, 1)
            n_e = base[:, NT, :]
            step(dve.tensor_scalar(over, n_e, float(CAP), None, ALU.is_gt))
            for k in range(1, OVK):
                step(dve.scalar_tensor_tensor(over, n_e, float(CAP + k * P), over, ALU.is_gt, ALU.add))
            step(dve.tensor_copy(cum[:, 0, :], over))
            cur = 0
            for shift in (1, 2, 4, 8):
                step(dve.tensor_copy(cum[:, 1 - cur, 0:shift], cum[:, cur, 0:shift]))
                step(dve.tensor_tensor(cum[:, 1 - cur, shift:E], cum[:, cur, shift:E], cum[:, cur, 0:E - shift], ALU.add))
                cur = 1 - cur
            incl, start = cum[:, cur, :], cum[:, 1 - cur, :]
            step(dve.tensor_tensor(start, incl, over, ALU.subtract))
            step(dve.tensor_scalar(start, start, float(P), float(E * P - CAP), ALU.mult, ALU.add))
            step(dve.tensor_tensor(start, start, e128[:, :], ALU.subtract))
            step(dve.tensor_scalar(isov, rank, float(CAP), None, ALU.is_ge))
            over_e = lambda a: a.unsqueeze(1).to_broadcast([P, NT, E])
            step(dve.tensor_tensor(isov, isov, over_e(start), ALU.mult))
            step(dve.tensor_tensor(ylin, rank, isov, ALU.add))
            step(dve.tensor_tensor(ylin, ylin, over_e(e128[:, :]), ALU.add))
            for c in range(2):
                step(dve.tensor_tensor(etmp, m12[:, c], ylin, ALU.mult))
                step(dve.tensor_reduce(yslot_f[:, c, :], etmp, X, ALU.add))
            step(dve.scalar_tensor_tensor(wmain[:, :, :], yslot_f[:, :, :], float(NSLOT), wtok[:, :, :], ALU.is_lt, ALU.mult))
            step(dve.tensor_scalar(yslot[:, :, :], yslot_f[:, :, :], float(NSLOT - 1), None, ALU.min))
            step(dve.tensor_tensor(jcmp, incl.unsqueeze(1).to_broadcast([P, MAXOV, E]), wide(jrow[:, :], [P, MAXOV, E]),
                                   ALU.is_le))
            step(dve.tensor_reduce(jsum, jcmp, X, ALU.add))
            step(dve.tensor_scalar(ctl[:, 0:MAXOV], jsum[0:1, :], float(E - 1), None, ALU.min))
            dve.tensor_copy(ctl[:, MAXOV:MAXOV + 1], incl[0:1, E - 1:E]).then_inc(routed, 1)

            def rows_out(b):
                return dve.tensor_tensor(xT[:, b, 0:4, :], ps[:, 0, :].rearrange("p (k s) -> p k s", k=4),
                                         wide(gffn_sb[:, 0:4], [P, 4, P]), ALU.mult)

            dve.wait_ge(h2T_act, NT)
            dve.sem_inc(y_evac_dve, 1)
            dve.wait_ge(xg_transposed, 1)
            rows_out(0).then_inc(xT_dve, 1)
            with dve.Fori(0, E // RING) as it:
                for u in range(RING):
                    i = it * RING + u
                    b = u % 2
                    dve.wait_ge(idx_full, i + 3)
                    dve.wait_ge(xg_loaded[b], it * (8 * RING) + 16 * (u // 2 + 1))
                    to_index(b).then_inc(idx_ready, 1)
                    dve.wait_ge(gact_ready, i + 1)
                    dve.wait_ge(up_full, i + 1)
                    dve.tensor_tensor(heT[:, b], gact[:, b],
                                      ps[:, 3, 0:FE].rearrange("p (c s) -> p c s", c=FC), ALU.mult).then_inc(he_ready, 1)
                    dve.wait_ge(xg_transposed, i + 2)
                    rows_out(1 - b).then_inc(xT_dve, 1)
                    expert_onehot(i + 3, 1 - b).then_inc(onehot_ready, 1)
                    dve.wait_ge(down_done, i + 1)
                    dve.wait_ge(yst_free, i + 1)
                    dve.tensor_copy(yst[:, b, 512:1024], ps[:, 5, :]).then_inc(y_evac_dve, 1)

            n_ov = dve.value_load(ctl[0:1, MAXOV:MAXOV + 1], min_val=0, max_val=MAXOV)
            dve.wait_ge(idx_full, E + 2)
            dve.wait_ge(onehot_ready, E + 3)
            dve.wait_ge(xg_loaded[0], 16 * (E // 2 + 1))
            dve.wait_ge(xg_loaded[1], 16 * (E // 2 + 1))
            dve.wait_ge(xT_act, E + 1)
            dve.wait_ge(yst_free, E + 2)
            with dve.Fori(0, MAXOV) as j:
                with dve.If(j < n_ov):
                    def ov_do(ins, n):
                        ins.then_inc(ov_step, 1)
                        dve.wait_ge(ov_step, j * OV_STEPS + n)

                    ov_do(dve.tensor_scalar(ovoff[:, :], yslot_f[:, :, :].rearrange("p c t -> p (c t)"), jbase[:, DS(j, 1)],
                                            None, ALU.subtract), 1)
                    for c in range(2):
                        ins = dve.tensor_tensor(onehot_all[:, c], iota_t, wide(ovoff[:, c * NT:(c + 1) * NT], [P, NT, P]),
                                                ALU.is_equal)
                    ins.then_inc(ov_onehot, 1)
                    dve.wait_ge(ov_idx_full, j + 1)
                    to_index(0).then_inc(ov_idx_ready, 1)
                    offs = ovoff[:, :].rearrange("p (c t) -> p c t", c=2)
                    ov_do(dve.tensor_scalar(ovw[:, :, :], offs, 0.0, None, ALU.is_ge), 2)
                    ov_do(dve.scalar_tensor_tensor(ovw[:, :, :], offs, float(P), ovw[:, :, :], ALU.is_lt, ALU.mult), 3)
                    ov_do(dve.tensor_tensor(ovw[:, :, :], ovw[:, :, :], wtok[:, :, :], ALU.mult), 4)
                    ov_do(dve.tensor_tensor(ovw[:, 0, :], ovw[:, 0, :], ovw[:, 1, :], ALU.add), 5)
                    ov_do(dve.tensor_scalar(slot_tok[:, :], ps[:, 6, 0:1], ps[:, 6, 1:2], float(NOWHERE), ALU.add, ALU.add), 6)
                    for t in range(NT):
                        ins = dve.tensor_scalar(slot_to_token[:, t, :], iota_row[:, :], float(t * P), slot_tok[:, 0:1],
                                                ALU.add, ALU.is_equal)
                    ov_do(ins, OV_STEPS)
                    dve.wait_ge(ov_transposed, j + 1)
                    dve.tensor_tensor(xT[:, 0], ps[:, 0:2, :].rearrange("p b (k s) -> p (b k) s", k=4),
                                      wide(gffn_sb[:, :], [P, KC, P]), ALU.mult).then_inc(ov_xT_ready, 1)
                    dve.wait_ge(ov_gact_ready, j + 1)
                    dve.tensor_tensor(heT[:, 0], gact[:, 0],
                                      ps[:, 3, 0:FE].rearrange("p (c s) -> p c s", c=FC), ALU.mult).then_inc(ov_he_ready, 1)
                    dve.wait_ge(ov_down_done, j + 1)
                    dve.tensor_copy(yst[:, 0, :].rearrange("p (b d) -> p b d", b=2), ps[:, 4:6, :]).then_inc(ov_y_ready, 1)
                    for t in range(NT):
                        n, b = rows(t), 4 - 2 * (t % 2)
                        dve.wait_ge(ov_combine_full, j * NT + (t + 1))
                        xt = x2[0:n, t, :].rearrange("p (b d) -> p b d", b=2)
                        dve.scalar_tensor_tensor(xt, ps[0:n, b:b + 2, :], ovw[0:n, 0, t:t + 1], xt,
                                                 ALU.mult, ALU.add).then_inc(ov_added, 1)
                    dve.wait_ge(ov_added, (j + 1) * NT)
                    dve.sem_inc(ov_tile_done, 1)
                dve.nop()

            def combine(t):
                n, b = rows(t), t % 2
                dve.wait_ge(y_gathered[b], 32 * (t // 2 + 1))
                if t >= 2:
                    dve.wait_ge(out_ready, t - 1)
                step(dve.scalar_tensor_tensor(acc[0:n, b, :], y1[0:n, b, :], wmain[0:n, 0, t:t + 1], x2[0:n, t, :],
                                              ALU.mult, ALU.add))
                dve.scalar_tensor_tensor(acc[0:n, b, :], y2[0:n, b, :], wmain[0:n, 1, t:t + 1], acc[0:n, b, :],
                                         ALU.mult, ALU.add).then_inc(acc_ready, 1)

            def finish(t):
                n, b = rows(t), t % 2
                dve.wait_ge(acc_squared, t + 1)
                y = row_scale(t)
                dve.scalar_tensor_tensor(yout[0:n, b, :], acc[0:n, b, :], y, gfin[0:n, :],
                                         ALU.mult, ALU.mult).then_inc(out_ready, 1)

            dve.wait_ge(y_all_stored, 1)
            dve.wait_ge(gfin_loaded, 16)
            combine(0)
            for t in range(NT):
                if t + 1 < NT:
                    combine(t + 1)
                finish(t)


_INS = ["x_prompt", "x_sample", "cache_k", "cache_v", "state_pool", "g_mix", "w_in", "w_pool", "pool_scale",
        "lam_q1", "lam_k1", "lam_q2", "lam_k2", "g_subln", "w_out", "g_ffn", "w_group", "b_group", "w_erouter",
        "b_erouter", "w_gate", "w_up", "w_down", "g_final"]
_OUTS = [("y_prompt", (1, N_PROMPT, D)), ("y_sample", (1, N_SAMPLE, D)),
         ("k_prompt", (1, 1, N_PROMPT, H, 2 * HD)), ("v_prompt", (1, 1, N_PROMPT, H, VD)),
         ("pool_prompt", (1, 1, HIST, PW)),
         ("k_sample", (1, 1, N_SAMPLE, H, 2 * HD)), ("v_sample", (1, 1, N_SAMPLE, H, VD)),
         ("pool_sample", (1, 1, HIST, PW))]


def kernel(**inputs):
    import numpy as _np
    import concourse.bacc as _bacc
    from concourse.bass_utils import run_bass_kernel_spmd as _run

    nc = _bacc.Bacc("TRN2", target_bir_lowering=False, num_devices=1)
    arrays, args = {}, {}
    for name in _INS:
        a = _np.ascontiguousarray(inputs[name])
        arrays[f"in_{name}"] = a
        args[name] = nc.dram_tensor(f"in_{name}", a.shape, mybir.dt.from_np(a.dtype), kind="ExternalInput").ap()
    for name, shape in _OUTS:
        args[name] = nc.dram_tensor(f"out_{name}", shape, F32, kind="ExternalOutput").ap()
    build(nc, **args)
    r = _run(nc, [arrays], core_ids=[0])
    return tuple(r.results[0][f"out_{name}"] for name, _ in _OUTS)
```

```python
import math
from contextlib import ExitStack

import numpy as np

import concourse.bass as bass
from concourse import mybir

F32 = mybir.dt.float32
BF16 = mybir.dt.bfloat16
I32 = mybir.dt.int32
ALU = mybir.AluOpType
ACT = mybir.ActivationFunctionType
X = mybir.AxisListType.X
DS = bass.ds

P = 128
D = 1024
KC = D // P
N_PROMPT, N_SAMPLE = 512, 64
T = N_PROMPT + N_SAMPLE
NT = 5
PT = N_PROMPT // P
PAST = 256
CHUNK = 64
HIST = 15
WINDOWS = (2, 4, 8, 16)
H = 4
HD = 64
VD = 2 * HD
PW = 512
SCALE = HD ** -0.5
NEG = -1e30
LAMBDA_INIT = 0.8 - 0.6 * math.exp(0.0)
EPS = 1e-6
G, EPG = 4, 4
E = G * EPG
FE = 256
FC = FE // P
NL = G + E
CAP = 128
MAXOV = (2 * T) // (CAP + 1)
OVK = -(-(T - CAP) // P)
NSLOT = E * P
RING = 4
NOWHERE = 1024
EARLY = E - RING + 1
UNITS = NT * H
OV_STEPS = 7
WB = KC * FE


def rows(t):
    return P if t < PT else N_SAMPLE


def build(nc, x_prompt, x_sample, cache_k, cache_v, state_pool, g_mix, w_in, w_pool, pool_scale,
          lam_q1, lam_k1, lam_q2, lam_k2, g_subln, w_out, g_ffn, w_group, b_group, w_erouter,
          b_erouter, w_gate, w_up, w_down, g_final,
          y_prompt, y_sample, k_prompt, v_prompt, pool_prompt, k_sample, v_sample, pool_sample):
    ctx = ExitStack()
    with ctx:
        def sb(name, shape, dt=F32):
            return ctx.enter_context(nc.sbuf_tensor(name, shape, dt))

        def sem(name):
            return ctx.enter_context(nc.semaphore(name))

        def sems(name, n):
            return [sem(f"{name}{i}") for i in range(n)]

        xp = x_prompt.rearrange("a (t p) d -> (a t) p d", p=P)
        xs = x_sample.rearrange("a s d -> (a s) d")
        win_v = w_in.rearrange("a (p k) n -> (a p) k n", k=KC)
        wout_v = w_out.rearrange("a (f p) n -> p (a f) n", p=P)
        ck_v = cache_k.rearrange("a b (t p) h d -> p (a b t) (h d)", p=P)
        cv_v = cache_v.rearrange("a b (t p) h d -> p (a b t) (h d)", p=P)
        kp_v = k_prompt.rearrange("a b (t p) h d -> (a b t) p (h d)", p=P)
        vp_v = v_prompt.rearrange("a b (t p) h d -> (a b t) p (h d)", p=P)
        ks_v = k_sample.rearrange("a b s h d -> (a b s) (h d)")
        vs_v = v_sample.rearrange("a b s h d -> (a b s) (h d)")
        yp_v = y_prompt.rearrange("a (t p) d -> (a t) p d", p=P)
        ys_v = y_sample.rearrange("a s d -> (a s) d")
        wg_v = w_gate.rearrange("a e (p k) f -> (a e) p (k f)", k=KC)
        wu_v = w_up.rearrange("a e (p k) f -> (a e) p (k f)", k=KC)
        wd_v = w_down.rearrange("a e (c p) n -> (a e) p c n", p=P)
        h2_dram = nc.dram_tensor("h2_rows", (T, D), F32, kind="Internal").ap()
        y_dram = nc.dram_tensor("expert_rows", (NSLOT, D), F32, kind="Internal").ap()

        region_a = sb("region_a", [P, 12800])
        w_in_sb = [region_a[:, b * 4096:(b + 1) * 4096].rearrange("p (k n) -> p k n", k=KC) for b in range(2)]
        hT = region_a[:, 8192:12800].rearrange("p (k t) -> p k t", k=KC)
        region_w = sb("region_w", [P, 8192])
        w_out_sb = region_w[:, :].rearrange("p (f n) -> p f n", f=KC)
        ring0 = sb("ring0", [P, 6144])
        ring = [ring0[:, :], region_a[:, 0:6144], region_a[:, 6144:12288], region_w[:, 0:6144]]
        wg_sb = [r[:, 0:WB].rearrange("p (k f) -> p k f", k=KC) for r in ring]
        wu_sb = [r[:, WB:2 * WB].rearrange("p (k f) -> p k f", k=KC) for r in ring]
        wd_sb = [r[:, 2 * WB:3 * WB].rearrange("p (c n) -> p c n", c=FC) for r in ring]

        region_q = sb("region_q", [P, 5632])
        qT = region_q[:, 0:2304].rearrange("p (h t) -> p h t", h=H)
        kT = region_q[:, 2304:4608].rearrange("p (h t) -> p h t", h=H)
        kcT = region_q[:, 4608:5632].rearrange("p (h t) -> p h t", h=H)
        x2 = region_q[:, 0:NT * D].rearrange("p (t d) -> p t d", t=NT)

        mixT = sb("mixT", [P, KC, T])

        region_v = sb("region_v", [P, 3584])
        v_pr = region_v[:, 0:2048].rearrange("p (t n) -> p t n", t=PT)
        v_sa = region_v[:, 2048:3584].rearrange("p (t n) -> p t n", t=3)
        h2n = region_v[:, 0:2048].rearrange("p (b d) -> p b d", b=2)
        h2T = region_v[:, 2048:3072].rearrange("p (k t) -> p k t", k=KC)
        onehot_all = region_v[:, 0:640].bitcast(BF16).rearrange("p (b t s) -> p b t s", b=2, t=NT)

        region_k = sb("region_k", [P, 2048])
        kc_raw = region_k[:, 0:1024].rearrange("p (t n) -> p t n", t=2)
        k_st = ring0[:, 0:NT * PW].rearrange("p (t n) -> p t n", t=NT)
        state_out = region_k[0:HIST, 0:1024].rearrange("p (b n) -> p b n", b=2)

        region_p = sb("region_p", [P, 2048])
        prob = region_p[:, :].rearrange("p (b c k) -> p b c k", b=2, c=2)
        xT = region_p[:, :].rearrange("p (b k s) -> p b k s", b=2, k=KC)
        region_t = sb("region_t", [P, 1536])
        aT = region_t[:, 0:1024].rearrange("p (b k) -> p b k", b=2)
        otok = region_t[:, 1024:1536]
        gact = region_t[:, 0:512].rearrange("p (b c s) -> p b c s", b=2, c=FC)
        heT = region_t[:, 512:1024].rearrange("p (b c s) -> p b c s", b=2, c=FC)

        region_x = sb("region_x", [P, 4096])
        xraw = region_x[:, 0:2048].rearrange("p (b d) -> p b d", b=2)
        xn = region_x[:, 2048:4096].rearrange("p (b d) -> p b d", b=2)
        EXT = HIST + N_PROMPT + HIST + N_SAMPLE
        S0 = 2 * HIST + N_PROMPT
        uext = region_x[:, 0:2 * EXT].rearrange("p (b t) -> p b t", b=2)
        usum = region_x[:, 2 * EXT:4 * EXT].rearrange("p (b t) -> p b t", b=2)
        w_pool_sb = region_x[:, 4 * EXT:4 * EXT + 512].rearrange("p (g e) -> p g e", g=H)
        xg = region_x[:, 0:2048].rearrange("p (b d) -> p b d", b=2)
        yst = region_x[:, 2048:4096].rearrange("p (b d) -> p b d", b=2)
        slot_to_token = region_x[:, D:D + NT * P].rearrange("p (t s) -> p t s", t=NT)

        mix_flat = mixT[:, :, :].rearrange("p k t -> p (k t)")
        y1 = [mix_flat[:, t * D:(t + 1) * D] for t in range(PT)] + [region_v[:, 2048:3072]]
        y2 = [region_w[:, 6144:7168], region_w[:, 7168:8192]] + [ring0[:, t * D:(t + 1) * D] for t in range(3)]
        gfin = region_k[:, 0:D]

        ident = sb("ident", [P, P])
        iota_row = sb("iota_row", [P, P])
        tri = sb("tri", [P, P], BF16)
        ones = sb("ones", [P, P], BF16)
        gmix_sb = sb("gmix_sb", [P, KC])
        gffn_sb = sb("gffn_sb", [P, KC])
        pscale = sb("pscale", [P, H])
        gsub = sb("gsub", [P, 1])
        wr = sb("wr", [P, KC, NL])
        bias = sb("bias", [P, NL])
        lam_in = sb("lam_in", [1, 4, HD])
        lam_t = sb("lam_t", [1, 8])
        neglam = sb("neglam", [P, 1])
        hist_in = sb("hist_in", [HIST, PW])
        histT = sb("histT", [P, H, HIST])
        ustate = sb("ustate", [P, 2, H, HIST])
        inv_cnt = sb("inv_cnt", [P, 16])
        ss = sb("ss", [P, NT])
        rs = sb("rs", [P, 3, NT])
        negm = sb("negm", [P, 2, 2])
        psums = sb("psums", [P, NT, H, 2])
        coef = sb("coef", [P, 2])
        oss = sb("oss", [P, NT, H])
        osc = sb("osc", [P, 4, H])
        rev = sb("rev", [P, 4])
        tokv = sb("tokv", [P, NT, 2], BF16)
        idx = sb("idx", [P, 2], I32)
        ctl = sb("ctl", [1, MAXOV + 1], I32)
        wtok = sb("wtok", [P, 2, NT])
        yslot = sb("yslot", [P, 2, NT], I32)
        yslot_late = sb("yslot_late", [P, 2, NT], I32)
        late_f = sb("late_f", [P, 2, NT])
        yslot_f = sb("yslot_f", [P, 2, NT])
        rm = sb("rm", [P, NT, E + 3])
        e128 = sb("e128", [P, E])
        jrow = sb("jrow", [P, MAXOV])
        jbase = sb("jbase", [P, MAXOV])
        ovoff = sb("ovoff", [P, 2 * NT])
        ovw = sb("ovw", [P, 2, NT])
        slot_tok = sb("slot_tok", [P, 1])
        wmain = sb("wmain", [P, 2, NT])
        fix = sb("fix", [P, HIST])

        scratch = [0]

        def rt(*shape):
            n = int(np.prod(shape))
            a = region_k[:, scratch[0]:scratch[0] + n]
            scratch[0] += n
            assert scratch[0] <= 2048
            if len(shape) == 1:
                return a
            names = "abcd"[:len(shape)]
            return a.rearrange(f"p ({' '.join(names)}) -> p {' '.join(names)}",
                               **{c: s for c, s in zip(names, shape)})
        lg = rt(NT, NL)
        g1h = rt(NT, G)
        esel = rt(NT, EPG)
        top = rt(2, NT, EPG)
        rt4 = rt(NT, G)
        rt1 = rt(4, NT)
        gex = rt(NT, G)
        m12 = rt(2, NT, E)
        msum = rt(NT, E)
        msum_b = rt((NT + 1) * E // 2).bitcast(BF16).rearrange("p (t e) -> p t e", t=NT + 1)
        over = rt(E)
        cum = rt(2, E)
        isov = rt(NT, E)
        rt4b = rt(NT, G)
        ylin = rt(NT, E)
        etmp = rt(NT, E)
        jcmp = rt(MAXOV, E)
        jsum = rt(MAXOV)

        ps = ctx.enter_context(nc.psum_tensor("ps", [P, 8, 512], F32))

        x_loaded = sems("x_loaded", 2)
        gmix_loaded = sem("gmix_loaded")
        consts_loaded = sem("consts_loaded")
        lam_loaded = sem("lam_loaded")
        gsub_loaded = sem("gsub_loaded")
        w_in_loaded = sems("w_in_loaded", 2)
        cache_loaded = sem("cache_loaded")
        w_pool_loaded = sem("w_pool_loaded")
        w_out_loaded = sem("w_out_loaded")
        xres_loaded = sems("xres_loaded", NT)
        ring_loaded = sems("ring_loaded", RING)
        gfin_loaded = sem("gfin_loaded")
        consts_made = sem("consts_made")
        pool_step = sem("pool_step")
        dve_step = sem("dve_step")
        x_squared = sem("x_squared")
        xn_ready = sem("xn_ready")
        x_transposed = sem("x_transposed")
        hT_dve = sem("hT_dve")
        hT_act = sem("hT_act")
        v_full = sem("v_full")
        v_evac = sem("v_evac")
        v_stored = sem("v_stored")
        qk_full = sem("qk_full")
        qkp_evac = sem("qkp_evac")
        qks_evac = sem("qks_evac")
        ktok_full = sem("ktok_full")
        ktok_evac = sem("ktok_evac")
        k_stored = sem("k_stored")
        kc_full = sem("kc_full")
        kc_evac = sem("kc_evac")
        hist_full = sem("hist_full")
        hist_evac = sem("hist_evac")
        lam_dots = sem("lam_dots")
        lam_exp = sem("lam_exp")
        lam_made = sem("lam_made")
        lam_spread = sem("lam_spread")
        scores_full = sem("scores_full")
        negm_ready = sem("negm_ready")
        exp_done = sem("exp_done")
        a_ready = sem("a_ready")
        aT_full = sem("aT_full")
        aT_evac = sem("aT_evac")
        pv_done = sem("pv_done")
        o_squared = sem("o_squared")
        o_ready = sem("o_ready")
        oT_full = sem("oT_full")
        oT_evac = sem("oT_evac")
        u_full = sem("u_full")
        u_evac_act = sem("u_evac_act")
        u_evac_dve = sem("u_evac_dve")
        u_summed = sem("u_summed")
        diff_ready = sem("diff_ready")
        pool_full = sem("pool_full")
        pool_evac_act = sem("pool_evac_act")
        pool_evac_dve = sem("pool_evac_dve")
        state_full = sem("state_full")
        state_evac = sem("state_evac")
        state_stored = sem("state_stored")
        op_full = sem("op_full")
        x2_ready = sem("x2_ready")
        x2_squared = sem("x2_squared")
        h2n_ready = sem("h2n_ready")
        h2_stored = sems("h2_stored", 2)
        h2_transposed = sem("h2_transposed")
        h2T_dve = sem("h2T_dve")
        h2T_act = sem("h2T_act")
        router_done = sem("router_done")
        gate_in = sem("gate_in")
        gate_exp = sem("gate_exp")
        mask_ready = sem("mask_ready")
        rank_full = sem("rank_full")
        routed = sem("routed")
        xg_cleared = sem("xg_cleared")
        onehot_ready = sem("onehot_ready")
        idx_full = sem("idx_full")
        idx_ready = sem("idx_ready")
        xg_loaded = sems("xg_loaded", 2)
        xg_transposed = sem("xg_transposed")
        xT_dve = sem("xT_dve")
        xT_act = sem("xT_act")
        gate_full = sem("gate_full")
        up_full = sem("up_full")
        gact_ready = sem("gact_ready")
        he_ready = sem("he_ready")
        down_done = sem("down_done")
        y_evac_act = sem("y_evac_act")
        y_evac_dve = sem("y_evac_dve")
        y_stored = sem("y_stored")
        yst_free = sem("yst_free")
        ov_step = sem("ov_step")
        ov_onehot = sem("ov_onehot")
        ov_idx_full = sem("ov_idx_full")
        ov_idx_ready = sem("ov_idx_ready")
        ov_gathered = sem("ov_gathered")
        ov_w_loaded = sem("ov_w_loaded")
        ov_transposed = sem("ov_transposed")
        ov_xT_ready = sem("ov_xT_ready")
        ov_gate_full = sem("ov_gate_full")
        ov_gact_ready = sem("ov_gact_ready")
        ov_he_ready = sem("ov_he_ready")
        ov_down_done = sem("ov_down_done")
        ov_y_ready = sem("ov_y_ready")
        ov_combine_full = sem("ov_combine_full")
        ov_added = sem("ov_added")
        ov_tile_done = sem("ov_tile_done")
        ov_w_free = sem("ov_w_free")
        ov_gather_begun = sem("ov_gather_begun")
        early_gathered = sem("early_gathered")
        y_gathered = sems("y_gathered", NT)
        acc_ready = sem("acc_ready")
        acc_squared = sem("acc_squared")
        out_ready = sem("out_ready")
        out_stored = sem("out_stored")
        wslots_ready = sem("wslots_ready")

        block = ctx.enter_context(nc.Block())
        V_BLK, K_BLK, Q_BLK, U_BLK = 3, 2, 1, 0
        IN_ORDER = (V_BLK, K_BLK, Q_BLK, U_BLK)

        @block.sync
        def _(sp):
            def load_x(t):
                src = xp[t] if t < PT else xs
                sp.dma_start(xraw[0:rows(t), t % 2, :], src).then_inc(x_loaded[t % 2], 16)

            def load_w_in(j):
                b = IN_ORDER[j]
                sp.dma_start(w_in_sb[j % 2], win_v[:, :, b * PW:(b + 1) * PW]).then_inc(w_in_loaded[j % 2], 16)

            def load_expert(slot, e, signal=None):
                signal = signal or ring_loaded[slot]
                sp.dma_start(ring[slot][:, 0:WB], wg_v[DS(e, 1)].rearrange("a p n -> (a p) n")).then_inc(signal, 16)
                sp.dma_start(ring[slot][:, WB:2 * WB], wu_v[DS(e, 1)].rearrange("a p n -> (a p) n")).then_inc(signal, 16)
                sp.dma_start(wd_sb[slot], wd_v[DS(e, 1)].rearrange("a p c n -> (a p) c n")).then_inc(signal, 16)

            load_x(0)
            sp.dma_start(gmix_sb[:, :], g_mix.rearrange("a (p k) -> (a p) k", k=KC)).then_inc(gmix_loaded, 16)
            load_w_in(0)
            load_x(1)
            for t in range(2, NT):
                sp.wait_ge(xn_ready, t - 1)
                load_x(t)
            load_w_in(1)
            sp.dma_start(kc_raw, ck_v).then_inc(cache_loaded, 16)
            sp.dma_start(hist_in[:, :], state_pool.rearrange("a b s c -> (a b s) c")).then_inc(cache_loaded, 16)
            sp.dma_start(v_sa[:, 0:2, :], cv_v).then_inc(cache_loaded, 16)
            for n, v in enumerate((lam_q1, lam_q2, lam_k1, lam_k2)):
                sp.dma_start(lam_in[:, n, :], v).then_inc(lam_loaded, 16)
            sp.dma_start(gsub[:, :], g_subln.rearrange("a (v o) -> (a v) o", o=1)).then_inc(gsub_loaded, 16)
            with nc.allow_non_contiguous_dma(reason="512 scale values"):
                sp.dma_start(pscale[:, :], pool_scale.rearrange("a (g p) -> p (a g)", p=P)).then_inc(w_pool_loaded, 16)
            for j in (2, 3):
                sp.wait_ge(*((v_full, NT) if j == 2 else (qk_full, H)))
                load_w_in(j)
                if j == 2:
                    sp.wait_ge(x_transposed, NT)
                    sp.dma_start(w_pool_sb, w_pool.rearrange("a g c e -> c (a g) e")).then_inc(w_pool_loaded, 16)
            sp.dma_start(w_out_sb, wout_v).then_inc(w_out_loaded, 16)
            sp.dma_start(gffn_sb[:, :], g_ffn.rearrange("a (p k) -> (a p) k", k=KC)).then_inc(consts_loaded, 16)
            sp.dma_start(wr[:, :, 0:G], w_group.rearrange("a (p k) g -> (a p) k g", k=KC)).then_inc(consts_loaded, 16)
            sp.dma_start(wr[:, :, G:NL], w_erouter.rearrange("a (p k) g -> (a p) k g", k=KC)).then_inc(consts_loaded, 16)
            sp.dma_start(bias[:, 0:G], b_group.to_broadcast([P, G])).then_inc(consts_loaded, 16)
            sp.dma_start(bias[:, G:NL], b_erouter.to_broadcast([P, E])).then_inc(consts_loaded, 16)
            sp.wait_ge(k_stored, 16 * NT)
            load_expert(0, 0)
            sp.wait_ge(scores_full, UNITS)
            for t in range(NT):
                src = xp[t] if t < PT else xs
                sp.dma_start(x2[0:rows(t), t, :], src).then_inc(xres_loaded[t], 16)
            sp.wait_ge(u_full, H)
            load_expert(1, 1)
            load_expert(2, 2)
            sp.wait_ge(op_full, NT)
            load_expert(3, 3)
            sp.wait_ge(routed, 1)
            sp.wait_ge(wslots_ready, 1)
            sp.dma_start(gfin, g_final.rearrange("(a d) -> a d", a=1).to_broadcast([P, D])).then_inc(gfin_loaded, 16)

            sp.sem_inc(yst_free, 2)

            def store_rows(i, b, row):
                sp.wait_ge(y_evac_act, i + 2)
                sp.wait_ge(y_evac_dve, i + 2)
                sp.dma_start(y_dram[row, :], yst[:, b, :]).then_inc(y_stored, 16)
                sp.wait_ge(y_stored, i * 16 + 16)
                sp.sem_inc(yst_free, 1)

            with sp.Fori(0, E // RING - 1) as it:
                for u in range(RING):
                    i = it * RING + u
                    sp.wait_ge(down_done, i + 1)
                    load_expert(u, i + RING)
                    store_rows(i, u % 2, DS(i * P, P))
            for i in range(E - RING, E):
                store_rows(i, i % 2, slice(i * P, (i + 1) * P))

            n_ov = sp.value_load(ctl[0:1, MAXOV:MAXOV + 1], min_val=0, max_val=MAXOV)
            with sp.Fori(0, MAXOV) as j:
                with sp.If(j < n_ov):
                    e = sp.value_load(ctl[0:1, DS(j, 1)], min_val=0, max_val=E - 1)
                    load_expert(RING - 1, e, ov_w_loaded)
                    sp.wait_ge(ov_down_done, j + 1)
                    sp.sem_inc(ov_w_free, 1)
                sp.nop()
            for t in range(NT):
                sp.wait_ge(out_ready, t + 1)
                sp.dma_start(yp_v[t] if t < PT else ys_v, y2[t][0:rows(t), :]).then_inc(out_stored, 16)
            sp.wait_ge(out_stored, 16 * NT)

        @block.gpsimd
        def _(pool):
            made = [0]

            def step(ins):
                made[0] += 1
                ins.then_inc(pool_step, 1)
                pool.wait_ge(pool_step, made[0])

            step(pool.memset(ident[:, :], 0.0))
            pool.affine_select(out=ident[:, :], in_=ident[:, :], compare_op=ALU.not_equal, fill=1.0, base=0,
                               pattern=[[-1, P]], channel_multiplier=1).then_inc(consts_made, 1)
            step(pool.memset(ones[:, :], 1.0))
            step(pool.affine_select(out=tri[:, :], in_=ones[:, :], compare_op=ALU.is_gt, fill=0.0, base=0,
                                    pattern=[[1, P]], channel_multiplier=-1))
            step(pool.iota(iota_row[:, :], pattern=[[1, P]], base=0, channel_multiplier=0,
                           allow_small_or_imprecise_dtypes=True))
            step(pool.iota(inv_cnt[:, :], pattern=[[1, 16]], base=1, channel_multiplier=0,
                           allow_small_or_imprecise_dtypes=True))
            step(pool.iota(rev[:, :], pattern=[[-1, 4]], base=4, channel_multiplier=0,
                           allow_small_or_imprecise_dtypes=True))
            step(pool.iota(e128[:, :], pattern=[[P, E]], base=0, channel_multiplier=0,
                           allow_small_or_imprecise_dtypes=True))
            step(pool.iota(jrow[:, :], pattern=[[1, MAXOV]], base=0, channel_multiplier=0,
                           allow_small_or_imprecise_dtypes=True))
            step(pool.iota(jbase[:, :], pattern=[[P, MAXOV]], base=E * P, channel_multiplier=0,
                           allow_small_or_imprecise_dtypes=True))
            step(pool.iota(tokv[:, :, 0], pattern=[[P, NT]], base=-NOWHERE, channel_multiplier=0,
                           allow_small_or_imprecise_dtypes=True))
            pool.iota(tokv[:, :, 1], pattern=[[0, NT]], base=0, channel_multiplier=1,
                      allow_small_or_imprecise_dtypes=True).then_inc(consts_made, 1)

            for t in range(NT):
                pool.wait_ge(v_evac, t + 1)
                dst = vp_v[t] if t < PT else vs_v
                src = v_pr[:, t, :] if t < PT else v_sa[0:N_SAMPLE, 2, :]
                pool.dma_start(dst, src).then_inc(v_stored, 16)
            for t in range(NT):
                pool.wait_ge(ktok_evac, t + 1)
                pool.dma_start(kp_v[t] if t < PT else ks_v, k_st[0:rows(t), t, :]).then_inc(k_stored, 16)

            pool.wait_ge(lam_made, 1)
            pool.partition_broadcast(neglam[:, :], lam_t[0:1, 6:7]).then_inc(lam_spread, 1)

            for g in range(H):
                pool.wait_ge(u_evac_act, 2 * g + 2)
                pool.wait_ge(u_evac_dve, g + 1)
                if g >= 1:
                    pool.wait_ge(diff_ready, g)
                src, shift = uext[:, g % 2, :], 1
                for lev in range(g + 1):
                    dst = usum[:, lev % 2, :]
                    lo = 2 * shift - 1
                    ins = pool.tensor_tensor(dst[:, lo:EXT], src[:, lo:EXT], src[:, lo - shift:EXT - shift], ALU.add)
                    step(ins)
                    src, shift = dst, 2 * shift
                pool.tensor_copy(ustate[:, 0, g, :], uext[:, g % 2, N_PROMPT:N_PROMPT + HIST])
                pool.tensor_copy(ustate[:, 1, g, :], uext[:, g % 2, EXT - HIST:EXT]).then_inc(u_summed, 1)
            pool.wait_ge(state_evac, 1)
            pool.dma_start(pool_prompt.rearrange("a b s c -> (a b s) c"), state_out[:, 0, :]).then_inc(state_stored, 16)
            pool.dma_start(pool_sample.rearrange("a b s c -> (a b s) c"), state_out[:, 1, :]).then_inc(state_stored, 16)

            for t in range(NT):
                pool.wait_ge(h2n_ready, t + 1)
                pool.dma_start(h2_dram[t * P:t * P + rows(t), :], h2n[0:rows(t), t % 2, :]).then_inc(h2_stored[t % 2], 16)
            pool.wait_ge(pool_full, 1)
            pool.memset(xg[:, :, :], 0.0).then_inc(xg_cleared, 1)
            pool.wait_ge(xg_cleared, 1)
            pool.wait_ge(h2_stored[0], 48)
            pool.wait_ge(h2_stored[1], 32)
            for i in range(E + 1):
                pool.wait_ge(idx_ready, i + 1)
                if i >= 2:
                    pool.wait_ge(xg_transposed, i - 1)
                pool.indirect_dma_start(
                    out=xg[:, i % 2, :], out_offset=None, in_=h2_dram,
                    in_offset=bass.IndirectOffsetOnAxis(ap=idx[:, i % 2:i % 2 + 1], axis=0),
                    bounds_check=T - 1, oob_is_err=False).then_inc(xg_loaded[i % 2], 16)
            def gather_back(t, slots, last_row, signal):
                n = rows(t)
                for c, dst in ((0, y1), (1, y2)):
                    pool.indirect_dma_start(
                        out=dst[t][0:n, :], out_offset=None, in_=y_dram[0:last_row + 1, :],
                        in_offset=bass.IndirectOffsetOnAxis(ap=slots[0:n, c, t:t + 1], axis=0),
                        bounds_check=last_row, oob_is_err=False).then_inc(signal, 16)

            pool.wait_ge(wslots_ready, 1)
            pool.wait_ge(y_stored, 16 * EARLY)
            for t in range(NT):
                gather_back(t, yslot, EARLY * P - 1, early_gathered)
            pool.wait_ge(early_gathered, 32 * NT)
            pool.wait_ge(y_stored, 16 * E)
            for t in range(NT):
                gather_back(t, yslot_late, NSLOT - 1, y_gathered[t])
            pool.wait_ge(xg_transposed, E + 1)
            n_ov = pool.value_load(ctl[0:1, MAXOV:MAXOV + 1], min_val=0, max_val=MAXOV)
            with pool.Fori(0, MAXOV) as j:
                with pool.If(j < n_ov):
                    pool.wait_ge(ov_idx_ready, j + 1)
                    pool.sem_inc(ov_gather_begun, 1)
                    pool.indirect_dma_start(
                        out=xg[:, 0, :], out_offset=None, in_=h2_dram,
                        in_offset=bass.IndirectOffsetOnAxis(ap=idx[:, 0:1], axis=0),
                        bounds_check=T - 1, oob_is_err=False).then_inc(ov_gathered, 16)
                pool.nop()
            pool.wait_ge(v_stored, 16 * NT)
            pool.wait_ge(k_stored, 16 * NT)
            pool.wait_ge(state_stored, 32)

        @block.tensor
        def _(pe):
            def transpose_x(t):
                n = rows(t)
                pe.wait_ge(xn_ready, t + 1)
                if t == 0:
                    pe.wait_ge(consts_made, 1)
                if t >= 2:
                    pe.wait_ge(hT_dve, t - 1)
                    pe.wait_ge(hT_act, t - 1)
                src = xn[0:n, t % 2, :].rearrange("p (q k) -> p k q", k=KC)
                for k in range(KC):
                    o = ps[:, 2 * (t % 2) + k // 4, (k % 4) * P:(k % 4) * P + n]
                    ins = pe.transpose(o, src[:, k, :], ident[0:n, 0:n])
                ins.then_inc(x_transposed, 1)

            def project_v(t):
                n = rows(t)
                pe.wait_ge(hT_dve, t + 1)
                pe.wait_ge(hT_act, t + 1)
                if t == 0:
                    pe.wait_ge(w_in_loaded[0], 16)
                if t >= 2:
                    pe.wait_ge(v_evac, t - 1)
                for k in range(KC):
                    ins = pe.matmul(ps[0:n, 4 + t % 2, :], hT[:, k, t * P:t * P + n], w_in_sb[0][:, k, :],
                                    start=(k == 0), stop=(k == KC - 1))
                ins.then_inc(v_full, 1)

            def project_head(j):
                c = j % H
                w = w_in_sb[1 if j < H else 0]
                if j == 0:
                    pe.wait_ge(w_in_loaded[1], 16)
                    pe.wait_ge(v_evac, NT)
                if j == H:
                    pe.wait_ge(w_in_loaded[0], 32)
                if j >= 2:
                    pe.wait_ge(qkp_evac, j - 1)
                    pe.wait_ge(qks_evac, j - 1)
                for k in range(KC):
                    lhs = w[:, k, c * P:(c + 1) * P]
                    pe.matmul(ps[:, 4 + j % 2, :], lhs, hT[:, k, 0:N_PROMPT], start=(k == 0), stop=(k == KC - 1))
                    ins = pe.matmul(ps[:, 6 + j % 2, 0:N_SAMPLE], lhs, hT[:, k, N_PROMPT:T],
                                    start=(k == 0), stop=(k == KC - 1))
                ins.then_inc(qk_full, 1)

            transpose_x(0)
            transpose_x(1)
            for t in range(NT):
                project_v(t)
                if t + 2 < NT:
                    transpose_x(t + 2)
            for j in range(H):
                project_head(j)
            project_head(H)
            pe.wait_ge(qkp_evac, H)
            pe.wait_ge(qks_evac, H)
            pe.wait_ge(hT_dve, NT)
            pe.wait_ge(hT_act, NT)
            for t in range(NT):
                n = rows(t)
                if t == 4:
                    pe.wait_ge(ktok_evac, 1)
                for h in range(H):
                    ins = pe.transpose(ps[0:n, t % 4, h * P:(h + 1) * P], kT[:, h, t * P:t * P + n], ident[:, :])
                ins.then_inc(ktok_full, 1)
            pe.wait_ge(cache_loaded, 48)
            for c in range(2):
                pe.wait_ge(ktok_evac, 2 + c)
                for h in range(2):
                    for t in range(2):
                        ins = pe.transpose(ps[:, 1 + c, (2 * h + t) * P:(2 * h + t + 1) * P],
                                           kc_raw[:, t, (2 * c + h) * P:(2 * c + h + 1) * P], ident[:, :])
                ins.then_inc(kc_full, 1)
            pe.wait_ge(ktok_evac, 4)
            for g in range(H):
                ins = pe.transpose(ps[:, 3, g * HIST:(g + 1) * HIST], hist_in[:, g * P:(g + 1) * P],
                                   ident[0:HIST, 0:HIST])
            ins.then_inc(hist_full, 1)
            for j in range(H + 1, 2 * H):
                project_head(j)

            pe.wait_ge(qkp_evac, 2 * H)
            pe.wait_ge(qks_evac, 2 * H)
            pe.wait_ge(kc_evac, 2)
            pe.wait_ge(ktok_evac, NT)
            pe.wait_ge(hist_evac, 1)

            def scores(n):
                t, h = divmod(n, H)
                b = 2 * (n % 2)
                if n >= 2:
                    pe.wait_ge(exp_done, n - 1)
                for c in range(2):
                    r = slice(c * HD, (c + 1) * HD)
                    q = qT[r, h, t * P:t * P + rows(t)]
                    if t < PT:
                        ins = pe.matmul(ps[:, b + c, 0:(t + 1) * P], q, kT[r, h, 0:(t + 1) * P], start=True, stop=True)
                    else:
                        pe.matmul(ps[0:N_SAMPLE, b + c, 0:PAST], q, kcT[r, h, :], start=True, stop=True)
                        ins = pe.matmul(ps[0:N_SAMPLE, b + c, PAST:PAST + N_SAMPLE], q, kT[r, h, N_PROMPT:T],
                                        start=True, stop=True)
                ins.then_inc(scores_full, 1)

            def key_tiles(t):
                return [(k, P) for k in range(t + 1)] if t < PT else [(0, P), (1, P), (2, N_SAMPLE)]

            def transpose_a(n):
                t, h = divmod(n, H)
                m = rows(t)
                pe.wait_ge(a_ready, n + 1)
                if n >= 1:
                    pe.wait_ge(aT_evac, n)
                for k, keys in key_tiles(t):
                    ins = pe.transpose(ps[0:keys, 4, k * P:k * P + m], prob[0:m, n % 2, 0, k * P:k * P + keys],
                                       ident[0:m, 0:m])
                ins.then_inc(aT_full, 1)

            def weighted_values(n):
                t, h = divmod(n, H)
                m = rows(t)
                pe.wait_ge(aT_evac, n + 1)
                if n == UNITS - H:
                    pe.wait_ge(cache_loaded, 48)
                if h == 0 and t >= 2:
                    pe.wait_ge(oT_evac, t - 1)
                tiles = key_tiles(t)
                for k, keys in tiles:
                    v = (v_pr if t < PT else v_sa)[0:keys, k, h * VD:(h + 1) * VD]
                    ins = pe.matmul(ps[0:m, 5 + 2 * (t % 2), h * VD:(h + 1) * VD], aT[0:keys, n % 2, k * P:k * P + m], v,
                                    start=(k == 0), stop=(k == len(tiles) - 1))
                ins.then_inc(pv_done, 1)

            def transpose_o(t):
                m = rows(t)
                pe.wait_ge(o_ready, t + 1)
                for h in range(H):
                    ins = pe.transpose(ps[:, 5 + 2 * (t % 2), h * P:h * P + m], otok[0:m, h * VD:(h + 1) * VD], ident[0:m, 0:m])
                ins.then_inc(oT_full, 1)

            def project_u(n, part):
                if n >= 4 * H:
                    return
                blk = n // 2
                g, half = divmod(blk, 2)
                for k in range(4 * (n % 2) + 2 * part, 4 * (n % 2) + 2 * part + 2):
                    if n == 0 and k == 0:
                        pe.wait_ge(w_in_loaded[1], 32)
                    if k == 0 and blk >= 1:
                        pe.wait_ge(u_evac_act, blk)
                    ins = pe.matmul(ps[:, 6, 0:T // 2], w_in_sb[1][:, k, g * P:(g + 1) * P],
                                    hT[:, k, half * (T // 2):(half + 1) * (T // 2)], start=(k == 0), stop=(k == KC - 1))
                    if k == KC - 1:
                        ins.then_inc(u_full, 1)

            scores(0)
            scores(1)
            for n in range(UNITS):
                if n + 2 < UNITS:
                    scores(n + 2)
                project_u(n, 0)
                if n >= 1:
                    weighted_values(n - 1)
                if n >= 6 and (n - 6) % H == 0:
                    transpose_o((n - 6) // H)
                transpose_a(n)
                project_u(n, 1)
            weighted_values(UNITS - 1)

            pe.wait_ge(exp_done, UNITS)
            pe.wait_ge(aT_evac, UNITS)
            pe.wait_ge(w_pool_loaded, 32)
            for g in range(H):
                pe.wait_ge(diff_ready, g + 1)
                pe.matmul(ps[:, g, :], w_pool_sb[:, g, :], mixT[:, g, 0:N_PROMPT], start=True, stop=True)
                ins = pe.matmul(ps[:, 4, g * N_SAMPLE:(g + 1) * N_SAMPLE], w_pool_sb[:, g, :],
                                mixT[:, g, N_PROMPT:T], start=True, stop=True)
            ins.then_inc(pool_full, 1)
            pe.wait_ge(u_evac_act, 2 * H)
            pe.wait_ge(oT_evac, NT - 1)
            for b in range(2):
                for g in range(H):
                    ins = pe.transpose(ps[0:HIST, 6 + b, g * P:(g + 1) * P], ustate[:, b, g, :], ident[:, :])
            ins.then_inc(state_full, 1)
            transpose_o(NT - 1)

            def project_out(t, half):
                n = rows(t)
                if t == 0 and half == 0:
                    pe.wait_ge(w_out_loaded, 16)
                    pe.wait_ge(oT_evac, NT)
                    pe.wait_ge(pool_evac_act, 1)
                    pe.wait_ge(pool_evac_dve, 1)
                if t >= 2 and half == 0:
                    pe.wait_ge(x2_ready, t - 1)
                for f in range(KC):
                    ins = pe.matmul(ps[0:n, 2 * (t % 2) + half, :], mixT[:, f, t * P:t * P + n],
                                    w_out_sb[:, f, half * 512:(half + 1) * 512],
                                    start=(f == 0), stop=(f == KC - 1))
                if half == 1:
                    ins.then_inc(op_full, 1)

            def transpose_h2(t):
                n = rows(t)
                pe.wait_ge(h2n_ready, t + 1)
                if t >= 1:
                    pe.wait_ge(h2T_dve, t)
                    pe.wait_ge(h2T_act, t)
                src = h2n[0:n, t % 2, :].rearrange("p (q k) -> p k q", k=KC)
                for k in range(KC):
                    ins = pe.transpose(ps[:, 4 + k // 4, (k % 4) * P:(k % 4) * P + n], src[:, k, :], ident[0:n, 0:n])
                ins.then_inc(h2_transposed, 1)

            def router_logits(t):
                pe.wait_ge(h2T_dve, t + 1)
                pe.wait_ge(h2T_act, t + 1)
                if t == 0:
                    pe.wait_ge(consts_loaded, 80)
                    pe.wait_ge(state_evac, 1)
                for k in range(KC):
                    ins = pe.matmul(ps[:, 6, t * NL:(t + 1) * NL], h2T[:, k, :], wr[:, k, :],
                                    start=(k == 0), stop=(k == KC - 1))
                ins.then_inc(router_done, 1)

            for t in range(NT):
                project_out(t, 0)
                if t >= 2:
                    router_logits(t - 2)
                project_out(t, 1)
                if t >= 1:
                    transpose_h2(t - 1)
            router_logits(NT - 2)
            transpose_h2(NT - 1)
            router_logits(NT - 1)

            pe.wait_ge(mask_ready, 1)
            pe.matmul(ps[:, 5, 0:(NT + 1) * E], tri[:, :], msum_b.rearrange("p t e -> p (t e)"), start=True, stop=False)
            for t in range(NT):
                ins = pe.matmul(ps[:, 5, (t + 1) * E:(NT + 1) * E].rearrange("p (t e) -> p t e", e=E), ones[:, :],
                                msum_b[:, t, :].unsqueeze(1).to_broadcast([P, NT - t, E]), start=False, stop=(t == NT - 1))
            ins.then_inc(rank_full, 1)

            def slot_tokens(b, signal):
                for t in range(NT):
                    ins = pe.matmul(ps[:, 6 + b, 0:2], onehot_all[:, b, t, :], tokv[:, t, :], start=(t == 0), stop=(t == NT - 1))
                ins.then_inc(signal, 1)

            def transpose_rows(b, signal):
                src = xg[:, b, :].rearrange("p (q k) -> p k q", k=KC)
                for k in range(KC):
                    ins = pe.transpose(ps[:, k // 4, (k % 4) * P:(k % 4 + 1) * P], src[:, k, :], ident[:, :])
                ins.then_inc(signal, 1)

            def gate_up(slot, b, gate_signal, up_signal):
                for w, bank, signal in ((wg_sb[slot], 2, gate_signal), (wu_sb[slot], 3, up_signal)):
                    for c in range(FC):
                        for k in range(KC):
                            ins = pe.matmul(ps[:, bank, c * P:(c + 1) * P], w[:, k, c * P:(c + 1) * P],
                                            xT[:, b, k, :], start=(k == 0), stop=(k == KC - 1))
                    if signal is not None:
                        ins.then_inc(signal, 1)

            def down(slot, b, signal):
                for half in range(2):
                    for c in range(FC):
                        ins = pe.matmul(ps[:, 4 + half, :], heT[:, b, c, :], wd_sb[slot][:, c, half * 512:(half + 1) * 512],
                                        start=(c == 0), stop=(c == FC - 1))
                ins.then_inc(signal, 1)

            for i in range(2):
                pe.wait_ge(onehot_ready, i + 1)
                slot_tokens(i, idx_full)
            pe.wait_ge(x2_ready, NT)
            pe.wait_ge(xg_loaded[0], 16)
            transpose_rows(0, xg_transposed)
            with pe.Fori(0, E // RING) as it:
                for u in range(RING):
                    i = it * RING + u
                    b = u % 2
                    pe.wait_ge(onehot_ready, i + 3)
                    pe.wait_ge(idx_ready, i + 1)
                    slot_tokens(b, idx_full)
                    pe.wait_ge(xT_dve, i + 1)
                    pe.wait_ge(xT_act, i + 1)
                    pe.wait_ge(ring_loaded[u], it * 48 + 48)
                    gate_up(u, b, gate_full, up_full)
                    pe.wait_ge(xg_loaded[1 - b], it * (8 * RING) + 16 * ((u + 1) // 2 + 1))
                    transpose_rows(1 - b, xg_transposed)
                    pe.wait_ge(he_ready, i + 1)
                    pe.wait_ge(y_evac_act, i + 1)
                    pe.wait_ge(y_evac_dve, i + 1)
                    down(u, b, down_done)

            n_ov = pe.value_load(ctl[0:1, MAXOV:MAXOV + 1], min_val=0, max_val=MAXOV)
            pe.wait_ge(idx_ready, E + 2)
            pe.wait_ge(xT_dve, E + 1)
            pe.wait_ge(xT_act, E + 1)
            pe.wait_ge(y_evac_act, E + 1)
            pe.wait_ge(y_evac_dve, E + 1)
            with pe.Fori(0, MAXOV) as j:
                with pe.If(j < n_ov):
                    pe.wait_ge(ov_onehot, j + 1)
                    for c in range(2):
                        for t in range(NT):
                            ins = pe.matmul(ps[:, 6, 0:2], onehot_all[:, c, t, :], tokv[:, t, :],
                                            start=(c == 0 and t == 0), stop=(c == 1 and t == NT - 1))
                    ins.then_inc(ov_idx_full, 1)
                    pe.wait_ge(ov_gathered, j * 16 + 16)
                    transpose_rows(0, ov_transposed)
                    pe.wait_ge(ov_xT_ready, j + 1)
                    pe.wait_ge(ov_w_loaded, j * 48 + 48)
                    gate_up(RING - 1, 0, None, ov_gate_full)
                    pe.wait_ge(ov_he_ready, j + 1)
                    down(RING - 1, 0, ov_down_done)
                    pe.wait_ge(ov_y_ready, j + 1)
                    for t in range(NT):
                        if t >= 2:
                            pe.wait_ge(ov_added, j * NT + (t - 1))
                        for half in range(2):
                            ins = pe.matmul(ps[0:rows(t), 4 - 2 * (t % 2) + half, :], slot_to_token[:, t, 0:rows(t)],
                                            yst[:, 0, half * 512:(half + 1) * 512], start=True, stop=True)
                        ins.then_inc(ov_combine_full, 1)
                pe.nop()

        @block.scalar
        def _(act):
            def transposed_times_gain(out, banks_col, gain, n, signal):
                for k in range(4):
                    ins = act.activation(out[:, 4 + k, 0:n], banks_col[:, k * P:k * P + n], ACT.Copy,
                                         scale=gain[:, 4 + k:5 + k])
                ins.then_inc(signal, 1)

            def hT_evac(t):
                n = rows(t)
                act.wait_ge(x_transposed, t + 1)
                if t == 0:
                    act.wait_ge(gmix_loaded, 16)
                transposed_times_gain(hT[:, :, t * P:t * P + n], ps[:, 2 * (t % 2) + 1, :], gmix_sb, n, hT_act)

            def v_out(t):
                n = rows(t)
                act.wait_ge(v_full, t + 1)
                dst = v_pr[:, t, :] if t < PT else v_sa[0:N_SAMPLE, 2, :]
                act.copy(dst, ps[0:n, 4 + t % 2, :]).then_inc(v_evac, 1)

            for t in range(NT):
                n = rows(t)
                act.wait_ge(x_loaded[t % 2], 16 * (t // 2 + 1))
                if t >= 2:
                    act.wait_ge(x_transposed, t - 1)
                act.activation(xn[0:n, t % 2, :], xraw[0:n, t % 2, :], ACT.Square,
                               accum_out=ss[0:n, t:t + 1]).then_inc(x_squared, 1)
                if t >= 1:
                    hT_evac(t - 1)
                if t >= 2:
                    v_out(t - 2)
            hT_evac(NT - 1)
            v_out(NT - 2)
            v_out(NT - 1)

            def head_out(j):
                act.wait_ge(qk_full, j + 1)
                if j < H:
                    act.copy(kT[:, j, 0:N_PROMPT], ps[:, 4 + j % 2, :]).then_inc(qkp_evac, 1)
                else:
                    act.activation(qT[:, j - H, 0:N_PROMPT], ps[:, 4 + j % 2, :], ACT.Copy, scale=-SCALE).then_inc(qkp_evac, 1)

            for j in range(H + 1):
                head_out(j)
            act.wait_ge(lam_dots, 1)
            act.activation(lam_t[:, 2:4], lam_t[:, 0:2], ACT.Exp).then_inc(lam_exp, 1)
            for c in range(2):
                act.wait_ge(kc_full, c + 1)
                act.copy(kcT[:, 2 * c:2 * c + 2, :], ps[:, 1 + c, :].rearrange("p (h t) -> p h t", h=2)).then_inc(kc_evac, 1)
            for j in range(H + 1, 2 * H):
                head_out(j)

            def exps(n):
                t, h = divmod(n, H)
                m, w = rows(t), (t + 1) * P if t < PT else PAST + N_SAMPLE
                act.wait_ge(negm_ready, n + 1)
                if n >= 2:
                    act.wait_ge(aT_full, n - 1)
                for c in range(2):
                    ins = act.activation(prob[0:m, n % 2, c, 0:w], ps[0:m, 2 * (n % 2) + c, 0:w], ACT.Exp,
                                         bias=negm[0:m, n % 2, c:c + 1], scale=-1.0,
                                         accum_out=psums[0:m, t, h, c:c + 1])
                ins.then_inc(exp_done, 1)

            def aT_out(n):
                t, h = divmod(n, H)
                act.wait_ge(aT_full, n + 1)
                if n >= 2:
                    act.wait_ge(pv_done, n - 1)
                if t < PT:
                    w = (t + 1) * P
                    act.copy(aT[:, n % 2, 0:w], ps[:, 4, 0:w]).then_inc(aT_evac, 1)
                else:
                    two = lambda a: a.rearrange("p (k q) -> p k q", k=2)[:, :, 0:N_SAMPLE]
                    act.copy(two(aT[:, n % 2, 0:2 * P]), two(ps[:, 4, 0:2 * P]))
                    act.copy(aT[0:N_SAMPLE, n % 2, 2 * P:2 * P + N_SAMPLE],
                             ps[0:N_SAMPLE, 4, 2 * P:2 * P + N_SAMPLE]).then_inc(aT_evac, 1)

            def o_squares(t):
                m = rows(t)
                act.wait_ge(pv_done, H * (t + 1))
                if t >= 1:
                    act.wait_ge(oT_full, t)
                for h in range(H):
                    ins = act.activation(otok[0:m, h * VD:(h + 1) * VD], ps[0:m, 5 + 2 * (t % 2), h * VD:(h + 1) * VD], ACT.Square,
                                         accum_out=oss[0:m, t, h:h + 1])
                ins.then_inc(o_squared, 1)

            def u_out(blk):
                g, half = divmod(blk, 2)
                u = uext[:, g % 2, :]
                act.wait_ge(u_full, blk + 1)
                if half == 0:
                    if g >= 2:
                        act.wait_ge(u_summed, g - 1)
                        act.wait_ge(diff_ready, g - 1)
                    elif g == 0:
                        act.wait_ge(xn_ready, NT)
                    act.copy(u[:, HIST:HIST + T // 2], ps[:, 6, 0:T // 2]).then_inc(u_evac_act, 1)
                else:
                    n = N_PROMPT - T // 2
                    act.copy(u[:, HIST + T // 2:HIST + N_PROMPT], ps[:, 6, 0:n])
                    act.copy(u[:, S0:EXT], ps[:, 6, n:T // 2]).then_inc(u_evac_act, 1)

            exps(0)
            for n in range(UNITS):
                if n % 2 == 0 and 2 <= n <= 4 * H:
                    u_out(n // 2 - 1)
                if n + 1 < UNITS:
                    exps(n + 1)
                if n % H == 1 and n >= H:
                    o_squares(n // H - 1)
                aT_out(n)
            o_squares(NT - 1)
            act.wait_ge(pool_full, 1)
            for g in range(H):
                ins = act.activation(mixT[:, g, 0:N_PROMPT], ps[:, g, :], ACT.Copy, scale=pscale[:, g:g + 1])
            ins.then_inc(pool_evac_act, 1)

            def h2_square(t):
                n = rows(t)
                act.wait_ge(x2_ready, t + 1)
                if t >= 2:
                    act.wait_ge(h2_transposed, t - 1)
                    act.wait_ge(h2_stored[t % 2], 16 * (t // 2))
                act.activation(h2n[0:n, t % 2, :], x2[0:n, t, :], ACT.Square,
                               accum_out=ss[0:n, t:t + 1]).then_inc(x2_squared, 1)

            def h2T_evac(t):
                act.wait_ge(h2_transposed, t + 1)
                if t >= 1:
                    act.wait_ge(router_done, t)
                transposed_times_gain(h2T, ps[:, 5, :], gffn_sb, rows(t), h2T_act)

            act.wait_ge(consts_loaded, 80)
            act.wait_ge(pv_done, UNITS)
            act.wait_ge(v_stored, 16 * NT)
            for t in range(NT):
                h2_square(t)
                if t >= 1:
                    h2T_evac(t - 1)
            h2T_evac(NT - 1)

            act.wait_ge(gate_in, 1)
            act.activation(gex, gex, ACT.Exp).then_inc(gate_exp, 1)
            act.wait_ge(gate_in, 2)
            act.activation(rt1[:, 3, :], rt1[:, 3, :], ACT.Exp).then_inc(gate_exp, 1)

            def rows_out(b, k):
                return act.activation(xT[:, b, k, :], ps[:, 1, (k - 4) * P:(k - 3) * P], ACT.Copy, scale=gffn_sb[:, k:k + 1])

            act.wait_ge(h2T_dve, NT)
            act.sem_inc(y_evac_act, 1)
            act.wait_ge(xg_transposed, 1)
            for k in range(4, KC):
                ins = rows_out(0, k)
            ins.then_inc(xT_act, 1)
            act.wait_ge(routed, 1)
            with act.Fori(0, E // RING) as it:
                for u in range(RING):
                    i = it * RING + u
                    b = u % 2
                    act.wait_ge(gate_full, i + 1)
                    act.activation(gact[:, b], ps[:, 2, 0:FE].rearrange("p (c s) -> p c s", c=FC),
                                   ACT.Silu).then_inc(gact_ready, 1)
                    act.wait_ge(xg_transposed, i + 2)
                    for k in range(4, KC):
                        ins = rows_out(1 - b, k)
                    ins.then_inc(xT_act, 1)
                    act.wait_ge(down_done, i + 1)
                    act.wait_ge(yst_free, i + 1)
                    act.copy(yst[:, b, 0:512], ps[:, 4, :]).then_inc(y_evac_act, 1)
            n_ov = act.value_load(ctl[0:1, MAXOV:MAXOV + 1], min_val=0, max_val=MAXOV)
            with act.Fori(0, MAXOV) as j:
                with act.If(j < n_ov):
                    act.wait_ge(ov_gate_full, j + 1)
                    act.activation(gact[:, 0], ps[:, 2, 0:FE].rearrange("p (c s) -> p c s", c=FC),
                                   ACT.Silu).then_inc(ov_gact_ready, 1)
                act.nop()
            for t in range(NT):
                n = rows(t)
                act.wait_ge(acc_ready, t + 1)
                act.activation(y2[t][0:n, :], y1[t][0:n, :], ACT.Square, accum_out=ss[0:n, t:t + 1]).then_inc(acc_squared, 1)

        @block.vector
        def _(dve):
            steps = [0]

            def step(ins):
                steps[0] += 1
                ins.then_inc(dve_step, 1)
                dve.wait_ge(dve_step, steps[0])

            def wide(a, shape):
                return a.unsqueeze(len(a.shape)).to_broadcast(shape)

            def inverse_root(y, m, tmp, half):
                dve.tensor_scalar(half, m, -0.5, None, ALU.mult)
                step(dve.tensor_scalar(tmp.bitcast(I32), m.bitcast(I32), 1, None, ALU.arith_shift_right))
                step(dve.tensor_scalar(y.bitcast(I32), tmp.bitcast(I32), -1.0, float(0x5F3759DF), ALU.mult, ALU.add))
                for _ in range(3):
                    if half.shape[-1] == 1:
                        step(dve.scalar_tensor_tensor(tmp, y, half, y, ALU.mult, ALU.mult))
                    else:
                        step(dve.tensor_tensor(tmp, y, y, ALU.mult))
                        step(dve.tensor_tensor(tmp, tmp, half, ALU.mult))
                    step(dve.scalar_tensor_tensor(y, tmp, 1.5, y, ALU.add, ALU.mult))

            def row_scale(t):
                n = rows(t)
                m, y, tmp, half = (rs[0:n, 1, t:t + 1], rs[0:n, 0, t:t + 1], rs[0:n, 2, t:t + 1], ovoff[0:n, t:t + 1])
                step(dve.tensor_scalar(m, ss[0:n, t:t + 1], 1.0 / D, EPS, ALU.mult, ALU.add))
                inverse_root(y, m, tmp, half)
                return y

            def hT_evac(t):
                n = rows(t)
                dve.wait_ge(x_transposed, t + 1)
                if t == 0:
                    dve.wait_ge(gmix_loaded, 16)
                dve.tensor_tensor(hT[:, 0:4, t * P:t * P + n],
                                  ps[:, 2 * (t % 2), :].rearrange("p (k t) -> p k t", k=4)[:, :, 0:n],
                                  wide(gmix_sb[:, 0:4], [P, 4, n]), ALU.mult).then_inc(hT_dve, 1)

            for t in range(NT):
                n = rows(t)
                dve.wait_ge(x_squared, t + 1)
                y = row_scale(t)
                dve.tensor_scalar(xn[0:n, t % 2, :], xraw[0:n, t % 2, :], y, None, ALU.mult).then_inc(xn_ready, 1)
                if t >= 1:
                    hT_evac(t - 1)
            hT_evac(NT - 1)

            dve.wait_ge(lam_loaded, 64)
            step(dve.tensor_tensor(lam_in[:, 0:2, :], lam_in[:, 0:2, :], lam_in[:, 2:4, :], ALU.mult))
            dve.tensor_reduce(lam_t[:, 0:2], lam_in[:, 0:2, :], X, ALU.add).then_inc(lam_dots, 1)
            dve.wait_ge(consts_made, 2)
            step(dve.reciprocal(inv_cnt[:, :], inv_cnt[:, :]))
            dve.wait_ge(gsub_loaded, 16)
            step(dve.tensor_scalar(gsub[:, :], gsub[:, :], 1.0 - LAMBDA_INIT, None, ALU.mult))

            def head_out(j):
                dve.wait_ge(qk_full, j + 1)
                dst = (kT if j < H else qT)[:, j % H, N_PROMPT:T]
                dve.tensor_scalar(dst, ps[:, 6 + j % 2, 0:N_SAMPLE], 1.0 if j < H else -SCALE, None,
                                  ALU.mult).then_inc(qks_evac, 1)

            for j in range(H + 1):
                head_out(j)
            for t in range(NT):
                n = rows(t)
                dve.wait_ge(ktok_full, t + 1)
                dve.tensor_copy(k_st[0:n, t, :], ps[0:n, t % 4, :]).then_inc(ktok_evac, 1)
            dve.wait_ge(hist_full, 1)
            dve.tensor_copy(histT[:, :, :], ps[:, 3, 0:H * HIST].rearrange("p (g s) -> p g s", g=H)).then_inc(hist_evac, 1)
            dve.wait_ge(lam_exp, 1)
            step(dve.tensor_tensor(lam_t[:, 4:5], lam_t[:, 3:4], lam_t[:, 2:3], ALU.subtract))
            dve.tensor_scalar(lam_t[:, 6:7], lam_t[:, 4:5], -LAMBDA_INIT, None, ALU.add).then_inc(lam_made, 1)
            for j in range(H + 1, 2 * H):
                head_out(j)

            def maxima(n):
                t, h = divmod(n, H)
                m, w, b = rows(t), (t + 1) * P if t < PT else PAST + N_SAMPLE, 2 * (n % 2)
                dve.wait_ge(scores_full, n + 1)
                if t < PT:
                    step(dve.memset(ps[0:CHUNK, b:b + 2, w - CHUNK:w], -NEG))
                if n >= 2:
                    dve.wait_ge(exp_done, n - 1)
                dve.tensor_reduce(negm[0:m, n % 2, :], ps[0:m, b:b + 2, 0:w], X, ALU.min).then_inc(negm_ready, 1)

            def differences(n):
                t, h = divmod(n, H)
                m, w = rows(t), (t + 1) * P if t < PT else PAST + N_SAMPLE
                dve.wait_ge(exp_done, n + 1)
                if n == 0:
                    dve.wait_ge(lam_spread, 1)
                step(dve.reciprocal(coef[0:m, 0:1], psums[0:m, t, h, 1:2]))
                step(dve.scalar_tensor_tensor(coef[0:m, 1:2], psums[0:m, t, h, 0:1], neglam[0:m, :], coef[0:m, 0:1],
                                              ALU.mult, ALU.mult))
                dve.scalar_tensor_tensor(prob[0:m, n % 2, 0, 0:w], prob[0:m, n % 2, 1, 0:w], coef[0:m, 1:2],
                                         prob[0:m, n % 2, 0, 0:w], ALU.mult, ALU.add).then_inc(a_ready, 1)

            def o_norm(t):
                m = rows(t)
                r0, q, fac = osc[0:m, 0, :], osc[0:m, 1, :], osc[0:m, 2, :]
                step(dve.reciprocal(r0, psums[0:m, t, :, 0]))
                step(dve.tensor_tensor(q, r0, r0, ALU.mult))
                dve.wait_ge(o_squared, t + 1)
                step(dve.tensor_tensor(q, q, oss[0:m, t, :], ALU.mult))
                step(dve.tensor_scalar(q, q, 1.0 / VD, EPS, ALU.mult, ALU.add))
                inverse_root(fac, q, osc[0:m, 3, :], ovoff[0:m, NT:NT + H])
                step(dve.tensor_tensor(fac, fac, r0, ALU.mult))
                dve.tensor_tensor(otok[0:m, :].rearrange("p (h v) -> p h v", h=H),
                                  ps[0:m, 5 + 2 * (t % 2), :].rearrange("p (h v) -> p h v", h=H),
                                  wide(fac, [m, H, VD]), ALU.mult).then_inc(o_ready, 1)

            def oT_out(t):
                m = rows(t)
                dve.wait_ge(oT_full, t + 1)
                dve.tensor_scalar(mixT[:, H:2 * H, t * P:t * P + m],
                                  ps[:, 5 + 2 * (t % 2), :].rearrange("p (h q) -> p h q", h=H)[:, :, 0:m],
                                  gsub[:, 0:1], None, ALU.mult).then_inc(oT_evac, 1)

            def u_history(g):
                if g >= 2:
                    dve.wait_ge(u_summed, g - 1)
                    dve.wait_ge(diff_ready, g - 1)
                else:
                    dve.wait_ge(x_transposed, NT)
                    dve.wait_ge(xn_ready, NT)
                    dve.memset(uext[:, g % 2, 0:HIST], 0.0)
                dve.tensor_copy(uext[:, g % 2, HIST + N_PROMPT:S0], histT[:, g, :]).then_inc(u_evac_dve, 1)

            def window_diff(g):
                w = WINDOWS[g]
                u, s = uext[:, g % 2, :], usum[:, g % 2, :]
                dve.wait_ge(u_summed, g + 1)
                if g >= 2:
                    dve.wait_ge(dve_step, steps[0])
                step(dve.tensor_tensor(fix[:, 0:w - 1], s[:, HIST:HIST + w - 1], inv_cnt[:, 0:w - 1], ALU.mult))
                step(dve.tensor_tensor(mixT[:, g, 0:w - 1], fix[:, 0:w - 1], u[:, HIST:HIST + w - 1], ALU.subtract))
                step(dve.scalar_tensor_tensor(mixT[:, g, w - 1:N_PROMPT], s[:, HIST + w - 1:HIST + N_PROMPT], 1.0 / w,
                                              u[:, HIST + w - 1:HIST + N_PROMPT], ALU.mult, ALU.subtract))
                dve.scalar_tensor_tensor(mixT[:, g, N_PROMPT:T], s[:, S0:EXT], 1.0 / w, u[:, S0:EXT],
                                         ALU.mult, ALU.subtract).then_inc(diff_ready, 1)

            maxima(0)
            for n in range(UNITS):
                if n + 1 < UNITS:
                    maxima(n + 1)
                if n >= 7 and (n - 7) % H == 0:
                    oT_out((n - 7) // H)
                if n % H == 2 and n < 4 * H:
                    u_history(n // H)
                differences(n)
                if n % H == 1 and n >= H:
                    o_norm(n // H - 1)
                if n % H == 0 and n >= 8:
                    window_diff((n - 8) // H)
            window_diff(H - 1)
            o_norm(NT - 1)
            dve.wait_ge(pool_full, 1)
            dve.tensor_tensor(mixT[:, 0:H, N_PROMPT:T], ps[:, 4, 0:H * N_SAMPLE].rearrange("p (g t) -> p g t", g=H),
                              wide(pscale[:, :], [P, H, N_SAMPLE]), ALU.mult).then_inc(pool_evac_dve, 1)
            dve.wait_ge(state_full, 1)
            dve.tensor_copy(state_out[:, :, :], ps[0:HIST, 6:8, :]).then_inc(state_evac, 1)
            oT_out(NT - 1)

            def residual(t):
                n = rows(t)
                dve.wait_ge(op_full, t + 1)
                dve.wait_ge(xres_loaded[t], 16)
                dve.tensor_tensor(x2[0:n, t, :].rearrange("p (b d) -> p b d", b=2),
                                  ps[0:n, 2 * (t % 2):2 * (t % 2) + 2, :],
                                  x2[0:n, t, :].rearrange("p (b d) -> p b d", b=2), ALU.add).then_inc(x2_ready, 1)

            def h2_norm(t):
                n = rows(t)
                dve.wait_ge(x2_squared, t + 1)
                y = row_scale(t)
                dve.tensor_scalar(h2n[0:n, t % 2, :], x2[0:n, t, :], y, None, ALU.mult).then_inc(h2n_ready, 1)

            def h2T_evac(t):
                n = rows(t)
                dve.wait_ge(h2_transposed, t + 1)
                if t >= 1:
                    dve.wait_ge(router_done, t)
                else:
                    dve.wait_ge(consts_loaded, 80)
                if n < P:
                    step(dve.memset(h2T[:, :, n:P], 0.0))
                dve.tensor_tensor(h2T[:, 0:4, 0:n], ps[:, 4, :].rearrange("p (k t) -> p k t", k=4)[:, :, 0:n],
                                  wide(gffn_sb[:, 0:4], [P, 4, n]), ALU.mult).then_inc(h2T_dve, 1)

            for t in range(NT):
                residual(t)
                if t >= 1:
                    h2T_evac(t - 1)
                h2_norm(t)
            h2T_evac(NT - 1)

            dve.wait_ge(router_done, NT)
            dve.wait_ge(state_stored, 32)
            T4, T44 = [P, NT, G], [P, NT, G, EPG]
            step(dve.tensor_tensor(lg, ps[:, 6, 0:NT * NL].rearrange("p (t l) -> p t l", t=NT),
                                   bias[:, :].unsqueeze(1).to_broadcast([P, NT, NL]), ALU.add))
            gl = lg[:, :, 0:G]
            el = lg[:, :, G:NL].rearrange("p t (g j) -> p t g j", g=G)

            def first_max(src, col, out):
                step(dve.tensor_reduce(rt1[:, col, :], src, X, ALU.max))
                step(dve.tensor_tensor(rt4, src, wide(rt1[:, col, :], T4), ALU.is_equal))
                step(dve.tensor_tensor(rt4, rt4, rev[:, :].unsqueeze(1).to_broadcast(T4), ALU.mult))
                step(dve.tensor_reduce(rt1[:, 2, :], rt4, X, ALU.max))
                step(dve.tensor_tensor(out, rt4, wide(rt1[:, 2, :], T4), ALU.is_equal))

            dve.memset(msum_b[:, NT, :], 0.0)
            dve.memset(rm[:, :, E:], -1.0)
            first_max(gl, 0, g1h)
            sel = etmp.rearrange("p t (g j) -> p t g j", g=G)
            dve.tensor_tensor(gex, gl, wide(rt1[:, 0, :], T4), ALU.subtract).then_inc(gate_in, 1)
            step(dve.tensor_tensor(sel, el, wide(g1h, T44), ALU.mult))
            step(dve.tensor_reduce(esel, etmp.rearrange("p t (g j) -> p t j g", g=G), X, ALU.add))
            first_max(esel, 0, top[:, 0])
            step(dve.scalar_tensor_tensor(rt4b, top[:, 0], NEG, esel, ALU.mult, ALU.add))
            first_max(rt4b, 1, top[:, 1])
            dve.tensor_tensor(rt1[:, 3, :], rt1[:, 1, :], rt1[:, 0, :], ALU.subtract).then_inc(gate_in, 1)
            for c in range(2):
                out = m12[:, c].rearrange("p t (g j) -> p t g j", g=G)
                ins = dve.tensor_tensor(out, wide(g1h, T44), top[:, c].unsqueeze(2).to_broadcast(T44), ALU.mult)
            step(ins)
            step(dve.memset(m12[N_SAMPLE:P, :, NT - 1, :], 0.0))
            step(dve.tensor_tensor(msum, m12[:, 0], m12[:, 1], ALU.add))
            dve.tensor_copy(msum_b[:, 0:NT, :], msum).then_inc(mask_ready, 1)
            dve.wait_ge(rank_full, 1)
            rank = ps[:, 5, 0:NT * E].rearrange("p (t e) -> p t e", t=NT)
            n_e = ps[:, 5, NT * E:(NT + 1) * E]
            step(dve.scalar_tensor_tensor(etmp, rank, 1.0, msum, ALU.add, ALU.mult))
            step(dve.tensor_scalar(rm[:, :, 0:E], etmp, -1.0, None, ALU.add))

            iota_t = iota_row[:, :].unsqueeze(1).to_broadcast([P, NT, P])

            def expert_onehot(e, b):
                col = rm[:, :, DS(e, 1)].rearrange("p t a -> p (t a)")
                return dve.tensor_tensor(onehot_all[:, b], iota_t, wide(col, [P, NT, P]), ALU.is_equal)

            def to_index(b):
                return dve.tensor_scalar(idx[:, b:b + 1], ps[:, 6 + b, 0:1], ps[:, 6 + b, 1:2],
                                         float(NOWHERE), ALU.add, ALU.add)

            dve.wait_ge(h2_stored[0], 48)
            dve.wait_ge(h2_stored[1], 32)
            expert_onehot(0, 0).then_inc(onehot_ready, 1)
            expert_onehot(1, 1).then_inc(onehot_ready, 1)
            for i in range(2):
                dve.wait_ge(idx_full, i + 1)
                to_index(i).then_inc(idx_ready, 1)
            expert_onehot(2, 0).then_inc(onehot_ready, 1)
            dve.wait_ge(gate_exp, 2)
            step(dve.tensor_reduce(rt1[:, 2, :], gex, X, ALU.add))
            step(dve.tensor_scalar(rt1[:, 1, :], rt1[:, 3, :], 1.0, None, ALU.add))
            step(dve.tensor_tensor(rt1[:, 1, :], rt1[:, 1, :], rt1[:, 2, :], ALU.mult))
            step(dve.reciprocal(wtok[:, 0, :], rt1[:, 1, :]))
            step(dve.tensor_tensor(wtok[:, 1, :], wtok[:, 0, :], rt1[:, 3, :], ALU.mult))
            step(dve.tensor_scalar(over, n_e, float(CAP), None, ALU.is_gt))
            for k in range(1, OVK):
                step(dve.scalar_tensor_tensor(over, n_e, float(CAP + k * P), over, ALU.is_gt, ALU.add))
            step(dve.tensor_copy(cum[:, 0, :], over))
            cur = 0
            for shift in (1, 2, 4, 8):
                step(dve.tensor_copy(cum[:, 1 - cur, 0:shift], cum[:, cur, 0:shift]))
                step(dve.tensor_tensor(cum[:, 1 - cur, shift:E], cum[:, cur, shift:E], cum[:, cur, 0:E - shift], ALU.add))
                cur = 1 - cur
            incl, start = cum[:, cur, :], cum[:, 1 - cur, :]
            step(dve.tensor_tensor(start, incl, over, ALU.subtract))
            step(dve.tensor_scalar(start, start, float(P), float(E * P - CAP), ALU.mult, ALU.add))
            step(dve.tensor_tensor(start, start, e128[:, :], ALU.subtract))
            step(dve.tensor_scalar(isov, rank, float(CAP), None, ALU.is_ge))
            over_e = lambda a: a.unsqueeze(1).to_broadcast([P, NT, E])
            step(dve.tensor_tensor(isov, isov, over_e(start), ALU.mult))
            step(dve.tensor_tensor(ylin, rank, isov, ALU.add))
            step(dve.tensor_tensor(ylin, ylin, over_e(e128[:, :]), ALU.add))
            for c in range(2):
                step(dve.tensor_tensor(etmp, m12[:, c], ylin, ALU.mult))
                step(dve.tensor_reduce(yslot_f[:, c, :], etmp, X, ALU.add))
            step(dve.scalar_tensor_tensor(wmain[:, :, :], yslot_f[:, :, :], float(NSLOT), wtok[:, :, :], ALU.is_lt, ALU.mult))
            step(dve.tensor_scalar(yslot[:, :, :], yslot_f[:, :, :], float(NSLOT - 1), None, ALU.min))
            step(dve.tensor_scalar(late_f[:, :, :], yslot_f[:, :, :], float(EARLY * P), float(NSLOT), ALU.is_lt, ALU.mult))
            step(dve.scalar_tensor_tensor(late_f[:, :, :], yslot_f[:, :, :], float(NSLOT - 1), late_f[:, :, :], ALU.min, ALU.add))
            dve.tensor_copy(yslot_late[:, :, :], late_f[:, :, :]).then_inc(wslots_ready, 1)
            step(dve.tensor_tensor(jcmp, incl.unsqueeze(1).to_broadcast([P, MAXOV, E]), wide(jrow[:, :], [P, MAXOV, E]),
                                   ALU.is_le))
            step(dve.tensor_reduce(jsum, jcmp, X, ALU.add))
            step(dve.tensor_scalar(ctl[:, 0:MAXOV], jsum[0:1, :], float(E - 1), None, ALU.min))
            dve.tensor_copy(ctl[:, MAXOV:MAXOV + 1], incl[0:1, E - 1:E]).then_inc(routed, 1)

            def rows_out(b):
                return dve.tensor_tensor(xT[:, b, 0:4, :], ps[:, 0, :].rearrange("p (k s) -> p k s", k=4),
                                         wide(gffn_sb[:, 0:4], [P, 4, P]), ALU.mult)

            dve.wait_ge(h2T_act, NT)
            dve.sem_inc(y_evac_dve, 1)
            dve.wait_ge(xg_transposed, 1)
            rows_out(0).then_inc(xT_dve, 1)
            with dve.Fori(0, E // RING) as it:
                for u in range(RING):
                    i = it * RING + u
                    b = u % 2
                    dve.wait_ge(idx_full, i + 3)
                    dve.wait_ge(xg_loaded[b], it * (8 * RING) + 16 * (u // 2 + 1))
                    to_index(b).then_inc(idx_ready, 1)
                    dve.wait_ge(gact_ready, i + 1)
                    dve.wait_ge(up_full, i + 1)
                    dve.tensor_tensor(heT[:, b], gact[:, b],
                                      ps[:, 3, 0:FE].rearrange("p (c s) -> p c s", c=FC), ALU.mult).then_inc(he_ready, 1)
                    dve.wait_ge(xg_transposed, i + 2)
                    rows_out(1 - b).then_inc(xT_dve, 1)
                    expert_onehot(i + 3, 1 - b).then_inc(onehot_ready, 1)
                    dve.wait_ge(down_done, i + 1)
                    dve.wait_ge(yst_free, i + 1)
                    dve.tensor_copy(yst[:, b, 512:1024], ps[:, 5, :]).then_inc(y_evac_dve, 1)

            n_ov = dve.value_load(ctl[0:1, MAXOV:MAXOV + 1], min_val=0, max_val=MAXOV)
            dve.wait_ge(idx_full, E + 2)
            dve.wait_ge(onehot_ready, E + 3)
            dve.wait_ge(xg_loaded[0], 16 * (E // 2 + 1))
            dve.wait_ge(xg_loaded[1], 16 * (E // 2))
            dve.wait_ge(xT_act, E + 1)
            dve.wait_ge(yst_free, E + 2)
            with dve.Fori(0, MAXOV) as j:
                with dve.If(j < n_ov):
                    def ov_do(ins, n):
                        ins.then_inc(ov_step, 1)
                        dve.wait_ge(ov_step, j * OV_STEPS + n)

                    ov_do(dve.tensor_scalar(ovoff[:, :], yslot_f[:, :, :].rearrange("p c t -> p (c t)"), jbase[:, DS(j, 1)],
                                            None, ALU.subtract), 1)
                    for c in range(2):
                        ins = dve.tensor_tensor(onehot_all[:, c], iota_t, wide(ovoff[:, c * NT:(c + 1) * NT], [P, NT, P]),
                                                ALU.is_equal)
                    ins.then_inc(ov_onehot, 1)
                    dve.wait_ge(ov_idx_full, j + 1)
                    to_index(0).then_inc(ov_idx_ready, 1)
                    offs = ovoff[:, :].rearrange("p (c t) -> p c t", c=2)
                    ov_do(dve.tensor_scalar(ovw[:, :, :], offs, 0.0, None, ALU.is_ge), 2)
                    ov_do(dve.scalar_tensor_tensor(ovw[:, :, :], offs, float(P), ovw[:, :, :], ALU.is_lt, ALU.mult), 3)
                    ov_do(dve.tensor_tensor(ovw[:, :, :], ovw[:, :, :], wtok[:, :, :], ALU.mult), 4)
                    ov_do(dve.tensor_tensor(ovw[:, 0, :], ovw[:, 0, :], ovw[:, 1, :], ALU.add), 5)
                    ov_do(dve.tensor_scalar(slot_tok[:, :], ps[:, 6, 0:1], ps[:, 6, 1:2], float(NOWHERE), ALU.add, ALU.add), 6)
                    for t in range(NT):
                        ins = dve.tensor_scalar(slot_to_token[:, t, :], iota_row[:, :], float(t * P), slot_tok[:, 0:1],
                                                ALU.add, ALU.is_equal)
                    ov_do(ins, OV_STEPS)
                    dve.wait_ge(ov_transposed, j + 1)
                    dve.tensor_tensor(xT[:, 0], ps[:, 0:2, :].rearrange("p b (k s) -> p (b k) s", k=4),
                                      wide(gffn_sb[:, :], [P, KC, P]), ALU.mult).then_inc(ov_xT_ready, 1)
                    dve.wait_ge(ov_gact_ready, j + 1)
                    dve.tensor_tensor(heT[:, 0], gact[:, 0],
                                      ps[:, 3, 0:FE].rearrange("p (c s) -> p c s", c=FC), ALU.mult).then_inc(ov_he_ready, 1)
                    dve.wait_ge(ov_down_done, j + 1)
                    dve.tensor_copy(yst[:, 0, :].rearrange("p (b d) -> p b d", b=2), ps[:, 4:6, :]).then_inc(ov_y_ready, 1)
                    for t in range(NT):
                        n, b = rows(t), 4 - 2 * (t % 2)
                        dve.wait_ge(ov_combine_full, j * NT + (t + 1))
                        xt = x2[0:n, t, :].rearrange("p (b d) -> p b d", b=2)
                        dve.scalar_tensor_tensor(xt, ps[0:n, b:b + 2, :], ovw[0:n, 0, t:t + 1], xt,
                                                 ALU.mult, ALU.add).then_inc(ov_added, 1)
                    dve.wait_ge(ov_added, (j + 1) * NT)
                    dve.sem_inc(ov_tile_done, 1)
                dve.nop()

            def combine(t):
                n = rows(t)
                dve.wait_ge(early_gathered, 32 * NT)
                dve.wait_ge(y_gathered[t], 32)
                step(dve.scalar_tensor_tensor(y1[t][0:n, :], y1[t][0:n, :], wmain[0:n, 0, t:t + 1], x2[0:n, t, :],
                                              ALU.mult, ALU.add))
                dve.scalar_tensor_tensor(y1[t][0:n, :], y2[t][0:n, :], wmain[0:n, 1, t:t + 1], y1[t][0:n, :],
                                         ALU.mult, ALU.add).then_inc(acc_ready, 1)

            def finish(tiles):
                c = slice(tiles[0], tiles[-1] + 1)
                dve.wait_ge(acc_squared, tiles[-1] + 1)
                m, y, tmp, half = rs[:, 1, c], rs[:, 0, c], rs[:, 2, c], ovoff[:, c]
                step(dve.tensor_scalar(m, ss[:, c], 1.0 / D, EPS, ALU.mult, ALU.add))
                inverse_root(y, m, tmp, half)
                for t in tiles:
                    n = rows(t)
                    dve.scalar_tensor_tensor(y2[t][0:n, :], y1[t][0:n, :], rs[0:n, 0, t:t + 1], gfin[0:n, :],
                                             ALU.mult, ALU.mult).then_inc(out_ready, 1)

            dve.wait_ge(gfin_loaded, 16)
            step(dve.memset(ss[N_SAMPLE:P, NT - 1:NT], 1.0))
            for t in range(4):
                combine(t)
            finish(range(3))
            combine(4)
            finish(range(3, NT))


_INS = ["x_prompt", "x_sample", "cache_k", "cache_v", "state_pool", "g_mix", "w_in", "w_pool", "pool_scale",
        "lam_q1", "lam_k1", "lam_q2", "lam_k2", "g_subln", "w_out", "g_ffn", "w_group", "b_group", "w_erouter",
        "b_erouter", "w_gate", "w_up", "w_down", "g_final"]
_OUTS = [("y_prompt", (1, N_PROMPT, D)), ("y_sample", (1, N_SAMPLE, D)),
         ("k_prompt", (1, 1, N_PROMPT, H, 2 * HD)), ("v_prompt", (1, 1, N_PROMPT, H, VD)),
         ("pool_prompt", (1, 1, HIST, PW)),
         ("k_sample", (1, 1, N_SAMPLE, H, 2 * HD)), ("v_sample", (1, 1, N_SAMPLE, H, VD)),
         ("pool_sample", (1, 1, HIST, PW))]


def kernel(**inputs):
    import numpy as _np
    import concourse.bacc as _bacc
    from concourse.bass_utils import run_bass_kernel_spmd as _run

    nc = _bacc.Bacc("TRN2", target_bir_lowering=False, num_devices=1)
    arrays, args = {}, {}
    for name in _INS:
        a = _np.ascontiguousarray(inputs[name])
        arrays[f"in_{name}"] = a
        args[name] = nc.dram_tensor(f"in_{name}", a.shape, mybir.dt.from_np(a.dtype), kind="ExternalInput").ap()
    for name, shape in _OUTS:
        args[name] = nc.dram_tensor(f"out_{name}", shape, F32, kind="ExternalOutput").ap()
    build(nc, **args)
    r = _run(nc, [arrays], core_ids=[0])
    return tuple(r.results[0][f"out_{name}"] for name, _ in _OUTS)
```

```python
import math
from contextlib import ExitStack

import numpy as np

import concourse.bass as bass
from concourse import mybir

F32 = mybir.dt.float32
F32R = mybir.dt.float32r
BF16 = mybir.dt.bfloat16
I32 = mybir.dt.int32
ALU = mybir.AluOpType
ACT = mybir.ActivationFunctionType
X = mybir.AxisListType.X
DS = bass.ds

P = 128
D = 1024
KC = D // P
N_PROMPT, N_SAMPLE = 512, 64
T = N_PROMPT + N_SAMPLE
NT = 5
PT = N_PROMPT // P
PAST = 256
CHUNK = 64
HIST = 15
WINDOWS = (2, 4, 8, 16)
H = 4
HD = 64
VD = 2 * HD
PW = 512
SCALE = HD ** -0.5
NEG = -1e30
LAMBDA_INIT = 0.8 - 0.6 * math.exp(0.0)
EPS = 1e-6
G, EPG = 4, 4
E = G * EPG
FE = 256
FC = FE // P
NL = G + E
CAP = 128
MAXOV = (2 * T) // (CAP + 1)
OVK = -(-(T - CAP) // P)
NSLOT = (E - 1) * P
RING = 4
POOL_TILES = (3, 4)
GATHER_ORDER = (0, 3, 1, 4, 2)
OWN_TILES = (0, 1, 2)
ACT_OWN = (0, 1)
ACT_LATE = 3
BY_ACT = ACT_OWN + (ACT_LATE,)
BY_DVE = tuple(t for t in range(len(OWN_TILES + POOL_TILES)) if t not in BY_ACT)
NOWHERE = 1024
UNITS = NT * H
OV_STEPS = 7
WB = KC * FE


def rows(t):
    return P if t < PT else N_SAMPLE


def build(nc, x_prompt, x_sample, cache_k, cache_v, state_pool, g_mix, w_in, w_pool, pool_scale,
          lam_q1, lam_k1, lam_q2, lam_k2, g_subln, w_out, g_ffn, w_group, b_group, w_erouter,
          b_erouter, w_gate, w_up, w_down, g_final,
          y_prompt, y_sample, k_prompt, v_prompt, pool_prompt, k_sample, v_sample, pool_sample):
    ctx = ExitStack()
    with ctx:
        def sb(name, shape, dt=F32):
            return ctx.enter_context(nc.sbuf_tensor(name, shape, dt))

        def sb_both(name, shape):
            with nc.sbuf_tensor(name, shape, F32) as plain:
                pass
            return plain, ctx.enter_context(nc.sbuf_tensor(name + "_r", shape, F32R))

        def sem(name):
            return ctx.enter_context(nc.semaphore(name))

        def sems(name, n):
            return [sem(f"{name}{i}") for i in range(n)]

        xp = x_prompt.rearrange("a (t p) d -> (a t) p d", p=P)
        xs = x_sample.rearrange("a s d -> (a s) d")
        win_v = w_in.rearrange("a (p k) n -> (a p) k n", k=KC)
        wout_v = w_out.rearrange("a (f p) n -> p (a f) n", p=P)
        ck_v = cache_k.rearrange("a b (t p) h d -> p (a b t) (h d)", p=P)
        cv_v = cache_v.rearrange("a b (t p) h d -> p (a b t) (h d)", p=P)
        kp_v = k_prompt.rearrange("a b (t p) h d -> (a b t) p (h d)", p=P)
        vp_v = v_prompt.rearrange("a b (t p) h d -> (a b t) p (h d)", p=P)
        ks_v = k_sample.rearrange("a b s h d -> (a b s) (h d)")
        vs_v = v_sample.rearrange("a b s h d -> (a b s) (h d)")
        yp_v = y_prompt.rearrange("a (t p) d -> (a t) p d", p=P)
        ys_v = y_sample.rearrange("a s d -> (a s) d")
        wg_v = w_gate.rearrange("a e (p k) f -> (a e) p (k f)", k=KC)
        wu_v = w_up.rearrange("a e (p k) f -> (a e) p (k f)", k=KC)
        wd_v = w_down.rearrange("a e (c p) n -> (a e) p c n", p=P)
        h2_dram = nc.dram_tensor("h2_rows", (T, D), F32, kind="Internal").ap()
        y_dram = nc.dram_tensor("expert_rows", (NSLOT, D), F32, kind="Internal").ap()

        region_a, region_a_r = sb_both("region_a", [P, 12800])
        region_w, region_w_r = sb_both("region_w", [P, 8192])
        hT_hi, hT_lo = (region_a_r[:, b * 4608:(b + 1) * 4608].rearrange("p (k t) -> p k t", k=KC) for b in range(2))
        w_in_sb = [region_w[:, b * 4096:(b + 1) * 4096].rearrange("p (k n) -> p k n", k=KC) for b in range(2)]
        w_in_lo = [region_w_r[:, b * 4096:(b + 1) * 4096].rearrange("p (k n) -> p k n", k=KC) for b in range(2)]
        w_out_sb = region_w[:, :].rearrange("p (f n) -> p f n", f=KC)
        w_out_lo = region_w_r[:, :].rearrange("p (f n) -> p f n", f=KC)
        ring0, ring0_r = sb_both("ring0", [P, 6144])
        ring = [ring0[:, :], region_a[:, 0:6144], region_a[:, 6144:12288], region_w[:, 0:6144]]
        wg_sb = [r[:, 0:WB].rearrange("p (k f) -> p k f", k=KC) for r in ring]
        wu_sb = [r[:, WB:2 * WB].rearrange("p (k f) -> p k f", k=KC) for r in ring]
        wd_sb = [r[:, 2 * WB:3 * WB].rearrange("p (c n) -> p c n", c=FC) for r in ring]

        region_q = sb("region_q", [P, 5632])
        qT = region_q[:, 0:2304].rearrange("p (h t) -> p h t", h=H)
        kT = region_q[:, 2304:4608].rearrange("p (h t) -> p h t", h=H)
        kcT = region_q[:, 4608:5632].rearrange("p (h t) -> p h t", h=H)
        x2 = region_q[:, 0:NT * D].rearrange("p (t d) -> p t d", t=NT)

        mix, mix_r = sb_both("mix", [P, KC * T])
        mixT = mix[:, :].rearrange("p (k t) -> p k t", k=KC)
        mix_hi = mix_r[:, :].rearrange("p (k t) -> p k t", k=KC)
        w_in_hi = [a.rearrange("p (k n) -> p k n", k=KC) for a in (ring0_r[:, 0:4096], mix_r[:, 0:4096])]

        region_v = sb("region_v", [P, 3584])
        v_pr = region_v[:, 0:2048].rearrange("p (t n) -> p t n", t=PT)
        v_sa = region_v[:, 2048:3584].rearrange("p (t n) -> p t n", t=3)
        h2n = region_v[:, 0:2048].rearrange("p (b d) -> p b d", b=2)
        h2T = region_v[:, 2048:3072].rearrange("p (k t) -> p k t", k=KC)
        onehot_all = region_v[:, 0:640].bitcast(BF16).rearrange("p (b t s) -> p b t s", b=2, t=NT)

        region_k, region_k_r = sb_both("region_k", [P, 1792])
        hist_in = region_k[0:HIST, 1024:1024 + PW]
        kc_raw = region_k[:, 0:1024].rearrange("p (t n) -> p t n", t=2)
        k_st = region_a[:, 9216:9216 + NT * PW].rearrange("p (t n) -> p t n", t=NT)
        state_out = region_k[0:HIST, 0:1024].rearrange("p (b n) -> p b n", b=2)

        mix_lo = [region_a_r[:, 11520:11520 + T], region_a_r[:, 11520 + T:11520 + 2 * T], region_a_r[:, 8192:8192 + T],
                  region_k_r[:, 1024:1024 + T], *(region_a_r[:, 9216 + h * T:9216 + (h + 1) * T] for h in range(H))]
        mix_lo_heads = region_a_r[:, 9216:9216 + H * T].rearrange("p (h t) -> p h t", h=H)

        region_p, region_p_r = sb_both("region_p", [P, 2048])
        prob = region_p[:, :].rearrange("p (b c k) -> p b c k", b=2, c=2)
        xT = region_p[:, :].rearrange("p (b k s) -> p b k s", b=2, k=KC)
        region_t = sb("region_t", [P, 1536])
        aT = region_t[:, 0:1024].rearrange("p (b k) -> p b k", b=2)
        otok = region_t[:, 1024:1536]
        gact = region_t[:, 0:512].rearrange("p (b c s) -> p b c s", b=2, c=FC)
        heT = region_t[:, 512:1024].rearrange("p (b c s) -> p b c s", b=2, c=FC)

        region_x, region_x_r = sb_both("region_x", [P, 4096])
        xraw = region_x[:, 0:2048].rearrange("p (b d) -> p b d", b=2)
        xn = region_x[:, 2048:4096].rearrange("p (b d) -> p b d", b=2)
        EXT = HIST + N_PROMPT + HIST + N_SAMPLE
        S0 = 2 * HIST + N_PROMPT
        uext = region_x[:, 0:2 * EXT].rearrange("p (b t) -> p b t", b=2)
        usum = region_x[:, 2 * EXT:4 * EXT].rearrange("p (b t) -> p b t", b=2)
        w_pool_sb = region_x[:, 4 * EXT:4 * EXT + 512].rearrange("p (g e) -> p g e", g=H)
        xg = region_x[:, 0:2048].rearrange("p (b d) -> p b d", b=2)
        yst = region_x[:, 2048:4096].rearrange("p (b d) -> p b d", b=2)
        slot_to_token = region_x[:, D:D + NT * P].rearrange("p (t s) -> p t s", t=NT)

        w_hi_extra = sb("w_hi_extra", [P, D], F32R)
        w_out_hi = [region_p_r[:, 0:D], region_p_r[:, D:2 * D], region_x_r[:, 0:D], region_x_r[:, D:2 * D], ring0_r[:, 4096:5120], ring0_r[:, 5120:6144],
                    region_x_r[:, 3072:4096], w_hi_extra[:, :]]

        y1 = [mix[:, t * D:(t + 1) * D] for t in range(PT)] + [region_v[:, 2048:3072]]
        y2 = [region_w[:, 6144:7168], region_w[:, 7168:8192]] + [ring0[:, t * D:(t + 1) * D] for t in range(3)]
        gfin = region_k[:, 0:D]

        ident = sb("ident", [P, P])
        iota_row = sb("iota_row", [P, P])
        tri = sb("tri", [P, P], BF16)
        ones = sb("ones", [P, P], BF16)
        gmix_sb = sb("gmix_sb", [P, KC])
        gffn_sb = sb("gffn_sb", [P, KC])
        pscale = sb("pscale", [P, H])
        gsub = sb("gsub", [P, 1])
        wr = sb("wr", [P, KC, NL])
        bias = sb("bias", [P, NL])
        lam_in = sb("lam_in", [1, 4, HD])
        lam_t = sb("lam_t", [1, 8])
        neglam = sb("neglam", [P, 1])
        histT = sb("histT", [P, H, HIST])
        ustate = sb("ustate", [P, 2, H, HIST])
        inv_cnt = sb("inv_cnt", [P, 16])
        ss = sb("ss", [P, NT])
        ss2 = sb("ss2", [P, 2, NT])
        warm = sb("warm", [P, 1])
        rs = sb("rs", [P, 3, NT])
        negm = sb("negm", [P, 2, 2])
        psums = sb("psums", [P, NT, H, 2])
        coef = sb("coef", [P, 2])
        oss = sb("oss", [P, NT, H])
        osc = sb("osc", [P, 4, H])
        rev = sb("rev", [P, 4])
        tokv = sb("tokv", [P, NT, 2], BF16)
        idx = sb("idx", [P, 2], I32)
        ctl = sb("ctl", [1, MAXOV + 1], I32)
        wtok = sb("wtok", [P, 2, NT])
        yslot = sb("yslot", [P, 2, NT], I32)
        w_last = sb("w_last", [P, 2, NT])
        yslot_f = sb("yslot_f", [P, 2, NT])
        rm = sb("rm", [P, NT, E])
        e128 = sb("e128", [P, E])
        jrow = sb("jrow", [P, MAXOV])
        jbase = sb("jbase", [P, MAXOV])
        ovoff = sb("ovoff", [P, 2 * NT])
        eps_col = sb("eps_col", [P, 1])
        ovw = sb("ovw", [P, 2, NT])
        slot_tok = sb("slot_tok", [P, 1])
        wmain = sb("wmain", [P, 2, NT])
        fix = sb("fix", [P, HIST])

        scratch = [0]

        def rt(*shape):
            n = int(np.prod(shape))
            a = region_k[:, scratch[0]:scratch[0] + n]
            scratch[0] += n
            assert scratch[0] <= 1792
            if len(shape) == 1:
                return a
            names = "abcd"[:len(shape)]
            return a.rearrange(f"p ({' '.join(names)}) -> p {' '.join(names)}",
                               **{c: s for c, s in zip(names, shape)})
        lg = rt(NT, NL)
        g1h = rt(NT, G)
        top = rt(2, NT, G, EPG)
        rt4 = rt(NT, G)
        rt16 = rt(NT, G, EPG)
        grp = rt(3, NT, G)
        rt1 = rt(4, NT)
        gex = rt(NT, G)
        m12 = rt(2, NT, E)
        msum = rt(NT, E)
        msum_b = rt((NT + 1) * E // 2).bitcast(BF16).rearrange("p (t e) -> p t e", t=NT + 1)
        over = rt(E)
        cum = rt(2, E)
        isov = rt(NT, E)
        rt16b = rt(NT, G, EPG)
        ylin = rt(NT, E)
        etmp = rt(NT, E)
        jcmp = rt(MAXOV, E)
        jsum = rt(MAXOV)

        ps = ctx.enter_context(nc.psum_tensor("ps", [P, 8, 512], F32))

        x_loaded = sems("x_loaded", 2)
        gmix_loaded = sem("gmix_loaded")
        consts_loaded = sem("consts_loaded")
        lam_loaded = sem("lam_loaded")
        gsub_loaded = sem("gsub_loaded")
        w_v_loaded = sems("w_v_loaded", KC // 2)
        w_in_loaded = sems("w_in_loaded", 3)
        w_q_loaded = sem("w_q_loaded")
        w_hi_ready = sem("w_hi_ready")
        w_lo_ready = sem("w_lo_ready")
        w_lo_by_pool = sem("w_lo_by_pool")
        w_out_hi_ready = sem("w_out_hi_ready")
        w_out_lo_ready = sem("w_out_lo_ready")
        w_out_lo_by_pool = sem("w_out_lo_by_pool")
        cache_loaded = sem("cache_loaded")
        w_pool_loaded = sem("w_pool_loaded")
        w_out_loaded = sems("w_out_loaded", 2)
        xres_loaded = sems("xres_loaded", NT)
        ring_loaded = sems("ring_loaded", RING)
        gfin_loaded = sem("gfin_loaded")
        consts_made = sem("consts_made")
        pool_step = sem("pool_step")
        dve_step = sem("dve_step")
        x_squared = sem("x_squared")
        x_scale_ready = sem("x_scale_ready")
        x2_sum_ready = sem("x2_sum_ready")
        root_ready = sem("root_ready")
        xn_ready = sem("xn_ready")
        x_transposed = sem("x_transposed")
        hT_ready = sem("hT_ready")
        hT_act = sem("hT_act")
        v_full = sem("v_full")
        v_evac = sem("v_evac")
        v_stored = sem("v_stored")
        qk_full = sem("qk_full")
        qk_evac_act = sem("qk_evac_act")
        qk_evac_dve = sem("qk_evac_dve")
        ktok_full = sem("ktok_full")
        ktok_evac = sem("ktok_evac")
        k_stored = sem("k_stored")
        kc_full = sem("kc_full")
        kc_evac = sem("kc_evac")
        hist_full = sem("hist_full")
        hist_evac = sem("hist_evac")
        lam_dots = sem("lam_dots")
        lam_exp = sem("lam_exp")
        lam_made = sem("lam_made")
        lam_spread = sem("lam_spread")
        scores_full = sem("scores_full")
        negm_ready = sem("negm_ready")
        exp_done = sem("exp_done")
        a_ready = sem("a_ready")
        aT_full = sem("aT_full")
        aT_evac = sem("aT_evac")
        pv_done = sem("pv_done")
        o_squared = sem("o_squared")
        o_ready = sem("o_ready")
        oT_full = sem("oT_full")
        oT_evac = sem("oT_evac")
        u_full = sem("u_full")
        u_evac_act = sem("u_evac_act")
        u_evac_dve = sem("u_evac_dve")
        u_summed = sem("u_summed")
        diff_ready = sem("diff_ready")
        pool_full = sem("pool_full")
        pool_hi_ready = sem("pool_hi_ready")
        pool_evac = sem("pool_evac")
        pool_evac_sample = sem("pool_evac_sample")
        state_full = sem("state_full")
        state_evac = sem("state_evac")
        state_stored = sem("state_stored")
        op_full = sem("op_full")
        x2_ready = sem("x2_ready")
        x2_squared = sem("x2_squared")
        h2n_ready = sem("h2n_ready")
        h2_stored = sems("h2_stored", 2)
        h2_transposed = sem("h2_transposed")
        h2T_dve = sem("h2T_dve")
        h2T_act = sem("h2T_act")
        router_done = sem("router_done")
        wr_scaled = sem("wr_scaled")
        gate_in = sem("gate_in")
        gate_exp = sem("gate_exp")
        mask_ready = sem("mask_ready")
        rank_full = sem("rank_full")
        routed = sem("routed")
        xg_cleared = sem("xg_cleared")
        onehot_ready = sem("onehot_ready")
        idx_full = sem("idx_full")
        idx_ready = sem("idx_ready")
        xg_loaded = sems("xg_loaded", 2)
        xg_transposed = sem("xg_transposed")
        xT_dve = sem("xT_dve")
        xT_act = sem("xT_act")
        gate_full = sem("gate_full")
        up_full = sem("up_full")
        gact_ready = sem("gact_ready")
        he_ready = sem("he_ready")
        down_done = sem("down_done")
        y_evac_act = sem("y_evac_act")
        y_evac_dve = sem("y_evac_dve")
        y_stored = sem("y_stored")
        yst_free = sem("yst_free")
        ov_step = sem("ov_step")
        ov_onehot = sem("ov_onehot")
        ov_idx_full = sem("ov_idx_full")
        ov_idx_ready = sem("ov_idx_ready")
        ov_gathered = sem("ov_gathered")
        ov_w_loaded = sem("ov_w_loaded")
        ov_transposed = sem("ov_transposed")
        ov_xT_ready = sem("ov_xT_ready")
        ov_gate_full = sem("ov_gate_full")
        ov_gact_ready = sem("ov_gact_ready")
        ov_he_ready = sem("ov_he_ready")
        ov_down_done = sem("ov_down_done")
        ov_y_ready = sem("ov_y_ready")
        ov_combine_full = sem("ov_combine_full")
        ov_added = sem("ov_added")
        ov_tile_done = sem("ov_tile_done")
        ov_w_free = sem("ov_w_free")
        ov_gather_begun = sem("ov_gather_begun")
        last_onehot = sem("last_onehot")
        weighted = sem("weighted")
        last_full = sem("last_full")
        combined_by_pool = sem("combined_by_pool")
        y_gathered = sems("y_gathered", NT)
        acc_ready = sem("acc_ready")
        acc_squared = sem("acc_squared")
        factors_ready = sem("factors_ready")
        gained_by_pool = sem("gained_by_pool")
        gained_by_dve = sem("gained_by_dve")
        out_by_act = sem("out_by_act")
        out_by_dve = sem("out_by_dve")
        out_stored = sem("out_stored")
        wslots_ready = sem("wslots_ready")

        block = ctx.enter_context(nc.Block())
        HALF = T // 2
        V_EARLY = 2
        X_EARLY = 3
        V_POOL = 3
        V_BLK, K_BLK, Q_BLK, U_BLK = 3, 2, 1, 0
        IN_ORDER = (V_BLK, K_BLK, Q_BLK, U_BLK)

        @block.sync
        def _(sp):
            def load_x(t):
                src = xp[t] if t < PT else xs
                sp.dma_start(xraw[0:rows(t), t % 2, :], src).then_inc(x_loaded[t % 2], 16)

            def load_w_in(j):
                b, buf = IN_ORDER[j], 1 - j % 2
                if j == 2:
                    for part, loaded in ((0, w_in_loaded[1]), (1, w_q_loaded)):
                        cols = slice(part * PW // 2, (part + 1) * PW // 2)
                        sp.dma_start(w_in_sb[buf][:, :, cols],
                                     win_v[:, :, b * PW + cols.start:b * PW + cols.stop]).then_inc(loaded, 16)
                    return
                for k in range(0, KC, 2 if j == 0 else KC):
                    ks = slice(k, k + (2 if j == 0 else KC))
                    sp.dma_start(w_in_sb[buf][:, ks, :], win_v[:, ks, b * PW:(b + 1) * PW]).then_inc(
                        w_v_loaded[k // 2] if j == 0 else w_in_loaded[j - 1], 16)

            def load_gate_up(slot, e, signal=None):
                load_gate(slot, e, signal)
                load_up(slot, e, signal)

            def load_gate(slot, e, signal=None):
                signal = signal or ring_loaded[slot]
                sp.dma_start(ring[slot][:, 0:WB], wg_v[DS(e, 1)].rearrange("a p n -> (a p) n")).then_inc(signal, 16)

            def load_up(slot, e, signal=None):
                signal = signal or ring_loaded[slot]
                sp.dma_start(ring[slot][:, WB:2 * WB], wu_v[DS(e, 1)].rearrange("a p n -> (a p) n")).then_inc(signal, 16)

            def load_down(slot, e, signal=None):
                signal = signal or ring_loaded[slot]
                sp.dma_start(wd_sb[slot], wd_v[DS(e, 1)].rearrange("a p c n -> (a p) c n")).then_inc(signal, 16)

            def load_expert(slot, e, signal=None):
                load_gate_up(slot, e, signal)
                load_down(slot, e, signal)

            load_x(0)
            sp.dma_start(gmix_sb[:, :], g_mix.rearrange("a (p k) -> (a p) k", k=KC)).then_inc(gmix_loaded, 16)
            load_x(1)
            load_w_in(0)
            for t in range(2, NT):
                sp.wait_ge(xn_ready, t - 1)
                load_x(t)
                if t == X_EARLY:
                    load_w_in(1)
            sp.dma_start(kc_raw, ck_v).then_inc(cache_loaded, 16)
            sp.dma_start(hist_in, state_pool.rearrange("a b s c -> (a b s) c")).then_inc(cache_loaded, 16)
            sp.dma_start(v_sa[:, 0:2, :], cv_v).then_inc(cache_loaded, 16)
            for n, v in enumerate((lam_q1, lam_q2, lam_k1, lam_k2)):
                sp.dma_start(lam_in[:, n, :], v).then_inc(lam_loaded, 16)
            sp.dma_start(gsub[:, :], g_subln.rearrange("a (v o) -> (a v) o", o=1)).then_inc(gsub_loaded, 16)
            with nc.allow_non_contiguous_dma(reason="512 scale values"):
                sp.dma_start(pscale[:, :], pool_scale.rearrange("a (g p) -> p (a g)", p=P)).then_inc(w_pool_loaded, 16)
            for j in (2, 3):
                sp.wait_ge(*((v_full, NT) if j == 2 else (qk_full, H)))
                load_w_in(j)
                if j == 2:
                    sp.wait_ge(x_transposed, NT)
                    sp.dma_start(w_pool_sb, w_pool.rearrange("a g c e -> c (a g) e")).then_inc(w_pool_loaded, 16)
            def load_w_out(half):
                f = slice(half * H, (half + 1) * H)
                sp.dma_start(w_out_sb[:, f, :], wout_v[:, f, :]).then_inc(w_out_loaded[half], 16)

            sp.wait_ge(qk_full, 2 * H)
            load_w_out(1)
            sp.dma_start(gffn_sb[:, :], g_ffn.rearrange("a (p k) -> (a p) k", k=KC)).then_inc(consts_loaded, 16)
            sp.dma_start(wr[:, :, 0:G], w_group.rearrange("a (p k) g -> (a p) k g", k=KC)).then_inc(consts_loaded, 16)
            sp.dma_start(wr[:, :, G:NL], w_erouter.rearrange("a (p k) g -> (a p) k g", k=KC)).then_inc(consts_loaded, 16)
            sp.dma_start(bias[:, 0:G], b_group.to_broadcast([P, G])).then_inc(consts_loaded, 16)
            sp.dma_start(bias[:, G:NL], b_erouter.to_broadcast([P, E])).then_inc(consts_loaded, 16)
            sp.wait_ge(u_full, 2 * H)
            load_w_out(0)
            load_gate_up(0, 0)
            load_expert(1, 1)
            load_gate(2, 2)
            sp.wait_ge(scores_full, UNITS)
            for t in range(NT):
                src = xp[t] if t < PT else xs
                sp.dma_start(x2[0:rows(t), t, :], src).then_inc(xres_loaded[t], 16)
            sp.wait_ge(op_full, 2 * NT)
            sp.wait_ge(k_stored, 16 * NT)
            load_down(0, 0)
            load_up(2, 2)
            sp.wait_ge(h2_stored[0], 48)
            sp.wait_ge(h2_stored[1], 32)
            load_down(2, 2)
            sp.wait_ge(xg_loaded[0], 16)
            sp.wait_ge(xg_loaded[1], 16)
            load_expert(3, 3)
            sp.wait_ge(routed, 1)
            sp.wait_ge(wslots_ready, 1)
            sp.dma_start(gfin, g_final.rearrange("(a d) -> a d", a=1).to_broadcast([P, D])).then_inc(gfin_loaded, 16)

            sp.sem_inc(yst_free, 2)

            def store_rows(i, b, row):
                sp.wait_ge(y_evac_act, i + 2)
                sp.wait_ge(y_evac_dve, i + 2)
                sp.dma_start(y_dram[row, :], yst[:, b, :]).then_inc(y_stored, 16)

            def free_rows(i):
                sp.wait_ge(y_stored, i * 16 + 16)
                sp.sem_inc(yst_free, 1)

            with sp.Fori(0, E // RING - 1) as it:
                for u in range(RING):
                    i = it * RING + u
                    store_rows(i, u % 2, DS(i * P, P))
                    load_expert(u, i + RING)
                    free_rows(i)
            for i in range(E - RING, E - 1):
                store_rows(i, i % 2, slice(i * P, (i + 1) * P))
                free_rows(i)

            sp.wait_ge(down_done, E)
            n_ov = sp.value_load(ctl[0:1, MAXOV:MAXOV + 1], min_val=0, max_val=MAXOV)
            with sp.If(n_ov > 0):
                with sp.Fori(0, MAXOV) as j:
                    with sp.If(j < n_ov):
                        e = sp.value_load(ctl[0:1, DS(j, 1)], min_val=0, max_val=E - 1)
                        load_expert(RING - 1, e, ov_w_loaded)
                        sp.wait_ge(ov_down_done, j + 1)
                        sp.sem_inc(ov_w_free, 1)
                    sp.nop()
            for t in range(NT):
                if t in BY_ACT:
                    sp.wait_ge(out_by_act, BY_ACT.index(t) + 1)
                else:
                    sp.wait_ge(out_by_dve, BY_DVE.index(t) + 1)
                sp.dma_start(yp_v[t] if t < PT else ys_v, y2[t][0:rows(t), :]).then_inc(out_stored, 16)
            sp.wait_ge(out_stored, 16 * NT)

        @block.gpsimd
        def _(pool):
            made = [0]

            def step(ins):
                made[0] += 1
                ins.then_inc(pool_step, 1)
                pool.wait_ge(pool_step, made[0])

            pool.memset(eps_col[:, :], EPS)
            pool.memset(ones[:, :], 1.0)
            step(pool.memset(ident[:, :], 0.0))
            pool.affine_select(out=ident[:, :], in_=ident[:, :], compare_op=ALU.not_equal, fill=1.0, base=0,
                               pattern=[[-1, P]], channel_multiplier=1).then_inc(consts_made, 1)
            step(pool.affine_select(out=tri[:, :], in_=ones[:, :], compare_op=ALU.is_gt, fill=0.0, base=0,
                                    pattern=[[1, P]], channel_multiplier=-1))
            step(pool.iota(iota_row[:, :], pattern=[[1, P]], base=0, channel_multiplier=0,
                           allow_small_or_imprecise_dtypes=True))
            step(pool.iota(inv_cnt[:, :], pattern=[[1, 16]], base=1, channel_multiplier=0,
                           allow_small_or_imprecise_dtypes=True))
            step(pool.iota(rev[:, :], pattern=[[-1, 4]], base=4, channel_multiplier=0,
                           allow_small_or_imprecise_dtypes=True))
            step(pool.iota(e128[:, :], pattern=[[P, E]], base=0, channel_multiplier=0,
                           allow_small_or_imprecise_dtypes=True))
            step(pool.iota(jrow[:, :], pattern=[[1, MAXOV]], base=0, channel_multiplier=0,
                           allow_small_or_imprecise_dtypes=True))
            step(pool.iota(jbase[:, :], pattern=[[P, MAXOV]], base=E * P, channel_multiplier=0,
                           allow_small_or_imprecise_dtypes=True))
            step(pool.iota(tokv[:, :, 0], pattern=[[P, NT]], base=-NOWHERE, channel_multiplier=0,
                           allow_small_or_imprecise_dtypes=True))
            pool.iota(tokv[:, :, 1], pattern=[[0, NT]], base=0, channel_multiplier=1,
                      allow_small_or_imprecise_dtypes=True).then_inc(consts_made, 1)

            for c in range(KC - V_POOL, KC):
                pool.wait_ge(w_hi_ready, c + 1)
                pool.tensor_tensor(w_in_lo[1][:, c, :], w_in_sb[1][:, c, :], w_in_hi[1][:, c, :].bitcast(F32),
                                   ALU.subtract).then_inc(w_lo_by_pool, 1)

            for t in range(NT):
                pool.wait_ge(v_evac, t + 1)
                dst = vp_v[t] if t < PT else vs_v
                src = v_pr[:, t, :] if t < PT else v_sa[0:N_SAMPLE, 2, :]
                pool.dma_start(dst, src).then_inc(v_stored, 16)
            for t in range(NT):
                pool.wait_ge(ktok_evac, t + 1)
                pool.dma_start(kp_v[t] if t < PT else ks_v, k_st[0:rows(t), t, :]).then_inc(k_stored, 16)

            pool.wait_ge(lam_made, 1)
            pool.partition_broadcast(neglam[:, :], lam_t[0:1, 6:7]).then_inc(lam_spread, 1)

            for g in range(H):
                pool.wait_ge(u_evac_act, 2 * g + 2)
                pool.wait_ge(u_evac_dve, g + 1)
                if g >= 1:
                    pool.wait_ge(diff_ready, g)
                src, shift = uext[:, g % 2, :], 1
                for lev in range(g + 1):
                    dst = usum[:, lev % 2, :]
                    lo = 2 * shift - 1
                    ins = pool.tensor_tensor(dst[:, lo:EXT], src[:, lo:EXT], src[:, lo - shift:EXT - shift], ALU.add)
                    step(ins)
                    src, shift = dst, 2 * shift
                pool.tensor_copy(ustate[:, 0, g, :], uext[:, g % 2, N_PROMPT:N_PROMPT + HIST])
                pool.tensor_copy(ustate[:, 1, g, :], uext[:, g % 2, EXT - HIST:EXT]).then_inc(u_summed, 1)
                for c in ((), (0,), (1, 2), (3,))[g]:
                    pool.wait_ge(w_out_hi_ready, c + 1)
                    pool.tensor_tensor(w_out_lo[:, H + c, :], w_out_sb[:, H + c, :], w_out_hi[H + c].bitcast(F32),
                                       ALU.subtract).then_inc(w_out_lo_by_pool, 1)
            pool.wait_ge(state_evac, 1)
            pool.dma_start(pool_prompt.rearrange("a b s c -> (a b s) c"), state_out[:, 0, :]).then_inc(state_stored, 16)
            pool.dma_start(pool_sample.rearrange("a b s c -> (a b s) c"), state_out[:, 1, :]).then_inc(state_stored, 16)

            for t in range(NT):
                pool.wait_ge(h2n_ready, t + 1)
                pool.dma_start(h2_dram[t * P:t * P + rows(t), :], h2n[0:rows(t), t % 2, :]).then_inc(h2_stored[t % 2], 16)
            pool.wait_ge(op_full, 2 * NT)
            pool.memset(xg[:, :, :], 0.0).then_inc(xg_cleared, 1)
            pool.wait_ge(xg_cleared, 1)
            pool.wait_ge(h2_stored[0], 48)
            pool.wait_ge(h2_stored[1], 32)
            def gather_rows(i):
                pool.wait_ge(idx_ready, i + 1)
                if i >= 2:
                    pool.wait_ge(xg_transposed, i - 1)
                pool.indirect_dma_start(
                    out=xg[:, i % 2, :], out_offset=None, in_=h2_dram,
                    in_offset=bass.IndirectOffsetOnAxis(ap=idx[:, i % 2:i % 2 + 1], axis=0),
                    bounds_check=T - 1, oob_is_err=False).then_inc(xg_loaded[i % 2], 16)

            for i in range(E):
                gather_rows(i)
            pool.wait_ge(wslots_ready, 1)
            pool.wait_ge(y_stored, 16 * (E - 1))
            for t in GATHER_ORDER:
                n = rows(t)
                for c, dst in ((0, y1), (1, y2)):
                    pool.indirect_dma_start(
                        out=dst[t][0:n, :], out_offset=None, in_=y_dram,
                        in_offset=bass.IndirectOffsetOnAxis(ap=yslot[0:n, c, t:t + 1], axis=0),
                        bounds_check=NSLOT - 1, oob_is_err=False).then_inc(y_gathered[t], 16)
            pool.wait_ge(xg_transposed, E)
            n_ov = pool.value_load(ctl[0:1, MAXOV:MAXOV + 1], min_val=0, max_val=MAXOV)
            with pool.If(n_ov > 0):
                with pool.Fori(0, MAXOV) as j:
                    with pool.If(j < n_ov):
                        pool.wait_ge(ov_idx_ready, j + 1)
                        pool.sem_inc(ov_gather_begun, 1)
                        pool.indirect_dma_start(
                            out=xg[:, 0, :], out_offset=None, in_=h2_dram,
                            in_offset=bass.IndirectOffsetOnAxis(ap=idx[:, 0:1], axis=0),
                            bounds_check=T - 1, oob_is_err=False).then_inc(ov_gathered, 16)
                    pool.nop()
            pool.wait_ge(last_onehot, 1)
            for j, t in enumerate(POOL_TILES):
                n = rows(t)
                pool.wait_ge(weighted, j + 1)
                step(pool.tensor_tensor(y1[t][0:n, :], y1[t][0:n, :], y2[t][0:n, :], ALU.add))
                pool.tensor_tensor(y1[t][0:n, :], y1[t][0:n, :], x2[0:n, t, :], ALU.add).then_inc(combined_by_pool, 1)
            pool.wait_ge(gfin_loaded, 16)
            for t in ACT_OWN:
                pool.wait_ge(acc_ready, t + 1)
                pool.tensor_tensor(y2[t][:, :], y1[t][:, :], gfin, ALU.mult).then_inc(gained_by_pool, 1)
            pool.wait_ge(v_stored, 16 * NT)
            pool.wait_ge(k_stored, 16 * NT)
            pool.wait_ge(state_stored, 32)

        @block.tensor
        def _(pe):
            def transpose_x(t):
                n = rows(t)
                pe.wait_ge(xn_ready, t + 1)
                if t == 0:
                    pe.wait_ge(consts_made, 1)
                if t >= 2:
                    pe.wait_ge(hT_ready, t - 1)
                src = xn[0:n, t % 2, :].rearrange("p (q k) -> p k q", k=KC)
                for k in range(KC):
                    o = ps[:, 2 * (t % 2) + k // 4, (k % 4) * P:(k % 4) * P + n]
                    ins = pe.transpose(o, src[:, k, :], ident[0:n, 0:n])
                ins.then_inc(x_transposed, 1)

            def three_passes(out, lhs_hi, lhs_lo, rhs_hi, rhs_lo, first, last):
                pe.matmul(out, lhs_hi, rhs_hi, start=first, stop=False)
                pe.matmul(out, lhs_hi, rhs_lo, start=False, stop=False)
                return pe.matmul(out, lhs_lo, rhs_hi, start=False, stop=last)

            def project_v(t):
                n = rows(t)
                pe.wait_ge(hT_ready, t + 1)
                if t >= 2:
                    pe.wait_ge(v_evac, t - 1)
                for k in range(KC):
                    if t == 0 and k < KC - V_POOL:
                        pe.wait_ge(w_lo_ready, k + 1)
                    elif t == 0:
                        pe.wait_ge(w_lo_by_pool, k - (KC - V_POOL) + 1)
                    ins = three_passes(ps[0:n, 4 + t % 2, :], hT_hi[:, k, t * P:t * P + n], hT_lo[:, k, t * P:t * P + n],
                                       w_in_hi[1][:, k, :], w_in_lo[1][:, k, :], k == 0, k == KC - 1)
                ins.then_inc(v_full, 1)

            def project_columns(bank, buf, k, c, half):
                t, c = slice(half * HALF, (half + 1) * HALF), slice(c * P, (c + 1) * P)
                return three_passes(ps[:, bank, 0:HALF], w_in_hi[buf][:, k, c], w_in_lo[buf][:, k, c],
                                    hT_hi[:, k, t], hT_lo[:, k, t], k == 0, k == KC - 1)

            def project_head(j):
                pe.wait_ge(w_lo_ready, KC - V_POOL + j + 1)
                if j == 1:
                    pe.wait_ge(v_evac, NT)
                if j >= 2:
                    pe.wait_ge(qk_evac_act, j - 1)
                    pe.wait_ge(qk_evac_dve, j - 1)
                for half in range(2):
                    for k in range(KC):
                        ins = project_columns(6 - 2 * (j % 2) + half, j // H, k, j % H, half)
                ins.then_inc(qk_full, 1)

            transpose_x(0)
            transpose_x(1)
            for t in range(NT):
                project_v(t)
                if t + 2 < NT:
                    transpose_x(t + 2)
            for j in range(H):
                project_head(j)
            project_head(H)
            pe.wait_ge(qk_evac_act, H)
            pe.wait_ge(qk_evac_dve, H)
            pe.wait_ge(hT_ready, NT)
            for t in range(NT):
                n = rows(t)
                if t == 4:
                    pe.wait_ge(ktok_evac, 1)
                for h in range(H):
                    ins = pe.transpose(ps[0:n, t % 4, h * P:(h + 1) * P], kT[:, h, t * P:t * P + n], ident[:, :])
                ins.then_inc(ktok_full, 1)
            pe.wait_ge(cache_loaded, 48)
            for c in range(2):
                pe.wait_ge(ktok_evac, 2 + c)
                for h in range(2):
                    for t in range(2):
                        ins = pe.transpose(ps[:, 1 + c, (2 * h + t) * P:(2 * h + t + 1) * P],
                                           kc_raw[:, t, (2 * c + h) * P:(2 * c + h + 1) * P], ident[:, :])
                ins.then_inc(kc_full, 1)
            pe.wait_ge(ktok_evac, 4)
            for g in range(H):
                ins = pe.transpose(ps[:, 3, g * HIST:(g + 1) * HIST], hist_in[:, g * P:(g + 1) * P],
                                   ident[0:HIST, 0:HIST])
            ins.then_inc(hist_full, 1)
            for j in range(H + 1, 2 * H - 1):
                project_head(j)

            pe.wait_ge(qk_evac_act, H + 2)
            pe.wait_ge(qk_evac_dve, H + 2)
            pe.wait_ge(kc_evac, 2)
            pe.wait_ge(ktok_evac, NT)
            pe.wait_ge(hist_evac, 1)

            def scores(n):
                t, h = divmod(n, H)
                b = 2 * (n % 2)
                if n >= 2:
                    pe.wait_ge(exp_done, n - 1)
                for c in range(2):
                    r = slice(c * HD, (c + 1) * HD)
                    q = qT[r, h, t * P:t * P + rows(t)]
                    if t < PT:
                        ins = pe.matmul(ps[:, b + c, 0:(t + 1) * P], q, kT[r, h, 0:(t + 1) * P], start=True, stop=True)
                    else:
                        pe.matmul(ps[0:N_SAMPLE, b + c, 0:PAST], q, kcT[r, h, :], start=True, stop=True)
                        ins = pe.matmul(ps[0:N_SAMPLE, b + c, PAST:PAST + N_SAMPLE], q, kT[r, h, N_PROMPT:T],
                                        start=True, stop=True)
                ins.then_inc(scores_full, 1)

            def key_tiles(t):
                return [(k, P) for k in range(t + 1)] if t < PT else [(0, P), (1, P), (2, N_SAMPLE)]

            def transpose_a(n):
                t, h = divmod(n, H)
                m = rows(t)
                pe.wait_ge(a_ready, n + 1)
                if n >= 1:
                    pe.wait_ge(aT_evac, n)
                for k, keys in key_tiles(t):
                    ins = pe.transpose(ps[0:keys, 4, k * P:k * P + m], prob[0:m, n % 2, 0, k * P:k * P + keys],
                                       ident[0:m, 0:m])
                ins.then_inc(aT_full, 1)

            def weighted_values(n):
                t, h = divmod(n, H)
                m = rows(t)
                pe.wait_ge(aT_evac, n + 1)
                if n == UNITS - H:
                    pe.wait_ge(cache_loaded, 48)
                if h == 0 and t >= 2:
                    pe.wait_ge(oT_evac, t - 1)
                tiles = key_tiles(t)
                for k, keys in tiles:
                    v = (v_pr if t < PT else v_sa)[0:keys, k, h * VD:(h + 1) * VD]
                    ins = pe.matmul(ps[0:m, 5 + 2 * (t % 2), h * VD:(h + 1) * VD], aT[0:keys, n % 2, k * P:k * P + m], v,
                                    start=(k == 0), stop=(k == len(tiles) - 1))
                ins.then_inc(pv_done, 1)

            def transpose_o(t):
                m = rows(t)
                pe.wait_ge(o_ready, t + 1)
                for h in range(H):
                    ins = pe.transpose(ps[:, 5 + 2 * (t % 2), h * P:h * P + m], otok[0:m, h * VD:(h + 1) * VD], ident[0:m, 0:m])
                ins.then_inc(oT_full, 1)

            def project_u(n, part):
                if n >= 4 * H:
                    return
                blk = n // 2
                g, half = divmod(blk, 2)
                for k in range(4 * (n % 2) + 2 * part, 4 * (n % 2) + 2 * part + 2):
                    if k == 0 and half == 0:
                        pe.wait_ge(w_lo_ready, KC - V_POOL + 2 * H + g + 1)
                    if k == 0 and blk >= 1:
                        pe.wait_ge(u_evac_act, blk)
                    ins = project_columns(6, 0, k, g, half)
                    if k == KC - 1:
                        ins.then_inc(u_full, 1)

            scores(0)
            scores(1)
            project_head(2 * H - 1)
            pe.wait_ge(qk_evac_act, 2 * H - 1)
            project_u(0, 0)
            project_u(0, 1)
            pe.wait_ge(qk_evac_act, 2 * H)
            pe.wait_ge(qk_evac_dve, 2 * H)
            for n in range(UNITS):
                if n + 2 < UNITS:
                    scores(n + 2)
                if n >= 1:
                    project_u(n, 0)
                if n >= 1:
                    weighted_values(n - 1)
                if n >= 7 and n % H == H - 1:
                    transpose_o(n // H - 1)
                transpose_a(n)
                if n >= 1:
                    project_u(n, 1)
            weighted_values(UNITS - 1)

            pe.wait_ge(exp_done, UNITS)
            pe.wait_ge(aT_evac, UNITS)
            pe.wait_ge(w_pool_loaded, 32)
            for g in range(H):
                pe.wait_ge(diff_ready, g + 1)
                pe.matmul(ps[:, g, :], w_pool_sb[:, g, :], mixT[:, g, 0:N_PROMPT], start=True, stop=True).then_inc(pool_full, 1)
                ins = pe.matmul(ps[:, 4, g * N_SAMPLE:(g + 1) * N_SAMPLE], w_pool_sb[:, g, :],
                                mixT[:, g, N_PROMPT:T], start=True, stop=True)
            ins.then_inc(pool_full, 1)
            pe.wait_ge(u_evac_act, 2 * H)
            pe.wait_ge(oT_evac, NT - 1)
            for b in range(2):
                for g in range(H):
                    ins = pe.transpose(ps[0:HIST, 6 + b, g * P:(g + 1) * P], ustate[:, b, g, :], ident[:, :])
            ins.then_inc(state_full, 1)

            def project_out(t, half, features):
                n = rows(t)
                for f in features:
                    if t == 0 and half == 0:
                        pe.wait_ge(*((w_out_lo_by_pool, f - H + 1) if f >= H else (w_out_lo_ready, f + 1)))
                    if f == H and half == 0:
                        pe.wait_ge(oT_evac, t + 1)
                        if t >= 2:
                            pe.wait_ge(x2_ready, 2 * (t - 1))
                    if t == 0 and half == 0:
                        pe.wait_ge(pool_evac, 2 if f >= H else H)
                    if t == 1 and half == 0 and f == H:
                        pe.wait_ge(pool_evac, H)
                    if f < H and t == 0 and half == 0:
                        pe.wait_ge(pool_evac_sample, 1)
                    h = slice(half * 512, (half + 1) * 512)
                    ins = three_passes(ps[0:n, 2 * (t % 2) + half, :],
                                       mix_hi[:, f, t * P:t * P + n], mix_lo[f][:, t * P:t * P + n],
                                       w_out_hi[f][:, h], w_out_lo[:, f, h], f == H, f == H - 1)
                if features[-1] == H - 1:
                    ins.then_inc(op_full, 1)

            def transpose_h2(t):
                n = rows(t)
                pe.wait_ge(h2n_ready, t + 1)
                if t == 0:
                    pe.wait_ge(oT_evac, NT)
                if t >= 1:
                    pe.wait_ge(h2T_dve, t)
                    pe.wait_ge(h2T_act, t)
                src = h2n[0:n, t % 2, :].rearrange("p (q k) -> p k q", k=KC)
                for k in range(KC):
                    ins = pe.transpose(ps[:, 4 + k // 4, (k % 4) * P:(k % 4) * P + n], src[:, k, :], ident[0:n, 0:n])
                ins.then_inc(h2_transposed, 1)

            def router_logits(t, chunks=range(KC)):
                pe.wait_ge(h2T_dve, t + 1)
                pe.wait_ge(h2T_act, t + 1)
                if t == 0:
                    pe.wait_ge(wr_scaled, 1)
                    pe.wait_ge(state_evac, 1)
                n = rows(t)
                for k in chunks:
                    ins = pe.matmul(ps[0:n, 6, t * NL:(t + 1) * NL], h2T[:, k, 0:n], wr[:, k, :],
                                    start=(k == 0), stop=(k == KC - 1))
                if chunks[-1] == KC - 1:
                    ins.then_inc(router_done, 1)

            heads, pools = range(H, 2 * H), range(H)
            for f in (heads, pools):
                for t in range(2):
                    project_out(t, 0, f)
                    project_out(t, 1, f)
                    if t == 1 and f is heads:
                        transpose_o(NT - 1)
            transpose_h2(0)
            for t in range(2, NT):
                project_out(t, 0, (*heads, *pools))
                router_logits(t - 2)
                project_out(t, 1, (*heads, *pools))
                transpose_h2(t - 1)
            router_logits(NT - 2, range(KC - 1))
            transpose_h2(NT - 1)
            router_logits(NT - 2, range(KC - 1, KC))
            router_logits(NT - 1)

            pe.wait_ge(mask_ready, 1)
            pe.matmul(ps[:, 5, 0:(NT + 1) * E], tri[:, :], msum_b.rearrange("p t e -> p (t e)"), start=True, stop=False)
            for t in range(NT):
                ins = pe.matmul(ps[:, 5, (t + 1) * E:(NT + 1) * E].rearrange("p (t e) -> p t e", e=E), ones[:, :],
                                msum_b[:, t, :].unsqueeze(1).to_broadcast([P, NT - t, E]), start=False, stop=(t == NT - 1))
            ins.then_inc(rank_full, 1)

            def slot_tokens(b, signal):
                for t in range(NT):
                    ins = pe.matmul(ps[:, 6 + b, 0:2], onehot_all[:, b, t, :], tokv[:, t, :], start=(t == 0), stop=(t == NT - 1))
                ins.then_inc(signal, 1)

            def transpose_rows(b, signal):
                src = xg[:, b, :].rearrange("p (q k) -> p k q", k=KC)
                for k in range(KC):
                    ins = pe.transpose(ps[:, k // 4, (k % 4) * P:(k % 4 + 1) * P], src[:, k, :], ident[:, :])
                ins.then_inc(signal, 1)

            def gate_up(slot, b, gate_signal, up_signal):
                for w, bank, signal in ((wg_sb[slot], 2, gate_signal), (wu_sb[slot], 3, up_signal)):
                    for c in range(FC):
                        for k in range(KC):
                            ins = pe.matmul(ps[:, bank, c * P:(c + 1) * P], w[:, k, c * P:(c + 1) * P],
                                            xT[:, b, k, :], start=(k == 0), stop=(k == KC - 1))
                    if signal is not None:
                        ins.then_inc(signal, 1)

            def down(slot, b, signal):
                for half in range(2):
                    for c in range(FC):
                        ins = pe.matmul(ps[:, 4 + half, :], heT[:, b, c, :], wd_sb[slot][:, c, half * 512:(half + 1) * 512],
                                        start=(c == 0), stop=(c == FC - 1))
                ins.then_inc(signal, 1)

            for i in range(2):
                pe.wait_ge(onehot_ready, i + 1)
                slot_tokens(i, idx_full)
            pe.wait_ge(x2_ready, NT)
            pe.wait_ge(xg_loaded[0], 16)
            transpose_rows(0, xg_transposed)
            def expert(it, u, left):
                i = it * RING + u
                b = u % 2
                if left is None or left >= 2:
                    pe.wait_ge(onehot_ready, i + 3)
                    pe.wait_ge(idx_ready, i + 1)
                    slot_tokens(b, idx_full)
                pe.wait_ge(xT_dve, i + 1)
                pe.wait_ge(xT_act, i + 1)
                pe.wait_ge(ring_loaded[u], it * 48 + 48)
                gate_up(u, b, gate_full, up_full)
                if left is None or left >= 1:
                    pe.wait_ge(xg_loaded[1 - b], it * (8 * RING) + 16 * ((u + 1) // 2 + 1))
                    transpose_rows(1 - b, xg_transposed)
                pe.wait_ge(he_ready, i + 1)
                pe.wait_ge(y_evac_act, i + 1)
                pe.wait_ge(y_evac_dve, i + 1)
                down(u, b, down_done)

            with pe.Fori(0, E // RING - 1) as it:
                for u in range(RING):
                    expert(it, u, None)
            for u in range(RING):
                expert(E // RING - 1, u, RING - 1 - u)

            n_ov = pe.value_load(ctl[0:1, MAXOV:MAXOV + 1], min_val=0, max_val=MAXOV)
            pe.wait_ge(idx_ready, E)
            pe.wait_ge(xT_dve, E)
            pe.wait_ge(xT_act, E)
            pe.wait_ge(y_evac_act, E + 1)
            pe.wait_ge(y_evac_dve, E + 1)
            with pe.If(n_ov > 0):
                with pe.Fori(0, MAXOV) as j:
                    with pe.If(j < n_ov):
                        pe.wait_ge(ov_onehot, j + 1)
                        for c in range(2):
                            for t in range(NT):
                                ins = pe.matmul(ps[:, 6, 0:2], onehot_all[:, c, t, :], tokv[:, t, :],
                                                start=(c == 0 and t == 0), stop=(c == 1 and t == NT - 1))
                        ins.then_inc(ov_idx_full, 1)
                        pe.wait_ge(ov_gathered, j * 16 + 16)
                        transpose_rows(0, ov_transposed)
                        pe.wait_ge(ov_xT_ready, j + 1)
                        pe.wait_ge(ov_w_loaded, j * 48 + 48)
                        gate_up(RING - 1, 0, None, ov_gate_full)
                        pe.wait_ge(ov_he_ready, j + 1)
                        down(RING - 1, 0, ov_down_done)
                        pe.wait_ge(ov_y_ready, j + 1)
                        for t in range(NT):
                            if t >= 2:
                                pe.wait_ge(ov_added, j * NT + (t - 1))
                            for half in range(2):
                                ins = pe.matmul(ps[0:rows(t), 4 - 2 * (t % 2) + half, :], slot_to_token[:, t, 0:rows(t)],
                                                yst[:, 0, half * 512:(half + 1) * 512], start=True, stop=True)
                            ins.then_inc(ov_combine_full, 1)
                    pe.nop()

            pe.wait_ge(last_onehot, 1)
            for t in range(NT):
                if t >= 3:
                    pe.wait_ge(acc_ready, t - 2)
                for half in range(2):
                    ins = pe.matmul(ps[0:rows(t), 4 - 2 * (t % 3) + half, :], slot_to_token[:, t, 0:rows(t)],
                                    yst[:, (E - 1) % 2, half * 512:(half + 1) * 512], start=True, stop=True)
                ins.then_inc(last_full, 1)

        @block.scalar
        def _(act):
            def square_x(t):
                n = rows(t)
                act.wait_ge(x_loaded[t % 2], 16 * (t // 2 + 1))
                if t >= 2:
                    act.wait_ge(x_transposed, t - 1)
                act.activation(xn[0:n, t % 2, :], xraw[0:n, t % 2, :], ACT.Square,
                               accum_out=ss[0:n, t:t + 1]).then_inc(x_squared, 1)

            def row_root(t):
                n = rows(t)
                act.activation(rs[0:n, 0, t:t + 1], ss[0:n, t:t + 1], ACT.Sqrt, scale=1.0 / D,
                               bias=eps_col[0:n, 0:1]).then_inc(root_ready, 1)

            def root_x(t):
                act.wait_ge(x_squared, t + 1)
                row_root(t)

            def scale_x(t):
                n = rows(t)
                act.wait_ge(x_scale_ready, t + 1)
                act.activation(xn[0:n, t % 2, :], xraw[0:n, t % 2, :], ACT.Copy, scale=rs[0:n, 0, t:t + 1]).then_inc(xn_ready, 1)

            def hT_his(t):
                n = rows(t)
                act.wait_ge(x_transposed, t + 1)
                if t == 0:
                    act.wait_ge(gmix_loaded, 16)
                for k in range(KC):
                    act.activation(hT_hi[:, k, t * P:t * P + n], ps[:, 2 * (t % 2) + k // 4, (k % 4) * P:(k % 4) * P + n],
                                   ACT.Copy, scale=gmix_sb[:, k:k + 1]).then_inc(hT_act, 1)

            def v_out(t):
                n = rows(t)
                act.wait_ge(v_full, t + 1)
                dst = v_pr[:, t, :] if t < PT else v_sa[0:N_SAMPLE, 2, :]
                act.copy(dst, ps[0:n, 4 + t % 2, :]).then_inc(v_evac, 1)

            def w_in_his(j, chunks=None):
                buf = 1 - j % 2
                for c in chunks or range(KC if j == 0 else H):
                    part = (slice(None), c, slice(None)) if j == 0 else (slice(None), slice(None), slice(c * P, (c + 1) * P))
                    if j == 0:
                        act.wait_ge(w_v_loaded[c // 2], 16)
                    elif c == 0:
                        act.wait_ge(w_in_loaded[j - 1], 16)
                    elif c == 2 and j == 2:
                        act.wait_ge(w_q_loaded, 16)
                    act.copy(w_in_hi[buf][part], w_in_sb[buf][part]).then_inc(w_hi_ready, 1)

            act.wait_ge(consts_made, 1)
            act.activation(warm[:, :], ones[:, 0:1], ACT.Sqrt)
            for t in range(2):
                square_x(t)
                root_x(t)
            for t in range(2):
                scale_x(t)
            w_in_his(0, range(V_EARLY))
            hT_his(0)
            w_in_his(0, range(V_EARLY, KC))
            for t in range(NT):
                if t + 1 < NT:
                    hT_his(t + 1)
                if t + 2 < NT:
                    square_x(t + 2)
                    root_x(t + 2)
                    scale_x(t + 2)
                if t == NT - 1:
                    w_in_his(1)
                v_out(t)

            def head_out(j):
                act.wait_ge(qk_full, j + 1)
                out = ps[:, 6 - 2 * (j % 2), 0:HALF]
                if j < H:
                    act.copy(kT[:, j, 0:HALF], out).then_inc(qk_evac_act, 1)
                else:
                    act.activation(qT[:, j - H, 0:HALF], out, ACT.Copy, scale=-SCALE).then_inc(qk_evac_act, 1)

            w_in_his(2)
            for j in range(H + 1):
                head_out(j)
            act.wait_ge(lam_dots, 1)
            act.activation(lam_t[:, 2:4], lam_t[:, 0:2], ACT.Exp).then_inc(lam_exp, 1)
            for c in range(2):
                act.wait_ge(kc_full, c + 1)
                act.copy(kcT[:, 2 * c:2 * c + 2, :], ps[:, 1 + c, :].rearrange("p (h t) -> p h t", h=2)).then_inc(kc_evac, 1)
            w_in_his(3)
            for j in range(H + 1, 2 * H):
                head_out(j)

            def w_out_his(c):
                f = (c + H) % KC
                if c == 0:
                    act.wait_ge(x_transposed, NT)
                if c == H:
                    act.wait_ge(aT_full, UNITS)
                if c == H + 2:
                    act.wait_ge(diff_ready, H)
                if c % H == 0:
                    act.wait_ge(w_out_loaded[f // H], 16)
                act.copy(w_out_hi[f], w_out_sb[:, f, :]).then_inc(w_out_hi_ready, 1)

            def exps(n):
                t, h = divmod(n, H)
                m, w = rows(t), (t + 1) * P if t < PT else PAST + N_SAMPLE
                act.wait_ge(negm_ready, n + 1)
                if n >= 2:
                    act.wait_ge(aT_full, n - 1)
                for c in range(2):
                    ins = act.activation(prob[0:m, n % 2, c, 0:w], ps[0:m, 2 * (n % 2) + c, 0:w], ACT.Exp,
                                         bias=negm[0:m, n % 2, c:c + 1], scale=-1.0,
                                         accum_out=psums[0:m, t, h, c:c + 1])
                ins.then_inc(exp_done, 1)

            def aT_out(n):
                t, h = divmod(n, H)
                act.wait_ge(aT_full, n + 1)
                if n >= 2:
                    act.wait_ge(pv_done, n - 1)
                if t < PT:
                    w = (t + 1) * P
                    act.copy(aT[:, n % 2, 0:w], ps[:, 4, 0:w]).then_inc(aT_evac, 1)
                else:
                    two = lambda a: a.rearrange("p (k q) -> p k q", k=2)[:, :, 0:N_SAMPLE]
                    act.copy(two(aT[:, n % 2, 0:2 * P]), two(ps[:, 4, 0:2 * P]))
                    act.copy(aT[0:N_SAMPLE, n % 2, 2 * P:2 * P + N_SAMPLE],
                             ps[0:N_SAMPLE, 4, 2 * P:2 * P + N_SAMPLE]).then_inc(aT_evac, 1)

            def o_squares(t):
                m = rows(t)
                act.wait_ge(pv_done, H * (t + 1))
                if t >= 1:
                    act.wait_ge(oT_full, t)
                for h in range(H):
                    ins = act.activation(otok[0:m, h * VD:(h + 1) * VD], ps[0:m, 5 + 2 * (t % 2), h * VD:(h + 1) * VD], ACT.Square,
                                         accum_out=oss[0:m, t, h:h + 1])
                ins.then_inc(o_squared, 1)

            def u_out(blk):
                g, half = divmod(blk, 2)
                u = uext[:, g % 2, :]
                act.wait_ge(u_full, blk + 1)
                if half == 0:
                    if g >= 2:
                        act.wait_ge(u_summed, g - 1)
                        act.wait_ge(diff_ready, g - 1)
                    elif g == 0:
                        act.wait_ge(xn_ready, NT)
                    act.copy(u[:, HIST:HIST + T // 2], ps[:, 6, 0:T // 2]).then_inc(u_evac_act, 1)
                else:
                    n = N_PROMPT - T // 2
                    act.copy(u[:, HIST + T // 2:HIST + N_PROMPT], ps[:, 6, 0:n])
                    act.copy(u[:, S0:EXT], ps[:, 6, n:T // 2]).then_inc(u_evac_act, 1)

            exps(0)
            for n in range(UNITS):
                if n % 2 == 0 and 2 <= n <= 4 * H:
                    u_out(n // 2 - 1)
                if n + 1 < UNITS:
                    exps(n + 1)
                if n % H == 1 and n >= H:
                    o_squares(n // H - 1)
                aT_out(n)
                if 2 * H <= n < 4 * H and n % 2 == 0:
                    w_out_his((n - 2 * H) // 2)
            for c in range(H, 2 * H):
                w_out_his(c)
            for g in range(H):
                act.wait_ge(pool_full, g + 1)
                act.activation(mix_hi[:, g, 0:N_PROMPT], ps[:, g, :], ACT.Copy, scale=pscale[:, g:g + 1]).then_inc(pool_hi_ready, 1)
            o_squares(NT - 1)

            def h2_square(t):
                n = rows(t)
                if t >= 2:
                    act.wait_ge(h2_transposed, t - 1)
                    act.wait_ge(h2_stored[t % 2], 16 * (t // 2))
                for half in range(2):
                    act.wait_ge(x2_ready, 2 * t + half + 1)
                    c = slice(half * 512, (half + 1) * 512)
                    act.activation(h2n[0:n, t % 2, c], x2[0:n, t, c], ACT.Square,
                                   accum_out=ss2[0:n, half, t:t + 1]).then_inc(x2_squared, 1)

            def h2T_evac(t):
                act.wait_ge(h2_transposed, t + 1)
                if t >= 1:
                    act.wait_ge(router_done, t)
                n = rows(t)
                act.copy(h2T[:, 4:KC, 0:n], ps[:, 5, :].rearrange("p (k t) -> p k t", k=4)[:, :, 0:n]).then_inc(h2T_act, 1)

            act.activation(warm[:, :], ones[:, 0:1], ACT.Sqrt)
            act.wait_ge(consts_loaded, 80)
            act.wait_ge(pv_done, UNITS)
            act.wait_ge(v_stored, 16 * NT)
            for t in range(NT):
                h2_square(t)
                if t == NT - 1:
                    h2T_evac(t - 1)
                act.wait_ge(x2_sum_ready, t + 1)
                row_root(t)
                if 1 <= t < NT - 1:
                    h2T_evac(t - 1)
            act.activation(warm[:, :], ones[:, 0:1], ACT.Exp)
            h2T_evac(NT - 1)

            act.wait_ge(gate_in, 1)
            act.activation(gex, gex, ACT.Exp).then_inc(gate_exp, 1)
            act.wait_ge(gate_in, 2)
            act.activation(rt1[:, 3, :], rt1[:, 3, :], ACT.Exp).then_inc(gate_exp, 1)
            act.activation(warm[:, :], gmix_sb[:, 0:1], ACT.Silu)

            def rows_out(b, k):
                return act.activation(xT[:, b, k, :], ps[:, 1, (k - 4) * P:(k - 3) * P], ACT.Copy, scale=gffn_sb[:, k:k + 1])

            act.wait_ge(h2T_dve, NT)
            act.sem_inc(y_evac_act, 1)
            act.wait_ge(xg_transposed, 1)
            for k in range(4, KC):
                ins = rows_out(0, k)
            ins.then_inc(xT_act, 1)
            act.wait_ge(routed, 1)
            def expert(it, u, left):
                i = it * RING + u
                b = u % 2
                act.wait_ge(gate_full, i + 1)
                act.activation(gact[:, b], ps[:, 2, 0:FE].rearrange("p (c s) -> p c s", c=FC),
                               ACT.Silu).then_inc(gact_ready, 1)
                if left is None or left >= 1:
                    act.wait_ge(xg_transposed, i + 2)
                    for k in range(4, KC):
                        ins = rows_out(1 - b, k)
                    ins.then_inc(xT_act, 1)
                act.wait_ge(down_done, i + 1)
                act.wait_ge(yst_free, i + 1)
                act.copy(yst[:, b, 0:512], ps[:, 4, :]).then_inc(y_evac_act, 1)

            with act.Fori(0, E // RING - 1) as it:
                for u in range(RING):
                    expert(it, u, None)
            for u in range(RING):
                expert(E // RING - 1, u, RING - 1 - u)
            n_ov = act.value_load(ctl[0:1, MAXOV:MAXOV + 1], min_val=0, max_val=MAXOV)
            with act.If(n_ov > 0):
                with act.Fori(0, MAXOV) as j:
                    with act.If(j < n_ov):
                        act.wait_ge(ov_gate_full, j + 1)
                        act.activation(gact[:, 0], ps[:, 2, 0:FE].rearrange("p (c s) -> p c s", c=FC),
                                       ACT.Silu).then_inc(ov_gact_ready, 1)
                    act.nop()
            def weigh(t):
                n = rows(t)
                act.wait_ge(y_gathered[t], 32)
                act.activation(y1[t][0:n, :], y1[t][0:n, :], ACT.Copy, scale=wmain[0:n, 0, t:t + 1])
                act.activation(y2[t][0:n, :], y2[t][0:n, :], ACT.Copy, scale=wmain[0:n, 1, t:t + 1]).then_inc(weighted, 1)

            def square_acc(t):
                n = rows(t)
                act.wait_ge(acc_ready, t + 1)
                act.activation(x2[0:n, t, :], y1[t][0:n, :], ACT.Square, accum_out=ss[0:n, t:t + 1]).then_inc(acc_squared, 1)

            def root(tiles):
                c = slice(tiles[0], tiles[-1] + 1)
                act.wait_ge(acc_squared, tiles[-1] + 1)
                act.activation(rs[:, 0, c], ss[:, c], ACT.Sqrt, scale=1.0 / D, bias=eps_col[:, 0:1]).then_inc(root_ready, 1)

            def scale_out(t):
                n = rows(t)
                act.activation(y2[t][0:n, :], y2[t][0:n, :], ACT.Copy, scale=rs[0:n, 0, t:t + 1]).then_inc(out_by_act, 1)

            act.activation(warm[:, :], ones[:, 0:1], ACT.Sqrt)
            for t in POOL_TILES:
                weigh(t)
            for t in OWN_TILES:
                square_acc(t)
            root(OWN_TILES)
            act.wait_ge(factors_ready, 1)
            for k, t in enumerate(ACT_OWN):
                act.wait_ge(gained_by_pool, k + 1)
                scale_out(t)
                square_acc(POOL_TILES[k])
            root(POOL_TILES)
            act.wait_ge(factors_ready, 2)
            act.wait_ge(gained_by_dve, 1)
            scale_out(ACT_LATE)

        @block.vector
        def _(dve):
            steps = [0]

            def step(ins):
                steps[0] += 1
                ins.then_inc(dve_step, 1)
                dve.wait_ge(dve_step, steps[0])

            def wide(a, shape):
                return a.unsqueeze(len(a.shape)).to_broadcast(shape)

            def root_guess(y, m, tmp, half):
                dve.tensor_scalar(half, m, -0.5, None, ALU.mult)
                step(dve.tensor_scalar(tmp.bitcast(I32), m.bitcast(I32), 1, None, ALU.arith_shift_right))
                step(dve.tensor_scalar(y.bitcast(I32), tmp.bitcast(I32), -1.0, float(0x5F3759DF), ALU.mult, ALU.add))

            def root_step(y, tmp, half, signal=None):
                if half.shape[-1] == 1:
                    step(dve.scalar_tensor_tensor(tmp, y, half, y, ALU.mult, ALU.mult))
                else:
                    step(dve.tensor_tensor(tmp, y, y, ALU.mult))
                    step(dve.tensor_tensor(tmp, tmp, half, ALU.mult))
                last = dve.scalar_tensor_tensor(y, tmp, 1.5, y, ALU.add, ALU.mult)
                if signal is None:
                    step(last)
                else:
                    last.then_inc(signal, 1)

            def refine_root(y, tmp, half, signal=None):
                step(dve.reciprocal(y, y))
                root_step(y, tmp, half, signal)

            def row_scale(t, roots, signal=None):
                n = rows(t)
                m, y, tmp, half = (rs[0:n, 1, t:t + 1], rs[0:n, 0, t:t + 1], rs[0:n, 2, t:t + 1], ovoff[0:n, t:t + 1])
                step(dve.tensor_scalar(m, ss[0:n, t:t + 1], 1.0 / D, EPS, ALU.mult, ALU.add))
                step(dve.tensor_scalar(half, m, -0.5, None, ALU.mult))
                dve.wait_ge(root_ready, roots)
                refine_root(y, tmp, half, signal)
                return y

            def hT_evac(t):
                n = rows(t)
                cols = slice(t * P, t * P + n)
                dve.wait_ge(x_transposed, t + 1)
                if t == 0:
                    dve.wait_ge(gmix_loaded, 16)
                for k in range(KC):
                    if k % 4 == 0:
                        dve.wait_ge(hT_act, KC * t + k + 4)
                    ins = dve.scalar_tensor_tensor(hT_lo[:, k, cols], ps[:, 2 * (t % 2) + k // 4, (k % 4) * P:(k % 4) * P + n],
                                                   gmix_sb[:, k:k + 1], hT_hi[:, k, cols].bitcast(F32), ALU.mult, ALU.subtract)
                ins.then_inc(hT_ready, 1)

            def w_in_los(j, first, last):
                buf = 1 - j % 2
                for c in range(first, last):
                    part = (slice(None), c, slice(None)) if j == 0 else (slice(None), slice(None), slice(c * P, (c + 1) * P))
                    dve.wait_ge(w_hi_ready, c + 1 if j == 0 else KC + (j - 1) * H + c + 1)
                    dve.tensor_tensor(w_in_lo[buf][part], w_in_sb[buf][part], w_in_hi[buf][part].bitcast(F32),
                                      ALU.subtract).then_inc(w_lo_ready, 1)

            def w_out_los(c):
                f = (c + H) % KC
                dve.wait_ge(w_out_hi_ready, c + 1)
                dve.tensor_tensor(w_out_lo[:, f, :], w_out_sb[:, f, :], w_out_hi[f].bitcast(F32),
                                  ALU.subtract).then_inc(w_out_lo_ready, 1)

            def x_scale(t):
                dve.wait_ge(x_squared, t + 1)
                row_scale(t, t + 1, x_scale_ready)

            x_scale(0)
            x_scale(1)
            w_in_los(0, 0, V_EARLY)
            hT_evac(0)
            w_in_los(0, V_EARLY, KC - V_POOL)
            for t in range(1, NT):
                if t + 1 < NT:
                    x_scale(t + 1)
                hT_evac(t)
            w_in_los(1, 0, H)

            dve.wait_ge(lam_loaded, 64)
            step(dve.tensor_tensor(lam_in[:, 0:2, :], lam_in[:, 0:2, :], lam_in[:, 2:4, :], ALU.mult))
            dve.tensor_reduce(lam_t[:, 0:2], lam_in[:, 0:2, :], X, ALU.add).then_inc(lam_dots, 1)
            dve.wait_ge(consts_made, 2)
            step(dve.reciprocal(inv_cnt[:, :], inv_cnt[:, :]))
            dve.wait_ge(gsub_loaded, 16)
            step(dve.tensor_scalar(gsub[:, :], gsub[:, :], 1.0 - LAMBDA_INIT, None, ALU.mult))

            def head_out(j):
                dve.wait_ge(qk_full, j + 1)
                dst = (kT if j < H else qT)[:, j % H, HALF:T]
                dve.tensor_scalar(dst, ps[:, 7 - 2 * (j % 2), 0:HALF], 1.0 if j < H else -SCALE, None,
                                  ALU.mult).then_inc(qk_evac_dve, 1)

            w_in_los(2, 0, H)
            for j in range(H + 1):
                head_out(j)
            for t in range(NT):
                n = rows(t)
                dve.wait_ge(ktok_full, t + 1)
                dve.tensor_copy(k_st[0:n, t, :], ps[0:n, t % 4, :]).then_inc(ktok_evac, 1)
            dve.wait_ge(hist_full, 1)
            dve.tensor_copy(histT[:, :, :], ps[:, 3, 0:H * HIST].rearrange("p (g s) -> p g s", g=H)).then_inc(hist_evac, 1)
            dve.wait_ge(lam_exp, 1)
            step(dve.tensor_tensor(lam_t[:, 4:5], lam_t[:, 3:4], lam_t[:, 2:3], ALU.subtract))
            dve.tensor_scalar(lam_t[:, 6:7], lam_t[:, 4:5], -LAMBDA_INIT, None, ALU.add).then_inc(lam_made, 1)
            w_in_los(3, 0, H)
            for j in range(H + 1, 2 * H):
                head_out(j)

            def maxima(n):
                t, h = divmod(n, H)
                m, w, b = rows(t), (t + 1) * P if t < PT else PAST + N_SAMPLE, 2 * (n % 2)
                dve.wait_ge(scores_full, n + 1)
                if t < PT:
                    step(dve.memset(ps[0:CHUNK, b:b + 2, w - CHUNK:w], -NEG))
                if n >= 2:
                    dve.wait_ge(exp_done, n - 1)
                dve.tensor_reduce(negm[0:m, n % 2, :], ps[0:m, b:b + 2, 0:w], X, ALU.min).then_inc(negm_ready, 1)

            def differences(n):
                t, h = divmod(n, H)
                m, w = rows(t), (t + 1) * P if t < PT else PAST + N_SAMPLE
                dve.wait_ge(exp_done, n + 1)
                if n == 0:
                    dve.wait_ge(lam_spread, 1)
                step(dve.reciprocal(coef[0:m, 0:1], psums[0:m, t, h, 1:2]))
                step(dve.scalar_tensor_tensor(coef[0:m, 1:2], psums[0:m, t, h, 0:1], neglam[0:m, :], coef[0:m, 0:1],
                                              ALU.mult, ALU.mult))
                dve.scalar_tensor_tensor(prob[0:m, n % 2, 0, 0:w], prob[0:m, n % 2, 1, 0:w], coef[0:m, 1:2],
                                         prob[0:m, n % 2, 0, 0:w], ALU.mult, ALU.add).then_inc(a_ready, 1)

            def o_norm(t, part):
                m = rows(t)
                r0, q, fac = osc[0:m, 0, :], osc[0:m, 1, :], osc[0:m, 2, :]
                tmp, half = osc[0:m, 3, :], ovoff[0:m, NT:NT + H]
                if part == 0:
                    step(dve.reciprocal(r0, psums[0:m, t, :, 0]))
                    step(dve.tensor_tensor(q, r0, r0, ALU.mult))
                    dve.wait_ge(o_squared, t + 1)
                    step(dve.tensor_tensor(q, q, oss[0:m, t, :], ALU.mult))
                    step(dve.tensor_scalar(q, q, 1.0 / VD, EPS, ALU.mult, ALU.add))
                    root_guess(fac, q, tmp, half)
                elif part == 1:
                    root_step(fac, tmp, half)
                    root_step(fac, tmp, half)
                else:
                    root_step(fac, tmp, half)
                    step(dve.tensor_tensor(fac, fac, r0, ALU.mult))
                    dve.tensor_tensor(otok[0:m, :].rearrange("p (h v) -> p h v", h=H),
                                      ps[0:m, 5 + 2 * (t % 2), :].rearrange("p (h v) -> p h v", h=H),
                                      wide(fac, [m, H, VD]), ALU.mult).then_inc(o_ready, 1)

            def oT_out(t):
                m = rows(t)
                cols = slice(t * P, t * P + m)
                oT = ps[:, 5 + 2 * (t % 2), :].rearrange("p (h q) -> p h q", h=H)[:, :, 0:m]
                dve.wait_ge(oT_full, t + 1)
                if t == 0:
                    dve.wait_ge(k_stored, 16 * NT)
                step(dve.tensor_scalar(mix_hi[:, H:2 * H, cols], oT, gsub[:, 0:1], None, ALU.mult))
                dve.scalar_tensor_tensor(mix_lo_heads[:, :, cols], oT, gsub[:, 0:1], mix_hi[:, H:2 * H, cols].bitcast(F32),
                                         ALU.mult, ALU.subtract).then_inc(oT_evac, 1)

            def u_history(g):
                if g >= 2:
                    dve.wait_ge(u_summed, g - 1)
                    dve.wait_ge(diff_ready, g - 1)
                else:
                    dve.wait_ge(x_transposed, NT)
                    dve.wait_ge(xn_ready, NT)
                    dve.memset(uext[:, g % 2, 0:HIST], 0.0)
                dve.tensor_copy(uext[:, g % 2, HIST + N_PROMPT:S0], histT[:, g, :]).then_inc(u_evac_dve, 1)

            def window_diff(g):
                w = WINDOWS[g]
                u, s = uext[:, g % 2, :], usum[:, g % 2, :]
                dve.wait_ge(u_summed, g + 1)
                if g >= 2:
                    dve.wait_ge(dve_step, steps[0])
                step(dve.tensor_tensor(fix[:, 0:w - 1], s[:, HIST:HIST + w - 1], inv_cnt[:, 0:w - 1], ALU.mult))
                step(dve.tensor_tensor(mixT[:, g, 0:w - 1], fix[:, 0:w - 1], u[:, HIST:HIST + w - 1], ALU.subtract))
                step(dve.scalar_tensor_tensor(mixT[:, g, w - 1:N_PROMPT], s[:, HIST + w - 1:HIST + N_PROMPT], 1.0 / w,
                                              u[:, HIST + w - 1:HIST + N_PROMPT], ALU.mult, ALU.subtract))
                dve.scalar_tensor_tensor(mixT[:, g, N_PROMPT:T], s[:, S0:EXT], 1.0 / w, u[:, S0:EXT],
                                         ALU.mult, ALU.subtract).then_inc(diff_ready, 1)

            maxima(0)
            for n in range(UNITS):
                if n + 1 < UNITS:
                    maxima(n + 1)
                if n >= 8 and n % H == 0:
                    oT_out(n // H - 2)
                if n % H == 2 and n < 4 * H:
                    u_history(n // H)
                differences(n)
                if n % H >= 1 and n >= H:
                    o_norm(n // H - 1, n % H - 1)
                if n % H == 0 and n >= 8:
                    window_diff((n - 8) // H)
            oT_out(NT - 2)
            window_diff(H - 1)
            for c in range(H, 2 * H):
                w_out_los(c)
            for g in range(H):
                dve.wait_ge(pool_hi_ready, g + 1)
                dve.scalar_tensor_tensor(mix_lo[g][:, 0:N_PROMPT], ps[:, g, :], pscale[:, g:g + 1], mix_hi[:, g, 0:N_PROMPT].bitcast(F32),
                                         ALU.mult, ALU.subtract).then_inc(pool_evac, 1)
            dve.wait_ge(pool_full, H + 1)
            step(dve.tensor_tensor(mix_hi[:, 0:H, N_PROMPT:T], ps[:, 4, 0:H * N_SAMPLE].rearrange("p (g t) -> p g t", g=H),
                                   wide(pscale[:, :], [P, H, N_SAMPLE]), ALU.mult))
            for g in range(H):
                ins = dve.scalar_tensor_tensor(mix_lo[g][:, N_PROMPT:T], ps[:, 4, g * N_SAMPLE:(g + 1) * N_SAMPLE],
                                               pscale[:, g:g + 1], mix_hi[:, g, N_PROMPT:T].bitcast(F32), ALU.mult, ALU.subtract)
            ins.then_inc(pool_evac_sample, 1)
            for part in range(3):
                o_norm(NT - 1, part)
            dve.wait_ge(state_full, 1)
            dve.tensor_copy(state_out[:, :, :], ps[0:HIST, 6:8, :]).then_inc(state_evac, 1)
            oT_out(NT - 1)

            def residual(t, half):
                n = rows(t)
                c = slice(half * 512, (half + 1) * 512)
                dve.wait_ge(op_full, 2 * t + half + 1)
                dve.wait_ge(xres_loaded[t], 16)
                dve.tensor_tensor(x2[0:n, t, c], ps[0:n, 2 * (t % 2) + half, :], x2[0:n, t, c], ALU.add).then_inc(x2_ready, 1)

            def h2_norm(t):
                n = rows(t)
                dve.wait_ge(x2_squared, 2 * t + 2)
                dve.tensor_tensor(ss[0:n, t:t + 1], ss2[0:n, 0, t:t + 1], ss2[0:n, 1, t:t + 1], ALU.add).then_inc(x2_sum_ready, 1)
                dve.wait_ge(x2_sum_ready, t + 1)
                y = row_scale(t, NT + t + 1)
                dve.tensor_scalar(h2n[0:n, t % 2, :], x2[0:n, t, :], y, None, ALU.mult).then_inc(h2n_ready, 1)

            def h2T_evac(t):
                n = rows(t)
                dve.wait_ge(h2_transposed, t + 1)
                if t >= 1:
                    dve.wait_ge(router_done, t)
                dve.tensor_copy(h2T[:, 0:4, 0:n], ps[:, 4, :].rearrange("p (k t) -> p k t", k=4)[:, :, 0:n]).then_inc(h2T_dve, 1)

            dve.wait_ge(consts_loaded, 80)
            dve.tensor_tensor(wr[:, :, :], wr[:, :, :], wide(gffn_sb[:, :], [P, KC, NL]), ALU.mult).then_inc(wr_scaled, 1)
            dve.wait_ge(state_stored, 32)
            step(dve.memset(lg[N_SAMPLE:P, NT - 1, :], 0.0))
            for t in range(NT):
                residual(t, 0)
                residual(t, 1)
                if t >= 1:
                    h2T_evac(t - 1)
                h2_norm(t)
            h2T_evac(NT - 1)

            dve.wait_ge(router_done, NT)
            T4, T44 = [P, NT, G], [P, NT, G, EPG]
            for t in (slice(0, PT), slice(PT, NT)):
                n, m = (P, PT) if t.start == 0 else (N_SAMPLE, 1)
                ins = dve.tensor_tensor(lg[0:n, t, :], ps[0:n, 6, t.start * NL:t.stop * NL].rearrange("p (t l) -> p t l", t=m),
                                        bias[0:n, :].unsqueeze(1).to_broadcast([n, m, NL]), ALU.add)
            step(ins)
            gl = lg[:, :, 0:G]
            el = lg[:, :, G:NL].rearrange("p t (g j) -> p t g j", g=G)

            def first_max(src, best, mask, scratch, out, rev_b, shape):
                yield lambda: dve.tensor_reduce(best, src, X, ALU.max)
                yield lambda: dve.tensor_tensor(mask, src, wide(best, shape), ALU.is_equal)
                yield lambda: dve.tensor_tensor(mask, mask, rev_b, ALU.mult)
                yield lambda: dve.tensor_reduce(scratch, mask, X, ALU.max)
                yield lambda: dve.tensor_tensor(out, mask, wide(scratch, shape), ALU.is_equal)

            dve.memset(msum_b[:, NT, :], 0.0)
            rev4 = rev[:, :].unsqueeze(1).to_broadcast(T4)
            rev16 = rev[:, :].unsqueeze(1).unsqueeze(1).to_broadcast(T44)
            of_group = list(first_max(gl, rt1[:, 0, :], rt4, rt1[:, 2, :], g1h, rev4, T4))
            first = list(first_max(el, grp[:, 0], rt16, grp[:, 2], top[:, 0], rev16, T44))
            second = list(first_max(rt16b, grp[:, 1], rt16, grp[:, 2], top[:, 1], rev16, T44))
            for a, b in zip(of_group, first):
                a()
                step(b())
            dve.tensor_tensor(gex, gl, wide(rt1[:, 0, :], T4), ALU.subtract).then_inc(gate_in, 1)
            step(dve.scalar_tensor_tensor(rt16b, top[:, 0], NEG, el, ALU.mult, ALU.add))
            for b in second:
                step(b())
            for c in range(2):
                out = m12[:, c].rearrange("p t (g j) -> p t g j", g=G)
                ins = dve.tensor_tensor(out, wide(g1h, T44), top[:, c], ALU.mult)
            step(ins)
            step(dve.memset(m12[N_SAMPLE:P, :, NT - 1, :], 0.0))
            step(dve.tensor_tensor(msum, m12[:, 0], m12[:, 1], ALU.add))
            dve.tensor_copy(msum_b[:, 0:NT, :], msum).then_inc(mask_ready, 1)
            step(dve.tensor_tensor(rt4, grp[:, 1], grp[:, 0], ALU.subtract))
            step(dve.tensor_tensor(rt4, rt4, g1h, ALU.mult))
            dve.tensor_reduce(rt1[:, 3, :], rt4, X, ALU.add).then_inc(gate_in, 1)
            dve.wait_ge(rank_full, 1)
            rank = ps[:, 5, 0:NT * E].rearrange("p (t e) -> p t e", t=NT)
            n_e = ps[:, 5, NT * E:(NT + 1) * E]
            step(dve.scalar_tensor_tensor(etmp, rank, 1.0, msum, ALU.add, ALU.mult))
            step(dve.tensor_scalar(rm[:, :, :], etmp, -1.0, None, ALU.add))

            iota_t = iota_row[:, :].unsqueeze(1).to_broadcast([P, NT, P])

            def expert_onehot(e, b):
                col = (rm[:, :, e:e + 1] if isinstance(e, int) else rm[:, :, DS(e, 1)]).rearrange("p t a -> p (t a)")
                return dve.tensor_tensor(onehot_all[:, b], iota_t, wide(col, [P, NT, P]), ALU.is_equal)

            def to_index(b):
                return dve.tensor_scalar(idx[:, b:b + 1], ps[:, 6 + b, 0:1], ps[:, 6 + b, 1:2],
                                         float(NOWHERE), ALU.add, ALU.add)

            def rows_out(b):
                return dve.tensor_tensor(xT[:, b, 0:4, :], ps[:, 0, :].rearrange("p (k s) -> p k s", k=4),
                                         wide(gffn_sb[:, 0:4], [P, 4, P]), ALU.mult)

            dve.wait_ge(h2_stored[0], 48)
            dve.wait_ge(h2_stored[1], 32)
            for i in range(2):
                expert_onehot(i, i).then_inc(onehot_ready, 1)
                dve.wait_ge(idx_full, i + 1)
                to_index(i).then_inc(idx_ready, 1)
            expert_onehot(2, 0).then_inc(onehot_ready, 1)
            dve.wait_ge(gate_exp, 2)
            step(dve.tensor_reduce(rt1[:, 2, :], gex, X, ALU.add))
            step(dve.tensor_scalar(rt1[:, 1, :], rt1[:, 3, :], 1.0, None, ALU.add))
            step(dve.tensor_tensor(rt1[:, 1, :], rt1[:, 1, :], rt1[:, 2, :], ALU.mult))
            step(dve.reciprocal(wtok[:, 0, :], rt1[:, 1, :]))
            step(dve.tensor_tensor(wtok[:, 1, :], wtok[:, 0, :], rt1[:, 3, :], ALU.mult))
            step(dve.tensor_scalar(over, n_e, float(CAP), None, ALU.is_gt))
            for k in range(1, OVK):
                step(dve.scalar_tensor_tensor(over, n_e, float(CAP + k * P), over, ALU.is_gt, ALU.add))
            step(dve.tensor_copy(cum[:, 0, :], over))
            cur = 0
            for shift in (1, 2, 4, 8):
                step(dve.tensor_copy(cum[:, 1 - cur, 0:shift], cum[:, cur, 0:shift]))
                step(dve.tensor_tensor(cum[:, 1 - cur, shift:E], cum[:, cur, shift:E], cum[:, cur, 0:E - shift], ALU.add))
                cur = 1 - cur
            incl, start = cum[:, cur, :], cum[:, 1 - cur, :]
            step(dve.tensor_tensor(start, incl, over, ALU.subtract))
            step(dve.tensor_scalar(start, start, float(P), float(E * P - CAP), ALU.mult, ALU.add))
            step(dve.tensor_tensor(start, start, e128[:, :], ALU.subtract))
            dve.wait_ge(h2T_act, NT)
            dve.wait_ge(xg_transposed, 1)
            rows_out(0).then_inc(xT_dve, 1)
            step(dve.tensor_scalar(isov, rank, float(CAP), None, ALU.is_ge))
            over_e = lambda a: a.unsqueeze(1).to_broadcast([P, NT, E])
            step(dve.tensor_tensor(isov, isov, over_e(start), ALU.mult))
            step(dve.tensor_tensor(ylin, rank, isov, ALU.add))
            step(dve.tensor_tensor(ylin, ylin, over_e(e128[:, :]), ALU.add))
            for c in range(2):
                step(dve.tensor_tensor(etmp, m12[:, c], ylin, ALU.mult))
                step(dve.tensor_reduce(yslot_f[:, c, :], etmp, X, ALU.add))
            step(dve.scalar_tensor_tensor(wmain[:, :, :], yslot_f[:, :, :], float(NSLOT), wtok[:, :, :], ALU.is_lt, ALU.mult))
            step(dve.tensor_scalar(yslot[:, :, :], yslot_f[:, :, :], float(NSLOT - 1), None, ALU.min))
            step(dve.tensor_scalar(w_last[:, :, :], yslot_f[:, :, :], float(NSLOT), None, ALU.is_ge))
            step(dve.scalar_tensor_tensor(w_last[:, :, :], yslot_f[:, :, :], float(E * P), w_last[:, :, :], ALU.is_lt, ALU.mult))
            step(dve.tensor_tensor(w_last[:, :, :], w_last[:, :, :], wtok[:, :, :], ALU.mult))
            dve.tensor_tensor(w_last[:, 0, :], w_last[:, 0, :], w_last[:, 1, :], ALU.add).then_inc(wslots_ready, 1)
            step(dve.tensor_tensor(jcmp, incl.unsqueeze(1).to_broadcast([P, MAXOV, E]), wide(jrow[:, :], [P, MAXOV, E]),
                                   ALU.is_le))
            step(dve.tensor_reduce(jsum, jcmp, X, ALU.add))
            step(dve.tensor_scalar(ctl[:, 0:MAXOV], jsum[0:1, :], float(E - 1), None, ALU.min))
            dve.tensor_copy(ctl[:, MAXOV:MAXOV + 1], incl[0:1, E - 1:E]).then_inc(routed, 1)

            dve.sem_inc(y_evac_dve, 1)
            def expert(it, u, left):
                i = it * RING + u
                b = u % 2
                if left is None or left >= 2:
                    dve.wait_ge(idx_full, i + 3)
                    dve.wait_ge(xg_loaded[b], it * (8 * RING) + 16 * (u // 2 + 1))
                    to_index(b).then_inc(idx_ready, 1)
                dve.wait_ge(gact_ready, i + 1)
                dve.wait_ge(up_full, i + 1)
                dve.tensor_tensor(heT[:, b], gact[:, b],
                                  ps[:, 3, 0:FE].rearrange("p (c s) -> p c s", c=FC), ALU.mult).then_inc(he_ready, 1)
                if left is None or left >= 1:
                    dve.wait_ge(xg_transposed, i + 2)
                    rows_out(1 - b).then_inc(xT_dve, 1)
                if left is None or left >= 3:
                    expert_onehot(i + 3, 1 - b).then_inc(onehot_ready, 1)
                dve.wait_ge(down_done, i + 1)
                dve.wait_ge(yst_free, i + 1)
                dve.tensor_copy(yst[:, b, 512:1024], ps[:, 5, :]).then_inc(y_evac_dve, 1)

            with dve.Fori(0, E // RING - 1) as it:
                for u in range(RING):
                    expert(it, u, None)
            for u in range(RING):
                expert(E // RING - 1, u, RING - 1 - u)

            n_ov = dve.value_load(ctl[0:1, MAXOV:MAXOV + 1], min_val=0, max_val=MAXOV)
            dve.wait_ge(idx_full, E)
            dve.wait_ge(onehot_ready, E)
            dve.wait_ge(xg_loaded[0], 8 * E)
            dve.wait_ge(xg_loaded[1], 8 * E)
            dve.wait_ge(xT_act, E)
            dve.wait_ge(yst_free, E + 1)
            with dve.If(n_ov > 0):
                with dve.Fori(0, MAXOV) as j:
                    with dve.If(j < n_ov):
                        def ov_do(ins, n):
                            ins.then_inc(ov_step, 1)
                            dve.wait_ge(ov_step, j * OV_STEPS + n)

                        ov_do(dve.tensor_scalar(ovoff[:, :], yslot_f[:, :, :].rearrange("p c t -> p (c t)"), jbase[:, DS(j, 1)],
                                                None, ALU.subtract), 1)
                        for c in range(2):
                            ins = dve.tensor_tensor(onehot_all[:, c], iota_t, wide(ovoff[:, c * NT:(c + 1) * NT], [P, NT, P]),
                                                    ALU.is_equal)
                        ins.then_inc(ov_onehot, 1)
                        dve.wait_ge(ov_idx_full, j + 1)
                        to_index(0).then_inc(ov_idx_ready, 1)
                        offs = ovoff[:, :].rearrange("p (c t) -> p c t", c=2)
                        ov_do(dve.tensor_scalar(ovw[:, :, :], offs, 0.0, None, ALU.is_ge), 2)
                        ov_do(dve.scalar_tensor_tensor(ovw[:, :, :], offs, float(P), ovw[:, :, :], ALU.is_lt, ALU.mult), 3)
                        ov_do(dve.tensor_tensor(ovw[:, :, :], ovw[:, :, :], wtok[:, :, :], ALU.mult), 4)
                        ov_do(dve.tensor_tensor(ovw[:, 0, :], ovw[:, 0, :], ovw[:, 1, :], ALU.add), 5)
                        ov_do(dve.tensor_scalar(slot_tok[:, :], ps[:, 6, 0:1], ps[:, 6, 1:2], float(NOWHERE), ALU.add, ALU.add), 6)
                        for t in range(NT):
                            ins = dve.tensor_scalar(slot_to_token[:, t, :], iota_row[:, :], float(t * P), slot_tok[:, 0:1],
                                                    ALU.add, ALU.is_equal)
                        ov_do(ins, OV_STEPS)
                        dve.wait_ge(ov_transposed, j + 1)
                        dve.tensor_tensor(xT[:, 0], ps[:, 0:2, :].rearrange("p b (k s) -> p (b k) s", k=4),
                                          wide(gffn_sb[:, :], [P, KC, P]), ALU.mult).then_inc(ov_xT_ready, 1)
                        dve.wait_ge(ov_gact_ready, j + 1)
                        dve.tensor_tensor(heT[:, 0], gact[:, 0],
                                          ps[:, 3, 0:FE].rearrange("p (c s) -> p c s", c=FC), ALU.mult).then_inc(ov_he_ready, 1)
                        dve.wait_ge(ov_down_done, j + 1)
                        dve.tensor_copy(yst[:, 0, :].rearrange("p (b d) -> p b d", b=2), ps[:, 4:6, :]).then_inc(ov_y_ready, 1)
                        for t in range(NT):
                            n, b = rows(t), 4 - 2 * (t % 2)
                            dve.wait_ge(ov_combine_full, j * NT + (t + 1))
                            xt = x2[0:n, t, :].rearrange("p (b d) -> p b d", b=2)
                            dve.scalar_tensor_tensor(xt, ps[0:n, b:b + 2, :], ovw[0:n, 0, t:t + 1], xt,
                                                     ALU.mult, ALU.add).then_inc(ov_added, 1)
                        dve.wait_ge(ov_added, (j + 1) * NT)
                        dve.sem_inc(ov_tile_done, 1)
                    dve.nop()

            dve.wait_ge(xg_transposed, E)
            dve.wait_ge(wslots_ready, 1)
            step(dve.tensor_scalar(slot_tok[:, :], ps[:, 7, 0:1], ps[:, 7, 1:2], float(NOWHERE), ALU.add, ALU.add))
            for t in range(NT):
                ins = dve.tensor_scalar(slot_to_token[:, t, :], iota_row[:, :], float(t * P), slot_tok[:, 0:1],
                                        ALU.add, ALU.is_equal)
            ins.then_inc(last_onehot, 1)

            def combine(t):
                n = rows(t)
                dve.wait_ge(y_gathered[t], 32)
                step(dve.scalar_tensor_tensor(y1[t][0:n, :], y1[t][0:n, :], wmain[0:n, 0, t:t + 1], x2[0:n, t, :],
                                              ALU.mult, ALU.add))
                step(dve.scalar_tensor_tensor(y1[t][0:n, :], y2[t][0:n, :], wmain[0:n, 1, t:t + 1], y1[t][0:n, :],
                                              ALU.mult, ALU.add))

            def add_last(t):
                n, b = rows(t), 4 - 2 * (t % 3)
                dve.wait_ge(last_full, t + 1)
                if t in POOL_TILES:
                    dve.wait_ge(combined_by_pool, POOL_TILES.index(t) + 1)
                acc = y1[t][0:n, :].rearrange("p (b d) -> p b d", b=2)
                dve.scalar_tensor_tensor(acc, ps[0:n, b:b + 2, :], w_last[0:n, 0, t:t + 1], acc,
                                         ALU.mult, ALU.add).then_inc(acc_ready, 1)

            def finish(tiles, nth, others):
                c = slice(tiles[0], tiles[-1] + 1)
                m, y, tmp, half = rs[:, 1, c], rs[:, 0, c], rs[:, 2, c], ovoff[:, c]
                dve.wait_ge(acc_squared, tiles[-1] + 1)
                step(dve.tensor_scalar(m, ss[:, c], 1.0 / D, EPS, ALU.mult, ALU.add))
                step(dve.tensor_scalar(half, m, -0.5, None, ALU.mult))
                dve.wait_ge(root_ready, 2 * NT + nth)
                refine_root(y, tmp, half, factors_ready)
                dve.wait_ge(factors_ready, nth)
                for t in tiles:
                    if t not in others:
                        n = rows(t)
                        dve.scalar_tensor_tensor(y2[t][0:n, :], y1[t][0:n, :], rs[0:n, 0, t:t + 1], gfin[0:n, :],
                                                 ALU.mult, ALU.mult).then_inc(out_by_dve, 1)

            dve.wait_ge(gfin_loaded, 16)
            step(dve.memset(ss[N_SAMPLE:P, NT - 1:NT], 1.0))
            for t in OWN_TILES:
                combine(t)
                if t >= 1:
                    add_last(t - 1)
            add_last(OWN_TILES[-1])
            add_last(POOL_TILES[0])
            finish(OWN_TILES, 1, ACT_OWN)
            add_last(POOL_TILES[1])
            dve.wait_ge(acc_ready, POOL_TILES.index(ACT_LATE) + len(OWN_TILES) + 1)
            n = rows(ACT_LATE)
            dve.tensor_tensor(y2[ACT_LATE][0:n, :], y1[ACT_LATE][0:n, :], gfin[0:n, :], ALU.mult).then_inc(gained_by_dve, 1)
            finish(POOL_TILES, 2, (ACT_LATE,))


_INS = ["x_prompt", "x_sample", "cache_k", "cache_v", "state_pool", "g_mix", "w_in", "w_pool", "pool_scale",
        "lam_q1", "lam_k1", "lam_q2", "lam_k2", "g_subln", "w_out", "g_ffn", "w_group", "b_group", "w_erouter",
        "b_erouter", "w_gate", "w_up", "w_down", "g_final"]
_OUTS = [("y_prompt", (1, N_PROMPT, D)), ("y_sample", (1, N_SAMPLE, D)),
         ("k_prompt", (1, 1, N_PROMPT, H, 2 * HD)), ("v_prompt", (1, 1, N_PROMPT, H, VD)),
         ("pool_prompt", (1, 1, HIST, PW)),
         ("k_sample", (1, 1, N_SAMPLE, H, 2 * HD)), ("v_sample", (1, 1, N_SAMPLE, H, VD)),
         ("pool_sample", (1, 1, HIST, PW))]


def kernel(**inputs):
    import numpy as _np
    import concourse.bacc as _bacc
    from concourse.bass_utils import run_bass_kernel_spmd as _run

    nc = _bacc.Bacc("TRN2", target_bir_lowering=False, num_devices=1)
    arrays, args = {}, {}
    for name in _INS:
        a = _np.ascontiguousarray(inputs[name])
        arrays[f"in_{name}"] = a
        args[name] = nc.dram_tensor(f"in_{name}", a.shape, mybir.dt.from_np(a.dtype), kind="ExternalInput").ap()
    for name, shape in _OUTS:
        args[name] = nc.dram_tensor(f"out_{name}", shape, F32, kind="ExternalOutput").ap()
    build(nc, **args)
    r = _run(nc, [arrays], core_ids=[0])
    return tuple(r.results[0][f"out_{name}"] for name, _ in _OUTS)
```
